# Optimizing a Trainium2 kernel written in Bass

```python
import jax, jax.numpy as jnp
from jax import lax
import numpy as np

D_MODEL = 2048
BATCH = 1
SEQ = 1024
DEPTH = 1

HEAD_DIM = 64
MIX_WIDTH = D_MODEL
A_WIDTH = 3 * MIX_WIDTH // 8
A_HEADS = A_WIDTH // HEAD_DIM
DILATED_BRANCHES = ((128, 1), (512, 4), (2048, 16))
BAND_BLOCK = 128
B_WIDTH = MIX_WIDTH // 4
B_HEADS = B_WIDTH // HEAD_DIM
FOX_BLOCK = 128
C_VWIDTH = MIX_WIDTH - A_WIDTH - B_WIDTH
C_HEADS = 4
C_DV = C_VWIDTH // C_HEADS
C_DK = C_DV // 2
C_KWIDTH = C_HEADS * C_DK
GATE_RANK = 16
GATE_TEMP = 16.0
GLA_CHUNK = 64
RMS_EPS = 1e-6

IN_SPLITS = (A_WIDTH, A_WIDTH, A_WIDTH, A_WIDTH,
             B_WIDTH, B_WIDTH, B_WIDTH, B_WIDTH, B_HEADS,
             C_KWIDTH, C_KWIDTH, C_VWIDTH, C_VWIDTH, GATE_RANK)
IN_WIDTH = int(sum(IN_SPLITS))
SPLIT_IDX = [int(i) for i in np.cumsum(IN_SPLITS)[:-1]]

kernel_name = "hymba_style_dilated_fox_gla_hybrid"

def rms_norm(x, g):
    xf = x.astype(jnp.float32)
    y = xf * lax.rsqrt(jnp.mean(xf * xf, axis=-1, keepdims=True) + RMS_EPS)
    return (y * g.astype(jnp.float32)).astype(x.dtype)

def dilated_branch(q, k, v, window, dilation):
    bsz, s, h, hd = q.shape
    steps = window // dilation
    L = s // dilation
    nb = -(-L // BAND_BLOCK)
    lp = nb * BAND_BLOCK

    def to_blocks(t):
        t = t.reshape(bsz, L, dilation, h, hd).transpose(0, 2, 1, 3, 4)
        t = jnp.pad(t, ((0, 0), (0, 0), (0, lp - L), (0, 0), (0, 0)))
        return t.reshape(bsz, dilation, nb, BAND_BLOCK, h, hd)

    def with_prev(t):
        prev = jnp.pad(t[:, :, :-1], ((0, 0), (0, 0), (1, 0), (0, 0), (0, 0), (0, 0)))
        return jnp.concatenate([prev, t], axis=3)

    qb = to_blocks(q)
    kb = with_prev(to_blocks(k))
    vb = with_prev(to_blocks(v))
    logits = jnp.einsum('brnqhe,brnkhe->brnhqk', qb, kb,
                        preferred_element_type=jnp.float32)
    qi = BAND_BLOCK + jnp.arange(BAND_BLOCK)
    ki = jnp.arange(2 * BAND_BLOCK)
    rel = qi[:, None] - ki[None, :]
    band = (rel >= 0) & (rel <= steps)
    key_idx = jnp.arange(nb)[:, None, None] * BAND_BLOCK - BAND_BLOCK + ki[None, None, :]
    mask = band[None] & (key_idx >= 0)
    logits = jnp.where(mask[None, None, :, None], logits, -jnp.inf)
    m = jnp.max(logits, axis=-1, keepdims=True)
    p = jnp.exp(logits - m)
    den = jnp.sum(p, axis=-1)
    out = jnp.einsum('brnhqk,brnkhe->brnqhe', p, vb.astype(jnp.float32))
    out = out / jnp.swapaxes(den, -1, -2)[..., None]
    lse = m[..., 0] + jnp.log(den)
    out = out.reshape(bsz, dilation, lp, h, hd)[:, :, :L]
    out = out.transpose(0, 2, 1, 3, 4).reshape(bsz, s, h, hd)
    lse = jnp.swapaxes(lse, -1, -2).reshape(bsz, dilation, lp, h)[:, :, :L]
    lse = lse.transpose(0, 2, 1, 3).reshape(bsz, s, h)
    return out, lse

def dilated_mixture(q, k, v):
    outs, lses = [], []
    for window, dilation in DILATED_BRANCHES:
        o, l = dilated_branch(q, k, v, window, dilation)
        outs.append(o)
        lses.append(l)
    wts = jax.nn.softmax(jnp.stack(lses), axis=0)
    return jnp.einsum('nbsh,nbshe->bshe', wts, jnp.stack(outs))

def forgetting_attention(q, k, v, log_f):
    bsz, s, h, hd = q.shape
    nb = s // FOX_BLOCK
    c = jnp.cumsum(log_f, axis=1)
    c_keys = jnp.swapaxes(c, 1, 2)
    qb = q.reshape(bsz, nb, FOX_BLOCK, h, hd).swapaxes(0, 1)
    cb = c.reshape(bsz, nb, FOX_BLOCK, h).swapaxes(0, 1)
    kpos = jnp.arange(s)
    vf = v.astype(jnp.float32)

    def block(args):
        qi, ci, i = args
        logits = jnp.einsum('bqhe,bkhe->bhqk', qi, k, preferred_element_type=jnp.float32)
        logits = logits + jnp.swapaxes(ci, 1, 2)[..., None] - c_keys[:, :, None, :]
        qpos = i * FOX_BLOCK + jnp.arange(FOX_BLOCK)
        logits = jnp.where(kpos[None, :] <= qpos[:, None], logits, -jnp.inf)
        p = jax.nn.softmax(logits, axis=-1)
        return jnp.einsum('bhqk,bkhe->bqhe', p, vf)

    out = lax.map(block, (qb, cb, jnp.arange(nb)))
    return out.swapaxes(0, 1).reshape(bsz, s, h, hd)

def gla_chunked(q, k, v, log_a):
    bsz, s, h, dk = q.shape
    dv = v.shape[-1]
    n = s // GLA_CHUNK

    def chunks(t):
        return t.astype(jnp.float32).reshape(bsz, n, GLA_CHUNK, *t.shape[2:]).swapaxes(0, 1)

    tri = jnp.tril(jnp.ones((GLA_CHUNK, GLA_CHUNK), dtype=bool))

    def step(state, inp):
        qc, kc, vc, ac = inp
        bc = jnp.cumsum(ac, axis=1)
        diff = bc[:, :, None] - bc[:, None, :]
        decay = jnp.exp(jnp.where(tri[None, :, :, None, None], diff, -jnp.inf))
        attn = jnp.einsum('bthd,bshd,btshd->bhts', qc, kc, decay)
        o = (jnp.einsum('bhts,bshv->bthv', attn, vc)
             + jnp.einsum('bthd,bhdv->bthv', qc * jnp.exp(bc), state))
        b_last = bc[:, -1]
        new_state = (state * jnp.exp(b_last)[..., None]
                     + jnp.einsum('bshd,bshv->bhdv', kc * jnp.exp(b_last[:, None] - bc), vc))
        return new_state, o

    state0 = jnp.zeros((bsz, h, dk, dv), jnp.float32)
    _, out = lax.scan(step, state0, (chunks(q), chunks(k), chunks(v), chunks(log_a)))
    return out.swapaxes(0, 1).reshape(bsz, s, h, dv)

def hybrid_layer(x, norm_g, w_in, a_q_gain, a_k_gain, b_q_gain, b_k_gain, fox_bias,
                 gla_gate_up, gla_gate_bias, gla_out_gain, w_out):
    bsz, s, _ = x.shape
    h = rms_norm(x, norm_g)
    proj = jnp.einsum('bsd,de->bse', h, w_in)
    (aq, ak, av, az, bq, bk, bv, bz, bf, cq, ck, cv, cz, cr) = jnp.split(proj, SPLIT_IDX, axis=-1)
    scale = HEAD_DIM ** -0.5

    heads_a = lambda t: t.reshape(bsz, s, A_HEADS, HEAD_DIM)
    qa = rms_norm(heads_a(aq), a_q_gain) * scale
    ka = rms_norm(heads_a(ak), a_k_gain)
    out_a = dilated_mixture(qa, ka, heads_a(av)).reshape(bsz, s, A_WIDTH)

    heads_b = lambda t: t.reshape(bsz, s, B_HEADS, HEAD_DIM)
    qb = rms_norm(heads_b(bq), b_q_gain) * scale
    kb = rms_norm(heads_b(bk), b_k_gain)
    log_f = jax.nn.log_sigmoid(bf.astype(jnp.float32) + fox_bias.astype(jnp.float32))
    out_b = forgetting_attention(qb, kb, heads_b(bv), log_f).reshape(bsz, s, B_WIDTH)

    qc = cq.reshape(bsz, s, C_HEADS, C_DK) * (C_DK ** -0.5)
    kc = ck.reshape(bsz, s, C_HEADS, C_DK)
    vc = cv.reshape(bsz, s, C_HEADS, C_DV)
    gate_logit = jnp.einsum('bsr,rk->bsk', cr, gla_gate_up) + gla_gate_bias
    log_a = (jax.nn.log_sigmoid(gate_logit.astype(jnp.float32)) / GATE_TEMP)
    log_a = log_a.reshape(bsz, s, C_HEADS, C_DK)
    out_c = rms_norm(gla_chunked(qc, kc, vc, log_a), gla_out_gain).reshape(bsz, s, C_VWIDTH)

    mixed = jnp.concatenate([
        out_a.astype(h.dtype) * jax.nn.silu(az),
        out_b.astype(h.dtype) * jax.nn.silu(bz),
        out_c.astype(h.dtype) * jax.nn.silu(cz)], axis=-1)
    return x + jnp.einsum('bse,ed->bsd', mixed, w_out)

def setup_inputs(seed: int = 0) -> dict:
    key = jax.random.key(seed)
    ks = jax.random.split(key, 13)
    nrm = jax.random.normal
    f32 = jnp.float32
    x = nrm(ks[0], (BATCH, SEQ, D_MODEL), f32)
    norm_g = 1.0 + 0.02 * nrm(ks[1], (DEPTH, D_MODEL), f32)
    w_in = nrm(ks[2], (DEPTH, D_MODEL, IN_WIDTH), f32) * D_MODEL ** -0.5
    a_q_gain = 1.0 + 0.02 * nrm(ks[3], (DEPTH, HEAD_DIM), f32)
    a_k_gain = 1.0 + 0.02 * nrm(ks[4], (DEPTH, HEAD_DIM), f32)
    b_q_gain = 1.0 + 0.02 * nrm(ks[5], (DEPTH, HEAD_DIM), f32)
    b_k_gain = 1.0 + 0.02 * nrm(ks[6], (DEPTH, HEAD_DIM), f32)
    fox_bias = (jnp.linspace(0.0, 6.0, B_HEADS, dtype=f32)[None, :]
                + 0.1 * nrm(ks[7], (DEPTH, B_HEADS), f32))
    gla_gate_up = nrm(ks[8], (DEPTH, GATE_RANK, C_KWIDTH), f32) * GATE_RANK ** -0.5
    gla_gate_bias = 0.1 * nrm(ks[9], (DEPTH, C_KWIDTH), f32)
    gla_out_gain = 1.0 + 0.02 * nrm(ks[10], (DEPTH, C_DV), f32)
    w_out = nrm(ks[11], (DEPTH, MIX_WIDTH, D_MODEL), f32) * MIX_WIDTH ** -0.5
    return {"x": x, "norm_g": norm_g, "w_in": w_in, "a_q_gain": a_q_gain,
            "a_k_gain": a_k_gain, "b_q_gain": b_q_gain, "b_k_gain": b_k_gain,
            "fox_bias": fox_bias, "gla_gate_up": gla_gate_up, "gla_gate_bias": gla_gate_bias,
            "gla_out_gain": gla_out_gain, "w_out": w_out}

def reference(x, norm_g, w_in, a_q_gain, a_k_gain, b_q_gain, b_k_gain, fox_bias,
              gla_gate_up, gla_gate_bias, gla_out_gain, w_out):
    for layer in range(DEPTH):
        x = hybrid_layer(x, norm_g[layer], w_in[layer], a_q_gain[layer], a_k_gain[layer],
                         b_q_gain[layer], b_k_gain[layer], fox_bias[layer],
                         gla_gate_up[layer], gla_gate_bias[layer], gla_out_gain[layer],
                         w_out[layer])
    return x


_drawn_inputs = setup_inputs


def setup_inputs(seed=0):
    import zlib

    import numpy as np

    out = dict(_drawn_inputs(seed))
    spreads = {}
    factors = {'norm_g': 3.716,
     'a_q_gain': 8.0,
     'a_k_gain': 8.0,
     'b_q_gain': 8.0,
     'b_k_gain': 8.0,
     'gla_gate_bias': 3.785,
     'gla_out_gain': 8.0}
    for name, (base, spread) in spreads.items():
        noise = np.random.default_rng([zlib.crc32(name.encode()), seed]).standard_normal(out[name].shape)
        drawn = base * np.exp(spread * noise) if base else spread * noise
        out[name] = __import__('jax').numpy.asarray(drawn.astype(out[name].dtype))
    for name, factor in factors.items():
        out[name] = (out[name] * factor).astype(out[name].dtype)
    return out
```

```python
import concourse.bass as bass
from concourse import mybir
from contextlib import ExitStack

P = 128
SEQ = 1024
D_MODEL = 2048
KT = D_MODEL // P
NT = SEQ // P
HALF = 512
HEAD = 64
A_WIDTH = 768
B_WIDTH = 512
B_HEADS = B_WIDTH // HEAD
C_HEADS = 4
C_DV = 192
C_DK = 96
C_K = C_HEADS * C_DK
C_V = C_HEADS * C_DV
RANK = 16
A_PAIRS = A_WIDTH // P
B_PAIRS = B_WIDTH // P
COL_B = 4 * A_WIDTH
COL_BF = COL_B + 4 * B_WIDTH
COL_CQ = COL_BF + B_HEADS
COL_CK = COL_CQ + C_K
COL_CV = COL_CK + C_K
COL_CZ = COL_CV + C_V
COL_CR = COL_CZ + C_V
IN_WIDTH = COL_CR + RANK
SMALL = B_HEADS + RANK
C_GROUPS = (COL_CR - COL_CQ) // P
PAIR_GROUPS = 4
ITEMS = 2 * NT
LEVELS = 7
S_A0 = C_GROUPS
S_LOOP_A = S_A0 + PAIR_GROUPS
S_B0 = S_LOOP_A + PAIR_GROUPS * (A_PAIRS - 1)
S_LOOP_B = S_B0 + PAIR_GROUPS
GROUPS = S_LOOP_B + PAIR_GROUPS * (B_PAIRS - 1)
Q_OUT = 4 * GROUPS
OUT_CG = D_MODEL // HALF
EPS = 1e-6
FAR = 1e30
LN2, LN3 = 0.6931471805599453, 1.0986122886681098

F32 = mybir.dt.float32
F32R = mybir.dt.float32r
I32 = mybir.dt.int32
ALU = mybir.AluOpType
ACT = mybir.ActivationFunctionType
AX_X = mybir.AxisListType.X

SLOTS = 8 * PAIR_GROUPS
LEVELS_AT = {1: (0, 1, 2), 2: (3, 4), 3: (5, 6)}
SLOT_S = [7 + (j * 22) // (ITEMS - 1) for j in range(ITEMS)]
MIX_SLOT = 6
SLOT_T = [s + 2 for s in SLOT_S]
SLOT_V = [s + 3 for s in SLOT_S]
OUT_ORDER = [k for k in range(KT) if k != A_PAIRS + B_PAIRS - 1] + [A_PAIRS + B_PAIRS - 1]


def steps_of(slot):
    out = []
    if slot == 0:
        out.append(("norm", 0))
    if slot == 2:
        out.append(("stack", 0))
    if slot == 4:
        out.append(("values", 0))
    out += [("product", j) for j in range(ITEMS) if SLOT_V[j] == slot]
    out += [("turn", j) for j in range(ITEMS) if SLOT_T[j] == slot]
    out += [("score", j) for j in range(ITEMS) if SLOT_S[j] == slot]
    if slot == 9:
        out.insert(0, ("gate", 0))
    return out


def blocks(ap, b):
    return ap.rearrange("p (n u r) -> p n u r", u=2, r=b)


def build(nc, x, norm_g, w_in, a_q_gain, a_k_gain, b_q_gain, b_k_gain, fox_bias,
          gla_gate_up, gla_gate_bias, gla_out_gain, w_out, out):
    x_rows, out_rows = x[0], out[0]
    w_in, w_out = w_in[0], w_out[0]
    w_in_k = w_in.rearrange("(k p) c -> p k c", p=P)
    w_out_k = w_out.rearrange("(k p) c -> p k c", p=P)
    proj = nc.dram_tensor("proj_scratch", (IN_WIDTH, SEQ), F32, kind="Internal").ap()
    mixed = nc.dram_tensor("mixed_scratch", (D_MODEL, SEQ), F32, kind="Internal").ap()
    decay = nc.dram_tensor("decay_scratch", (B_HEADS, SEQ), F32, kind="Internal").ap()

    with ExitStack() as ctx:
        def sb(name, shape, dt=F32, scope=ctx):
            return scope.enter_context(nc.sbuf_tensor(name, shape, dt))

        def sem(name):
            return ctx.enter_context(nc.semaphore(name))

        bank = [ctx.enter_context(nc.psum_tensor(f"acc{i}", [P, HALF], F32)) for i in range(2)]
        scores = ctx.enter_context(nc.psum_tensor("scores", [P, SEQ], F32))
        turned = ctx.enter_context(nc.psum_tensor("turned", [P, SEQ], F32))
        pv = ctx.enter_context(nc.psum_tensor("pv", [P, HALF], F32))
        spare = ctx.enter_context(nc.psum_tensor("spare", [P, HALF], F32))
        banks = [bank[0][:], bank[1][:], scores[:, 0:HALF], scores[:, HALF:], turned[:, 0:HALF], turned[:, HALF:],
                 pv[:], spare[:]]

        act_hi = sb("act_hi", [P, KT, SEQ], F32R)
        act_lo = sb("act_lo", [P, KT, SEQ], F32R)
        w_raw = sb("w_raw", [P, 2, HALF])
        w_hi = sb("w_hi", [P, 2, HALF], F32R)
        w_lo = sb("w_lo", [P, 2, HALF], F32R)
        stage = sb("stage", [P, 2, HALF])
        ident = sb("ident", [P, P])
        ident_r = sb("ident_r", [P, P], F32R)
        causal_r = sb("causal_r", [P, P], F32R)
        half_ones = sb("half_ones", [P, P])
        logit_bias = sb("logit_bias", [P, 2, SEQ])
        eps_col = sb("eps_col", [P, 1])
        gains = sb("gains", [P, 4])
        out_gain = sb("out_gain", [C_DK, 2])
        fox_col = sb("fox_col", [B_HEADS, 1])
        neg_max = sb("neg_max", [P, ITEMS])
        denom = sb("denom", [P, ITEMS])
        inv_denom = sb("inv_denom", [P, ITEMS])

        first = ExitStack()
        x_tile = sb("x_tile", [P, 2, D_MODEL], scope=first)
        g_wide = sb("g_wide", [P, D_MODEL], scope=first)
        junk = sb("junk", [P, D_MODEL], scope=first)
        x_ssq = sb("x_ssq", [P, NT], scope=first)
        x_mean = sb("x_mean", [P, NT], scope=first)
        x_root = sb("x_root", [P, NT], scope=first)
        x_rstd = sb("x_rstd", [P, NT], scope=first)
        dist_i = sb("dist_i", [P, SEQ], I32, scope=first)
        mod_i = sb("mod_i", [P, SEQ], I32, scope=first)
        dist = sb("dist", [P, SEQ], scope=first)
        count = sb("count", [P, SEQ], scope=first)
        term = sb("term", [P, SEQ], scope=first)
        causal = sb("causal", [P, P], scope=first)
        ws_raw = sb("ws_raw", [P, KT, SMALL], scope=first)
        ws_hi = sb("ws_hi", [P, KT, SMALL], F32R, scope=first)
        ws_lo = sb("ws_lo", [P, KT, SMALL], F32R, scope=first)
        small = sb("small", [SMALL, SEQ], scope=first)
        lf_abs, lf_min = junk[0:B_HEADS, 0:SEQ], junk[0:B_HEADS, SEQ:]
        c_sum = sb("c_sum", [B_HEADS, SEQ], scope=first)
        first.close()

        gla = ExitStack()
        level_mask = sb("level_mask", [P, LEVELS, HEAD], scope=gla)
        gate_up = sb("gate_up", [RANK, C_DK], scope=gla)
        gate_bias = sb("gate_bias", [C_DK, 1], scope=gla)
        g_qk = sb("g_qk", [P, 2, SEQ], scope=gla)
        g_v = sb("g_v", [C_DK, 2, SEQ], scope=gla)
        g_z = sb("g_z", [C_DK, 2, SEQ], scope=gla)
        g_b = sb("g_b", [C_DK, SEQ], scope=gla)
        g_t = sb("g_t", [C_DK, 2, SEQ], scope=gla)
        q_level = sb("q_level", [C_DK, 2, HALF], scope=gla)
        k_level = sb("k_level", [C_DK, 2, SEQ], scope=gla)
        v_rows = sb("v_rows", [P, NT, C_DV], scope=gla)
        k_rows = sb("k_rows", [P, NT, C_DK], scope=gla)
        state = sb("state", [C_DK, NT, C_DV], scope=gla)
        o_ssq = sb("o_ssq", [P, NT], scope=gla)
        o_rstd = sb("o_rstd", [P, NT], scope=gla)
        o_junk = sb("o_junk", [P, 2, C_DV], scope=gla)
        gla.close()
        weights_t = logit_bias[:, 1, :]
        rank_rows = v_rows[:, :, :].rearrange("p t v -> p (t v)")[0:RANK, 0:SEQ]
        g_q, g_k = g_qk[0:C_DK, 0, :], g_qk[0:C_DK, 1, :]
        o_rows = g_qk[:, :, :].rearrange("p a b -> p (a b)")[:, 0:NT * C_DV].rearrange("p (t v) -> p t v", v=C_DV)
        q_carry, k_carry = g_v[:, 0, :], g_v[:, 1, :]

        pairs = ExitStack()
        raw = sb("raw", [P, 2, SEQ], scope=pairs)
        sq = sb("sq", [P, SEQ], scope=pairs)
        vz = sb("vz", [P, SEQ], scope=pairs)
        q_st = sb("q_st", [P, 2, SEQ], F32R, scope=pairs)
        k_hi = sb("k_hi", [P, 2, SEQ], F32R, scope=pairs)
        k_lo = sb("k_lo", [P, 2, SEQ], F32R, scope=pairs)
        v_st = sb("v_st", [P, 2, NT, P], F32R, scope=pairs)
        prob = sb("prob", [P, SEQ], scope=pairs)
        pt_hi = sb("pt_hi", [P, SEQ], F32R, scope=pairs)
        pt_lo = sb("pt_lo", [P, SEQ], F32R, scope=pairs)
        o_pair = sb("o_pair", [P, SEQ], scope=pairs)
        o_low = sb("o_low", [HEAD, HALF], scope=pairs)
        pairs.close()

        last = ExitStack()
        _held = sb("held", [P, 2, SEQ], scope=last)
        res = sb("res", [P, NT, HALF], scope=last)
        last.close()

        consts, levels_ready, eps_ready, gains_in, small_in, g_in, rounded_consts = (
            sem(n) for n in "consts levels_ready eps_ready gains_in small_in g_in rounded_consts".split())
        x_squared, x_meaned, x_rooted, x_inverted, x_normed, x_turned, x_hi_done, x_lo_done = (
            sem(n) for n in "x_squared x_meaned x_rooted x_inverted x_normed x_turned x_hi_done x_lo_done".split())
        dist_chain, ws_hi_done, ws_lo_done, small_done, small_out, small_saved, lf_step, c_done = (
            sem(n) for n in "dist_chain ws_hi_done ws_lo_done small_done small_out small_saved lf_step c_done".split())
        c_saved = sem("c_saved")
        hi_done, lo_done, quarter_done, half_done, evac_done = (
            sem(n) for n in "hi_done lo_done quarter_done half_done evac_done".split())
        q_in, k_in, v_in, z_in, sq_done, ssq_done, root_done, normed = (
            sem(n) for n in "q_in k_in v_in z_in sq_done ssq_done root_done normed".split())
        qh_done, ql_done, kh_done, kl_done, v_turned, vh_done, vl_done, e_done = (
            sem(n) for n in "qh_done ql_done kh_done kl_done v_turned vh_done vl_done e_done".split())
        e1_done, inv_done, silu_done = (
            sem(n) for n in "e1_done inv_done silu_done".split())
        s_done, masked, exp_done, recip_done, prob_done, t_done, pth_done, ptl_done = (
            sem(n) for n in "s_done masked exp_done recip_done prob_done t_done pth_done ptl_done".split())
        pv_done, o_moved, o_summed, o_done, mixed_saved = (
            sem(n) for n in "pv_done o_moved o_summed o_done mixed_saved".split())
        gla_rank_in, gla_up_in, gla_bias_in, gla_q_in, gla_k_in, gla_v_in, gla_z_in, gla_saved = (
            sem(n) for n in "gla_rank_in gla_up_in gla_bias_in gla_q_in gla_k_in gla_v_in gla_z_in gla_saved".split())
        gla_gate, gla_sum, gla_abs, gla_exp, gla_log, gla_min, gla_a, gla_scan = (
            sem(n) for n in "gla_gate gla_sum gla_abs gla_exp gla_log gla_min gla_a gla_scan".split())
        gla_scaled = sem("gla_scaled")
        gla_diag, gla_zero, gla_diff, gla_decay, gla_ql, gla_kl, gla_lv, gla_put = (
            sem(n) for n in "gla_diag gla_zero gla_diff gla_decay gla_ql gla_kl gla_lv gla_put".split())
        gla_vt, gla_vcopy, gla_eb, gla_qe, gla_ldiff, gla_le, gla_ke, gla_kt = (
            sem(n) for n in "gla_vt gla_vcopy gla_eb gla_qe gla_ldiff gla_le gla_ke gla_kt".split())
        gla_kcopy, gla_ds, gla_state = (
            sem(n) for n in "gla_kcopy gla_ds gla_state".split())
        gla_o, gla_ocopy, gla_osq, gla_ln, gla_rstd, gla_norm, gla_ot, gla_ez = (
            sem(n) for n in "gla_o gla_ocopy gla_osq gla_ln gla_rstd gla_norm gla_ot gla_ez".split())
        gla_ez1, gla_zinv, gla_silu, gla_out = (
            sem(n) for n in "gla_ez1 gla_zinv gla_silu gla_out".split())
        mix_hi, mix_lo, out_ready, out_summed = (
            sem(n) for n in "mix_hi mix_lo out_ready out_summed".split())
        bias_in = [sem("bias_landed0"), sem("bias_landed1")]
        w_in_sem = [sem("w_landed0"), sem("w_landed1")]
        x_in = [sem("x_landed0"), sem("x_landed1")]
        proj_saved = [sem("proj_saved0"), sem("proj_saved1")]
        mix_in = [sem("mix_landed0"), sem("mix_landed1")]
        res_in = [sem(f"res_landed{t}") for t in range(NT)]
        out_saved = [sem(f"out_saved{t}") for t in range(NT)]

        block = ctx.enter_context(nc.Block())

        @block.sync
        def _(sp):
            def load_quarter(s, kq, col):
                if not (isinstance(s, int) and s == 0 and kq < 2):
                    sp.wait_ge(lo_done, 4 * s + kq - 1)
                sp.dma_start(w_raw[:, kq % 2, :].rearrange("p (k c) -> p k c", k=4),
                             w_in_k[:, 4 * kq:4 * kq + 4, bass.ds(col, P)]).then_inc(w_in_sem[kq % 2], 16)

            def load_rows(dst, row, n, name):
                sp.dma_start(dst, proj[bass.ds(row, n), :]).then_inc(name, 16)

            def saved(s):
                for th in range(2):
                    sp.wait_ge(proj_saved[th], 16 * (s + 1))

            sp.dma_start(g_wide[:], norm_g[0:1, :].broadcast_to([P, D_MODEL])).then_inc(g_in, 16)
            for t in range(2):
                sp.dma_start(x_tile[:, t, :], x_rows[t * P:(t + 1) * P, :]).then_inc(x_in[t], 16)
            for n, g in enumerate((a_q_gain, a_k_gain, b_q_gain, b_k_gain)):
                for h in range(2):
                    sp.dma_start(gains[h * HEAD:(h + 1) * HEAD, n:n + 1], g.rearrange("a d -> d a")).then_inc(gains_in, 16)
            for h in range(2):
                sp.dma_start(out_gain[:, h:h + 1], gla_out_gain[0:1, h * C_DK:(h + 1) * C_DK].rearrange("a d -> d a")).then_inc(gains_in, 16)
            sp.dma_start(fox_col[:], fox_bias.rearrange("a d -> d a")).then_inc(gains_in, 16)
            sp.dma_start(ws_raw[:, :, 0:B_HEADS], w_in_k[:, :, COL_BF:COL_BF + B_HEADS]).then_inc(small_in, 16)
            sp.dma_start(ws_raw[:, :, B_HEADS:SMALL], w_in_k[:, :, COL_CR:COL_CR + RANK]).then_inc(small_in, 16)
            load_quarter(0, 0, COL_CQ)
            load_quarter(0, 1, COL_CQ)
            for t in range(2, NT):
                sp.wait_ge(x_turned, 4 * (t - 1))
                sp.dma_start(x_tile[:, t % 2, :], x_rows[t * P:(t + 1) * P, :]).then_inc(x_in[t % 2], 16)
            sp.wait_ge(small_out, 1)
            sp.dma_start(proj[COL_CR:COL_CR + RANK, :], small[B_HEADS:SMALL, :]).then_inc(small_saved, 16)
            load_quarter(0, 2, COL_CQ)
            load_quarter(0, 3, COL_CQ)
            with sp.Fori(1, C_GROUPS) as s:
                for kq in range(4):
                    load_quarter(s, kq, COL_CQ + s * P)
            def gla_loads(c):
                load_quarter(S_A0 + c, 0, c * A_WIDTH)
                load_quarter(S_A0 + c, 1, c * A_WIDTH)
                sp.wait_ge(c_done, 1)
                sp.wait_ge(small_saved, 16)
                sp.wait_ge(c_saved, 16)
                saved(C_GROUPS - 1)
                sp.wait_ge(gla_saved, 16 * c)
                load_rows(g_q, COL_CQ + c * C_DK, C_DK, gla_q_in)
                load_rows(g_k, COL_CK + c * C_DK, C_DK, gla_k_in)
                sp.dma_start(gate_up[:], gla_gate_up[0][:, bass.ds(c * C_DK, C_DK)]).then_inc(gla_up_in, 16)
                sp.dma_start(gate_bias[:], gla_gate_bias[0:1, bass.ds(c * C_DK, C_DK)].rearrange("a d -> d a")).then_inc(gla_bias_in, 16)
                load_rows(rank_rows, COL_CR, RANK, gla_rank_in)
                sp.dma_start(g_v[:, :, :], proj[bass.ds(COL_CV + c * C_DV, C_DV), :].rearrange(
                    "(h p) t -> p h t", p=C_DK)).then_inc(gla_v_in, 16)
                sp.dma_start(g_z[:, :, :], proj[bass.ds(COL_CZ + c * C_DV, C_DV), :].rearrange(
                    "(h p) t -> p h t", p=C_DK)).then_inc(gla_z_in, 16)
                load_quarter(S_A0 + c, 2, c * A_WIDTH)
                load_quarter(S_A0 + c, 3, c * A_WIDTH)

            gla_loads(0)
            with sp.Fori(1, C_HEADS) as c:
                gla_loads(c)

            def pair_loads(pair, base, stride, row, next_group, next_base, next_stride, next_row):
                def weights(g, kqs):
                    if next_group is not None:
                        for kq in kqs:
                            load_quarter(next_group + g, kq, next_base + g * next_stride + next_row)

                weights(0, range(3))
                sp.wait_ge(gla_saved, 16 * C_HEADS)
                sp.wait_ge(ql_done, 2 * pair)
                saved(S_A0 + PAIR_GROUPS * pair + 1)
                load_rows(raw[:, 0, :], base + row, P, q_in)
                sp.wait_ge(kl_done, 4 * pair)
                load_rows(raw[:, 1, :], base + stride + row, P, k_in)
                weights(0, (3,))
                saved(S_A0 + PAIR_GROUPS * pair + 3)
                sp.wait_ge(o_done, 4 * pair)
                load_rows(vz[:], base + 2 * stride + row, P, v_in)
                if base == COL_B:
                    sp.wait_ge(masked, ITEMS * pair)
                    for h in range(2):
                        sp.dma_start(logit_bias[:, h, :], decay[bass.ds(2 * (pair - A_PAIRS) + h, 1), :]
                                         .broadcast_to([P, SEQ])).then_inc(bias_in[h], 16)
                sp.wait_ge(v_turned, 2 * (pair + 1))
                load_rows(vz[:], base + 3 * stride + row, P, z_in)
                for g in range(1, PAIR_GROUPS):
                    weights(g, range(4))

            def load_out_quarter(cg, kk):
                sp.wait_ge(lo_done, Q_OUT + 16 * cg + kk - 1)
                sp.dma_start(w_raw[:, kk % 2, :], w_out_k[:, OUT_ORDER[kk], bass.ds(cg * HALF, HALF)])\
                    .then_inc(w_in_sem[kk % 2], 16)

            pair_loads(0, 0, A_WIDTH, 0, S_LOOP_A, 0, A_WIDTH, P)
            with sp.Fori(1, A_PAIRS - 1) as p:
                pair_loads(p, 0, A_WIDTH, p * P, S_LOOP_A + 4 * p, 0, A_WIDTH, (p + 1) * P)
            pair_loads(A_PAIRS - 1, 0, A_WIDTH, (A_PAIRS - 1) * P, S_B0, COL_B, B_WIDTH, 0)
            with sp.Fori(0, B_PAIRS - 1) as p:
                pair_loads(A_PAIRS + p, COL_B, B_WIDTH, p * P, S_LOOP_B + 4 * p, COL_B, B_WIDTH, (p + 1) * P)
            load_out_quarter(0, 0)
            load_out_quarter(0, 1)
            pair_loads(A_PAIRS + B_PAIRS - 1, COL_B, B_WIDTH, (B_PAIRS - 1) * P, None, 0, 0, 0)

            def load_res(cg):
                for t in range(NT):
                    if not isinstance(cg, int):
                        sp.wait_ge(out_saved[t], 16 * cg)
                    sp.dma_start(res[:, t, :], x_rows[t * P:(t + 1) * P, bass.ds(cg * HALF, HALF)])\
                        .then_inc(res_in[t], 16)

            def save_out(cg, t):
                sp.wait_ge(out_summed, NT * cg + t + 1)
                sp.dma_start(out_rows[t * P:(t + 1) * P, bass.ds(cg * HALF, HALF)], res[:, t, :])\
                    .then_inc(out_saved[t], 16)

            sp.wait_ge(ql_done, 2 * (A_PAIRS + B_PAIRS))
            sp.wait_ge(kl_done, 4 * (A_PAIRS + B_PAIRS))
            for kk in range(KT):
                if kk == 0:
                    sp.wait_ge(mixed_saved, 16 * (A_PAIRS + B_PAIRS - 1))
                    sp.wait_ge(gla_saved, 16 * C_HEADS)
                if kk == KT - 1:
                    sp.wait_ge(mixed_saved, 16 * (A_PAIRS + B_PAIRS))
                if kk >= 2:
                    sp.wait_ge(mix_lo, kk - 1)
                sp.dma_start(raw[:, kk % 2, :], mixed[OUT_ORDER[kk] * P:(OUT_ORDER[kk] + 1) * P, :])\
                    .then_inc(mix_in[kk % 2], 16)
            sp.wait_ge(o_done, 4 * (A_PAIRS + B_PAIRS))
            sp.wait_ge(mixed_saved, 16 * (A_PAIRS + B_PAIRS))
            load_res(0)
            for kk in range(2, KT):
                load_out_quarter(0, kk)
            with sp.Fori(1, OUT_CG) as cg:
                load_out_quarter(cg, 0)
                load_out_quarter(cg, 1)
                for t in range(NT):
                    save_out(cg - 1, t)
                load_res(cg)
                for kk in range(2, KT):
                    load_out_quarter(cg, kk)
            for t in range(NT):
                save_out(OUT_CG - 1, t)
            for t in range(NT):
                sp.wait_ge(out_saved[t], 16 * OUT_CG)

        @block.gpsimd
        def _(pool):
            pool.memset(eps_col[:], EPS).then_inc(eps_ready, 1)
            pool.memset(ident[:], 0.0).then_inc(consts, 1)
            pool.memset(causal[:], 0.0).then_inc(consts, 1)
            pool.memset(half_ones[:], 0.0).then_inc(consts, 1)
            pool.wait_ge(consts, 3)
            pool.affine_select(out=ident[:], in_=ident[:], compare_op=ALU.not_equal, fill=1.0, base=0,
                                   pattern=[[-1, P]], channel_multiplier=1).then_inc(consts, 1)
            pool.affine_select(out=causal[:], in_=causal[:], compare_op=ALU.is_ge, fill=FAR, base=0,
                                   pattern=[[-1, P]], channel_multiplier=1).then_inc(consts, 1)
            pool.wait_ge(consts, 5)
            pool.memset(half_ones[0:HEAD, 0:HEAD], 1.0).then_inc(consts, 1)
            pool.wait_ge(consts, 6)
            pool.memset(half_ones[HEAD:P, HEAD:P], 1.0).then_inc(consts, 1)
            pool.wait_ge(consts, 7)
            pool.iota(dist_i[:], [[-1, SEQ]], base=(NT - 1) * P, channel_multiplier=1).then_inc(consts, 1)

            pool.wait_ge(c_done, 1)
            pool.wait_ge(small_saved, 16)
            pool.wait_ge(c_saved, 16)
            pool.memset(level_mask[:, :, :], 1.0).then_inc(levels_ready, 1)
            pool.wait_ge(levels_ready, 1)
            for l in range(LEVELS):
                b = 1 << l
                v = level_mask[:, l, :].rearrange("p (n r) -> p n r", r=b)
                pool.affine_select(out=v, in_=v, compare_op=ALU.is_ge, fill=0.0, base=0,
                                       pattern=[[-2 * b, HEAD // b], [0, b]], channel_multiplier=1).then_inc(levels_ready, 1)
            pool.wait_ge(levels_ready, 1 + LEVELS)
            for l in range(LEVELS):
                b = 1 << l
                v = level_mask[:, l, :].rearrange("p (n r) -> p n r", r=b)
                pool.affine_select(out=v, in_=v, compare_op=ALU.is_ge, fill=0.0, base=b - 1,
                                       pattern=[[2 * b, HEAD // b], [0, b]], channel_multiplier=-1).then_inc(levels_ready, 1)
            pool.memset(k_level[:, :, :], 0.0).then_inc(levels_ready, 1)
            pool.wait_ge(levels_ready, 2 + 2 * LEVELS)

            def gla_head(c):
                pool.wait_ge(gla_scaled, c + 1)
                pool.wait_ge(gla_k_in, 16 * (c + 1))
                for l in range(LEVELS):
                    b, n = 1 << l, LEVELS * c + l
                    pool.wait_ge(gla_lv, n - 1 if l >= 2 else LEVELS * c)
                    pool.wait_ge(gla_decay, n + 1)
                    pool.tensor_tensor(q_level[:, l % 2, :].rearrange("p (n r) -> p n r", r=b),
                                           blocks(g_q, b)[:, :, 1, :], blocks(g_t[:, l % 2, :], b)[:, :, 1, :],
                                           ALU.mult).then_inc(gla_ql, 1)
                    pool.tensor_tensor(blocks(k_level[:, l % 2, :], b)[:, :, 0, :], blocks(g_k, b)[:, :, 0, :],
                                           blocks(g_t[:, l % 2, :], b)[:, :, 0, :], ALU.mult).then_inc(gla_kl, 1)
                pool.wait_ge(gla_vt, 4 * (c + 1))
                pool.wait_ge(gla_eb, c + 1)
                pool.tensor_tensor(q_carry, g_q, g_t[:, 0, :], ALU.mult).then_inc(gla_qe, 1)
                pool.wait_ge(gla_le, c + 1)
                pool.tensor_tensor(k_carry, g_k, g_t[:, 1, :], ALU.mult).then_inc(gla_ke, 1)
                pool.wait_ge(gla_zinv, c + 1)
                pool.tensor_tensor(g_z[:, :, :], g_z[:, :, :], g_t[:, :, :], ALU.mult).then_inc(gla_silu, 1)

            gla_head(0)
            with pool.Fori(1, C_HEADS) as c:
                gla_head(c)

        @block.scalar
        def _(act):
            def split_hi(s, kq):
                slot = kq % 2
                if kq == 1 and not (isinstance(s, int) and s == 0):
                    act.wait_ge(half_done, 2 * s)
                if kq >= 2:
                    act.wait_ge(quarter_done, 3 * s + kq - 1)
                act.wait_ge(w_in_sem[slot], 16 * (2 * s + kq // 2 + 1))
                act.activation(w_hi[:, slot, :], w_raw[:, slot, :], ACT.Copy).then_inc(hi_done, 1)

            def split_hi_out(cg, kk):
                slot = kk % 2
                if kk == 1:
                    act.wait_ge(half_done, 2 * GROUPS) if isinstance(cg, int) and cg == 0 else \
                        act.wait_ge(out_ready, NT * cg)
                else:
                    act.wait_ge(quarter_done, 3 * GROUPS + (KT - 1) * cg + kk - 1)
                act.wait_ge(w_in_sem[slot], 16 * (2 * GROUPS + 8 * cg + kk // 2 + 1))
                act.activation(w_hi[:, slot, :], w_raw[:, slot, :], ACT.Copy).then_inc(hi_done, 1)

            def evac(s, th):
                act.wait_ge(half_done, 2 * s + th + 1)
                if not (isinstance(s, int) and s == 0):
                    act.wait_ge(proj_saved[th], 16 * s)
                act.activation(stage[:, th, :], bank[th][:], ACT.Copy).then_inc(evac_done, 1)

            def save(s, row):
                for th in range(2):
                    act.wait_ge(evac_done, 2 * s + th + 1)
                    act.dma_start(proj[bass.ds(row, P), th * HALF:(th + 1) * HALF], stage[:, th, :])\
                        .then_inc(proj_saved[th], 16)

            def group(s, row, steps):
                for slot in range(8):
                    if slot % 2 == 0:
                        split_hi(s, slot // 2 + 1)
                    if slot == 7:
                        evac(s, 0)
                    steps(slot)
                evac(s, 1)
                save(s, row)

            act.wait_ge(eps_ready, 1)
            for t in range(NT + 1):
                if t < NT:
                    act.wait_ge(x_in[t % 2], 16 * (t // 2 + 1))
                    act.activation(junk[:], x_tile[:, t % 2, :], ACT.Square, accum_out=x_ssq[:, t:t + 1]).then_inc(x_squared, 1)
                    act.wait_ge(x_meaned, t + 1)
                    act.activation(x_root[:, t:t + 1], x_mean[:, t:t + 1], ACT.Sqrt).then_inc(x_rooted, 1)
                if t >= 1:
                    for b in range(4):
                        act.wait_ge(x_turned, 4 * (t - 1) + b + 1)
                        act.activation(act_hi[:, 4 * b:4 * b + 4, (t - 1) * P:t * P],
                                           banks[4 * ((t - 1) % 2) + b].rearrange("p (k t) -> p k t", k=4), ACT.Copy).then_inc(x_hi_done, 1)
            act.wait_ge(small_in, 32)
            act.activation(ws_hi[:, :, :], ws_raw[:, :, :], ACT.Copy).then_inc(ws_hi_done, 1)
            split_hi(0, 0)
            act.wait_ge(consts, 8)
            act.activation(ident_r[:], ident[:], ACT.Copy).then_inc(rounded_consts, 1)
            act.activation(causal_r[:], causal[:], ACT.Copy).then_inc(rounded_consts, 1)
            act.wait_ge(small_done, 1)
            act.activation(small[:], scores[0:SMALL, :], ACT.Copy).then_inc(small_out, 1)

            group(0, COL_CQ, lambda slot: None)
            with act.Fori(1, C_GROUPS) as s:
                group(s, COL_CQ + s * P, lambda slot: None)

            act.wait_ge(lf_step, 1)
            act.activation(lf_abs, lf_min, ACT.Abs).then_inc(lf_step, 1)
            act.wait_ge(lf_step, 2)
            act.activation(lf_abs, lf_abs, ACT.Exp, scale=-1.0).then_inc(lf_step, 1)
            act.wait_ge(lf_step, 3)
            act.activation(lf_abs, lf_abs, ACT.Ln, bias=1.0).then_inc(lf_step, 1)
            act.wait_ge(c_done, 1)
            act.dma_start(decay[:, :], c_sum[:]).then_inc(c_saved, 16)

            def gla_steps(c, slot):
                if slot == 0:
                    act.wait_ge(gla_q_in, 16 * (c + 1))
                    act.mul(g_q, g_q, float(C_DK) ** -0.5).then_inc(gla_scaled, 1)
                    act.wait_ge(gla_sum, c + 1)
                    act.activation(g_t[:, 1, :], g_t[:, 0, :], ACT.Abs).then_inc(gla_abs, 1)
                    act.wait_ge(gla_abs, c + 1)
                    act.activation(g_t[:, 1, :], g_t[:, 1, :], ACT.Exp, scale=-1.0).then_inc(gla_exp, 1)
                    act.wait_ge(gla_exp, c + 1)
                    act.activation(g_t[:, 1, :], g_t[:, 1, :], ACT.Ln, bias=1.0).then_inc(gla_log, 1)
                if 1 <= slot <= 3:
                    for l in LEVELS_AT[slot]:
                        act.wait_ge(gla_diff, 2 * (LEVELS * c + l) + 2)
                        act.activation(g_t[:, l % 2, :], g_t[:, l % 2, :], ACT.Exp).then_inc(gla_decay, 1)
                if slot == 4:
                    for i in range(4):
                        act.wait_ge(gla_vt, 4 * c + i + 1)
                        act.activation(v_rows[:, 2 * i:2 * i + 2, :],
                                           banks[2 + i][:, 0:2 * C_DV].rearrange("p (t v) -> p t v", t=2), ACT.Copy).then_inc(gla_vcopy, 1)
                    act.wait_ge(gla_kl, LEVELS * (c + 1))
                    act.activation(g_t[:, 0, :], g_b[:], ACT.Exp).then_inc(gla_eb, 1)
                    act.wait_ge(gla_ldiff, c + 1)
                    act.activation(g_t[:, 1, :], g_t[:, 1, :], ACT.Exp).then_inc(gla_le, 1)
                    for i in range(2):
                        act.wait_ge(gla_kt, 2 * c + i + 1)
                        act.activation(k_rows[:, 4 * i:4 * i + 4, :],
                                           banks[6 + i][:, 0:4 * C_DK].rearrange("p (t d) -> p t d", t=4), ACT.Copy).then_inc(gla_kcopy, 1)
                if slot == 6:
                    act.wait_ge(gla_ke, c + 1)
                    act.wait_ge(gla_z_in, 16 * (c + 1))
                    act.wait_ge(gla_state, (NT - 1) * (c + 1))
                    act.activation(g_t[:, :, :], g_z[:, :, :], ACT.Exp, scale=-1.0).then_inc(gla_ez, 1)
                    for i in range(4):
                        act.wait_ge(gla_o, 4 * c + i + 1)
                        act.activation(o_rows[:, 2 * i:2 * i + 2, :],
                                           banks[2 + i][:, 0:2 * C_DV].rearrange("p (t v) -> p t v", t=2), ACT.Copy).then_inc(gla_ocopy, 1)
                        act.wait_ge(gla_ocopy, 4 * c + i + 1)
                        for t in (2 * i, 2 * i + 1):
                            act.wait_ge(gla_osq, NT * c + max(t - 1, 0))
                            ins = act.activation(o_junk[:, t % 2, :], o_rows[:, t, :], ACT.Square, accum_out=o_ssq[:, t:t + 1])
                            ins.then_inc(gla_osq, 1)
                    act.wait_ge(gla_osq, NT * (c + 1))
                    act.activation(o_rstd[:], o_ssq[:], ACT.Ln, scale=1.0 / C_DV, bias=eps_col[:]).then_inc(gla_ln, 1)
                    act.wait_ge(gla_ln, c + 1)
                    act.activation(o_rstd[:], o_rstd[:], ACT.Exp, scale=-0.5).then_inc(gla_rstd, 1)
                if slot == 7:
                    act.wait_ge(gla_out, 2 * (c + 1))
                    act.dma_start(mixed[bass.ds(A_WIDTH + B_WIDTH + c * C_DV, C_DV), :].rearrange(
                        "(h p) t -> p h t", p=C_DK), g_z[:, :, :]).then_inc(gla_saved, 16)

            group(S_A0, 0, lambda slot: gla_steps(0, slot))
            with act.Fori(1, C_HEADS) as c:
                group(S_A0 + c, c * A_WIDTH, lambda slot: gla_steps(c, slot))

            def norm(pair):
                for i, (name, ps) in enumerate(((q_in, scores), (k_in, turned))):
                    act.wait_ge(name, 16 * (pair + 1))
                    if i == 1:
                        act.wait_ge(normed, 2 * pair + 1)
                    else:
                        act.wait_ge(silu_done, pair)
                    act.activation(sq[:], raw[:, i, :], ACT.Square).then_inc(sq_done, 1)
                    act.wait_ge(ssq_done, 2 * pair + i + 1)
                    act.activation(sq[:], ps[:], ACT.Ln, scale=1.0 / HEAD, bias=eps_col[:]).then_inc(root_done, 1)
                    act.wait_ge(root_done, 4 * pair + 2 * i + 1)
                    act.activation(sq[:], sq[:], ACT.Exp, scale=-0.5).then_inc(root_done, 1)

            def stack(pair):
                act.wait_ge(normed, 2 * pair + 1)
                for h in range(2):
                    own = slice(h * HEAD, (h + 1) * HEAD)
                    act.activation(q_st[own, h, :], raw[own, 0, :], ACT.Copy).then_inc(qh_done, 1)
                act.wait_ge(normed, 2 * pair + 2)
                for h in range(2):
                    own, other = slice(h * HEAD, (h + 1) * HEAD), slice((1 - h) * HEAD, (2 - h) * HEAD)
                    act.activation(k_hi[own, h, :], raw[own, 1, :], ACT.Copy).then_inc(kh_done, 1)
                    act.activation(k_hi[other, h, :], raw[own, 1, :], ACT.Copy).then_inc(kh_done, 1)

            def values(pair):
                for b in range(2):
                    act.wait_ge(v_turned, 2 * pair + b + 1)
                    for h in range(2):
                        src = turned[:, b * HALF:(b + 1) * HALF].rearrange("p (t c) -> p t c", t=4)
                        act.activation(v_st[:, h, 4 * b:4 * b + 4, 0:HEAD], src[:, :, h * HEAD:(h + 1) * HEAD],
                                           ACT.Copy).then_inc(vh_done, 1)

            def gate(pair):
                act.wait_ge(z_in, 16 * (pair + 1))
                act.wait_ge(normed, 2 * pair + 2)
                act.activation(sq[:], vz[:], ACT.Exp, scale=-1.0).then_inc(e_done, 1)

            def score(pair, j):
                n = (j % NT + 1) * P
                act.wait_ge(masked, ITEMS * pair + j + 1)
                act.activation(prob[:, 0:n], prob[:, 0:n], ACT.Exp, scale=-1.0, bias=neg_max[:, j:j + 1],
                                   accum_out=denom[:, j:j + 1]).then_inc(exp_done, 1)

            def turn(pair, j):
                n = (j % NT + 1) * P
                act.wait_ge(pv_done, ITEMS * pair + j)
                act.wait_ge(t_done, ITEMS * pair + j + 1)
                act.activation(pt_hi[:, 0:n], turned[:, 0:n], ACT.Copy).then_inc(pth_done, 1)

            def product(pair, j):
                if j % 4 == 3:
                    u = j // 4
                    act.wait_ge(o_summed, 4 * pair + u)
                    act.wait_ge(pv_done, ITEMS * pair + j + 1)
                    act.activation(o_low[:], pv[HEAD:P, :], ACT.Copy).then_inc(o_moved, 1)

            def steps_at(pair, slot):
                for name, j in steps_of(slot):
                    if name == "norm":
                        norm(pair)
                    elif name == "stack":
                        stack(pair)
                    elif name == "values":
                        values(pair)
                    elif name == "gate":
                        gate(pair)
                    elif name == "score":
                        score(pair, j)
                    elif name == "turn":
                        turn(pair, j)
                    elif name == "product":
                        product(pair, j)

            def pair_body(pair, s0, base, stride, row, projecting=True):
                for g in range(PAIR_GROUPS):
                    def steps(slot, g=g):
                        steps_at(pair, 8 * g + slot)
                    if projecting:
                        group(s0 + g, base + g * stride + row, steps)
                    else:
                        for slot in range(8):
                            steps(slot)
                            mix_hi_part(8 * g + slot - MIX_SLOT)
                steps_at(pair, SLOTS)
                act.wait_ge(o_done, 4 * (pair + 1))
                act.dma_start(mixed[bass.ds(pair * P, P), :], o_pair[:]).then_inc(mixed_saved, 16)

            def mix_hi_part(kk):
                if 0 <= kk < KT - 1:
                    act.wait_ge(mix_in[kk % 2], 16 * (kk // 2 + 1))
                    act.wait_ge(half_done, 2 * GROUPS)
                    act.activation(act_hi[:, OUT_ORDER[kk], :], raw[:, kk % 2, :], ACT.Copy).then_inc(mix_hi, 1)

            pair_body(0, S_LOOP_A, 0, A_WIDTH, P)
            with act.Fori(1, A_PAIRS - 1) as p:
                pair_body(p, S_LOOP_A + 4 * p, 0, A_WIDTH, (p + 1) * P)
            pair_body(A_PAIRS - 1, S_B0, COL_B, B_WIDTH, 0)
            with act.Fori(0, B_PAIRS - 1) as p:
                pair_body(A_PAIRS + p, S_LOOP_B + 4 * p, COL_B, B_WIDTH, (p + 1) * P)
            pair_body(A_PAIRS + B_PAIRS - 1, None, 0, 0, 0, projecting=False)

            kk = KT - 1
            act.wait_ge(mix_in[kk % 2], 16 * (kk // 2 + 1))
            act.activation(act_hi[:, OUT_ORDER[kk], :], raw[:, kk % 2, :], ACT.Copy).then_inc(mix_hi, 1)
            for kk in range(KT):
                split_hi_out(0, kk + 1)
            with act.Fori(1, OUT_CG - 1) as cg:
                for kk in range(KT):
                    split_hi_out(cg, kk + 1)
            for kk in range(KT - 1):
                split_hi_out(OUT_CG - 1, kk + 1)

        @block.vector
        def _(dve):
            def split_lo(s, kq):
                slot = kq % 2
                dve.wait_ge(hi_done, 4 * s + kq + 1)
                dve.tensor_tensor(w_lo[:, slot, :], w_raw[:, slot, :], w_hi[:, slot, :].bitcast(F32), ALU.subtract).then_inc(lo_done, 1)

            def group(s, steps):
                for slot in range(8):
                    if slot % 2 == 0:
                        split_lo(s, slot // 2 + 1)
                    steps(slot)

            for t in range(NT + 1):
                if t < NT:
                    dve.wait_ge(x_squared, t + 1)
                    dve.tensor_scalar(x_mean[:, t:t + 1], x_ssq[:, t:t + 1], 1.0 / D_MODEL, EPS, ALU.mult, ALU.add).then_inc(x_meaned, 1)
                    dve.wait_ge(x_rooted, t + 1)
                    dve.reciprocal(x_rstd[:, t:t + 1], x_root[:, t:t + 1]).then_inc(x_inverted, 1)
                    dve.wait_ge(g_in, 16)
                    dve.wait_ge(x_inverted, t + 1)
                    dve.scalar_tensor_tensor(out=x_tile[:, t % 2, :], in0=x_tile[:, t % 2, :],
                                                 scalar=x_rstd[:, t:t + 1], in1=g_wide[:], op0=ALU.mult, op1=ALU.mult).then_inc(x_normed, 1)
                if t >= 1:
                    for b in range(4):
                        dve.wait_ge(x_hi_done, 4 * (t - 1) + b + 1)
                        at = (slice(None), slice(4 * b, 4 * b + 4), slice((t - 1) * P, t * P))
                        dve.tensor_tensor(act_lo[at], banks[4 * ((t - 1) % 2) + b].rearrange(
                            "p (k t) -> p k t", k=4), act_hi[at].bitcast(F32), ALU.subtract).then_inc(x_lo_done, 1)
            dve.wait_ge(ws_hi_done, 1)
            dve.tensor_tensor(ws_lo[:, :, :], ws_raw[:, :, :], ws_hi[:, :, :].bitcast(F32), ALU.subtract).then_inc(ws_lo_done, 1)
            split_lo(0, 0)

            step = [0]

            def link(ins):
                step[0] += 1
                ins.then_inc(dist_chain, 1)
                dve.wait_ge(dist_chain, step[0])

            dve.wait_ge(consts, 8)
            link(dve.tensor_copy(dist[:], dist_i[:]))
            link(dve.tensor_scalar(mod_i[:], dist_i[:], 3, None, ALU.bitwise_and))
            link(dve.tensor_copy(term[:], mod_i[:]))
            link(dve.tensor_scalar(term[:], term[:], 0.0, None, ALU.is_equal))
            link(dve.scalar_tensor_tensor(out=count[:], in0=dist[:], scalar=512.0, in1=term[:], op0=ALU.is_le, op1=ALU.mult))
            link(dve.scalar_tensor_tensor(out=count[:], in0=dist[:], scalar=128.0, in1=count[:], op0=ALU.is_le, op1=ALU.add))
            link(dve.tensor_scalar(mod_i[:], dist_i[:], 15, None, ALU.bitwise_and))
            link(dve.tensor_copy(term[:], mod_i[:]))
            link(dve.tensor_scalar(term[:], term[:], 0.0, None, ALU.is_equal))
            link(dve.tensor_tensor(count[:], count[:], term[:], ALU.add))
            link(dve.scalar_tensor_tensor(out=count[:], in0=dist[:], scalar=0.0, in1=count[:], op0=ALU.is_ge, op1=ALU.mult))
            link(dve.tensor_scalar(term[:], count[:], 0.5, FAR, ALU.is_lt, ALU.mult))
            link(dve.tensor_scalar(dist[:], count[:], 1.5, -LN2, ALU.is_ge, ALU.mult))
            link(dve.tensor_tensor(term[:], term[:], dist[:], ALU.add))
            link(dve.tensor_scalar(dist[:], count[:], 2.5, LN2 - LN3, ALU.is_ge, ALU.mult))
            link(dve.tensor_tensor(logit_bias[:, 0, :], term[:], dist[:], ALU.add))
            dve.wait_ge(gains_in, 16 * 11)
            for n in (0, 2):
                link(dve.tensor_scalar(gains[:, n:n + 1], gains[:, n:n + 1], -float(HEAD) ** -0.5, None, ALU.mult))

            group(0, lambda slot: None)
            with dve.Fori(1, C_GROUPS) as s:
                group(s, lambda slot: None)

            dve.wait_ge(small_out, 1)
            dve.tensor_scalar(lf_min, small[0:B_HEADS, :], fox_col[:], None, ALU.add).then_inc(lf_step, 1)
            dve.wait_ge(lf_step, 4)
            dve.scalar_tensor_tensor(out=lf_min, in0=lf_min, scalar=0.0, in1=lf_abs, op0=ALU.min,
                                         op1=ALU.subtract).then_inc(lf_step, 1)
            dve.wait_ge(lf_step, 5)
            dve.tensor_tensor_scan(out=c_sum[:], data0=lf_min, data1=lf_min, initial=0.0, op0=ALU.add,
                                       op1=ALU.bypass).then_inc(c_done, 1)

            dve.wait_ge(levels_ready, 2 + 2 * LEVELS)
            levels_put, items_scored = dve.alloc_register("levels_put"), dve.alloc_register("items_scored")
            dve.reg_mov(levels_put, 0)
            dve.reg_mov(items_scored, 0)

            def gla_steps(c, slot):
                if slot == 0:
                    dve.wait_ge(gla_bias_in, 16 * (c + 1))
                    dve.wait_ge(gla_silu, c)
                    dve.wait_ge(gla_gate, c + 1)
                    dve.tensor_scalar(g_t[:, 0, :], scores[0:C_DK, :], gate_bias[:], None, ALU.add).then_inc(gla_sum, 1)
                    dve.wait_ge(gla_log, c + 1)
                    dve.tensor_scalar(g_t[:, 0, :], g_t[:, 0, :], 0.0, 1.0 / 16, ALU.min, ALU.mult).then_inc(gla_min, 1)
                    dve.wait_ge(gla_min, c + 1)
                    dve.scalar_tensor_tensor(out=g_t[:, 0, :], in0=g_t[:, 1, :], scalar=-1.0 / 16, in1=g_t[:, 0, :],
                                                 op0=ALU.mult, op1=ALU.add).then_inc(gla_a, 1)
                    dve.wait_ge(gla_a, c + 1)
                    for t in range(NT):
                        at = slice(t * P, (t + 1) * P)
                        dve.tensor_tensor_scan(out=g_b[:, at], data0=g_t[:, 0, at], data1=g_t[:, 0, at],
                                                   initial=0.0, op0=ALU.add, op1=ALU.bypass).then_inc(gla_scan, 1)
                    dve.wait_ge(gla_scan, NT * (c + 1))
                    dve.memset(weights_t, 0.0).then_inc(gla_zero, 1)
                    dve.wait_ge(gla_zero, c + 1)
                    dve.wait_ge(gla_diag, c + 1)
                    put(weights_t.rearrange("p (t q) -> p t q", t=NT),
                        ident[:].unsqueeze(1).broadcast_to([P, NT, P]), turned[:].rearrange("p (t q) -> p t q", t=NT))
                if 1 <= slot <= 3:
                    for l in LEVELS_AT[slot]:
                        b, n = 1 << l, LEVELS * c + l
                        bv, ev = blocks(g_b[:], b), blocks(g_t[:, l % 2, :], b)
                        edge = bv[:, :, 0, b - 1:b].broadcast_to([C_DK, SEQ // (2 * b), b])
                        dve.wait_ge(gla_kl, n - 1 if l >= 2 else LEVELS * c)
                        dve.tensor_tensor(ev[:, :, 1, :], bv[:, :, 1, :], edge, ALU.subtract).then_inc(gla_diff, 1)
                        dve.tensor_tensor(ev[:, :, 0, :], edge, bv[:, :, 0, :], ALU.subtract).then_inc(gla_diff, 1)
                        if l >= 1:
                            put_level(c, l - 1)
                if slot == 4:
                    put_level(c, LEVELS - 1)
                    dve.wait_ge(gla_kl, LEVELS * (c + 1) - 1)
                    bt = g_b[:].rearrange("p (t q) -> p t q", t=NT)
                    dve.tensor_tensor(g_t[:, 1, :].rearrange("p (t q) -> p t q", t=NT),
                                          bt[:, :, P - 1:P].broadcast_to([C_DK, NT, P]), bt, ALU.subtract).then_inc(gla_ldiff, 1)
                if slot == 6:
                    for t in range(1, NT):
                        i = t - 1
                        src = banks[2 + i // 2][0:C_DK, (i % 2) * C_DV:(i % 2 + 1) * C_DV]
                        if t == 1:
                            dve.wait_ge(gla_eb, c + 1)
                            dve.wait_ge(gla_ds, c + 1)
                            dve.tensor_copy(state[:, 1, :], src).then_inc(gla_state, 1)
                        else:
                            dve.wait_ge(gla_state, (NT - 1) * c + t - 1)
                            dve.scalar_tensor_tensor(out=state[:, t, :], in0=state[:, t - 1, :],
                                                         scalar=g_t[:, 0, i * P + P - 1:i * P + P], in1=src,
                                                         op0=ALU.mult, op1=ALU.add).then_inc(gla_state, 1)
                    dve.wait_ge(gla_ez, c + 1)
                    dve.tensor_scalar(g_t[:, :, :], g_t[:, :, :], 1.0, None, ALU.add).then_inc(gla_ez1, 1)
                    dve.wait_ge(gla_ez1, c + 1)
                    dve.reciprocal(g_t[:, :, :], g_t[:, :, :]).then_inc(gla_zinv, 1)
                    dve.wait_ge(gla_rstd, c + 1)
                    dve.tensor_tensor(o_rows, o_rows, o_rstd[:].unsqueeze(2).broadcast_to([P, NT, C_DV]), ALU.mult).then_inc(gla_norm, 1)
                if slot == 7:
                    dve.wait_ge(gla_silu, c + 1)
                    for h in range(2):
                        dve.wait_ge(gla_ot, 2 * c + h + 1)
                        dve.scalar_tensor_tensor(out=g_z[:, h, :], in0=(scores, turned)[h][0:C_DK, :],
                                                     scalar=out_gain[:, h:h + 1], in1=g_z[:, h, :], op0=ALU.mult,
                                                     op1=ALU.mult).then_inc(gla_out, 1)

            def put(dst, mask, data):
                dve.reg_add(levels_put, levels_put, 1)
                dve.copy_predicated(dst, mask.bitcast(I32), data).then_inc(gla_put, 1)

            def put_level(c, l):
                b = 1 << l
                dve.wait_ge(gla_put, levels_put)
                dve.wait_ge(gla_lv, LEVELS * c + l + 1)
                put(blocks(weights_t, b)[:, :, 1, :].rearrange("p (t n) r -> p t n r", t=NT),
                    level_mask[:, l, :].rearrange("p (n r) -> p n r", r=b).unsqueeze(1).broadcast_to([P, NT, HEAD // b, b]),
                    banks[6 + l % 2].rearrange("p (t n r) -> p t n r", t=NT, r=b))

            group(S_A0, lambda slot: gla_steps(0, slot))
            with dve.Fori(1, C_HEADS) as c:
                group(S_A0 + c, lambda slot: gla_steps(c, slot))

            def norm(pair, kind):
                for i in range(2):
                    dve.wait_ge(root_done, 4 * pair + 2 * i + 2)
                    dve.scalar_tensor_tensor(out=raw[:, i, :], in0=raw[:, i, :],
                                                 scalar=gains[:, 2 * kind + i:2 * kind + i + 1], in1=sq[:],
                                                 op0=ALU.mult, op1=ALU.mult).then_inc(normed, 1)

            def stack(pair):
                for h in range(2):
                    own, other = slice(h * HEAD, (h + 1) * HEAD), slice((1 - h) * HEAD, (2 - h) * HEAD)
                    dve.wait_ge(qh_done, 2 * pair + h + 1)
                    dve.tensor_tensor(q_st[other, h, :], raw[own, 0, :], q_st[own, h, :].bitcast(F32), ALU.subtract).then_inc(ql_done, 1)
                for h in range(2):
                    own = slice(h * HEAD, (h + 1) * HEAD)
                    dve.wait_ge(kh_done, 4 * pair + 2 * h + 2)
                    for to in (slice(0, HEAD), slice(HEAD, P)):
                        dve.tensor_tensor(k_lo[to, h, :], raw[own, 1, :], k_hi[own, h, :].bitcast(F32),
                                              ALU.subtract).then_inc(kl_done, 1)

            def values(pair):
                for b in range(2):
                    dve.wait_ge(vh_done, 4 * pair + 2 * b + 2)
                    for h in range(2):
                        src = turned[:, b * HALF:(b + 1) * HALF].rearrange("p (t c) -> p t c", t=4)
                        at = v_st[:, h, 4 * b:4 * b + 4, :]
                        dve.tensor_tensor(at[:, :, HEAD:P], src[:, :, h * HEAD:(h + 1) * HEAD],
                                              at[:, :, 0:HEAD].bitcast(F32), ALU.subtract).then_inc(vl_done, 1)

            def gate(pair):
                dve.wait_ge(e_done, pair + 1)
                dve.tensor_scalar(sq[:], sq[:], 1.0, None, ALU.add).then_inc(e1_done, 1)
                dve.wait_ge(e1_done, pair + 1)
                dve.reciprocal(sq[:], sq[:]).then_inc(inv_done, 1)
                dve.wait_ge(inv_done, pair + 1)
                dve.tensor_tensor(vz[:], vz[:], sq[:], ALU.mult).then_inc(silu_done, 1)

            def score(pair, j, kind):
                h, i = j // NT, j % NT
                n = (i + 1) * P
                it = ITEMS * pair + j
                bias = logit_bias[:, 0, (NT - 1 - i) * P:SEQ] if kind == 0 else logit_bias[:, h, 0:n]
                dve.wait_ge(t_done, it)
                if kind == 1 and i == 0:
                    dve.wait_ge(bias_in[h], 16 * (pair - A_PAIRS + 1))
                dve.wait_ge(s_done, it + 1)
                dve.reg_add(items_scored, items_scored, 1)
                dve.tensor_tensor_reduce(out=prob[:, 0:n], in0=scores[:, 0:n], in1=bias, scale=1.0, scalar=3e38,
                                             op0=ALU.add, op1=ALU.min, accum_out=neg_max[:, j:j + 1]).then_inc(masked, 1)
                dve.wait_ge(exp_done, items_scored)
                dve.reciprocal(inv_denom[:, j:j + 1], denom[:, j:j + 1]).then_inc(recip_done, 1)
                dve.wait_ge(recip_done, it + 1)
                dve.tensor_scalar(prob[:, 0:n], prob[:, 0:n], inv_denom[:, j:j + 1], None, ALU.mult).then_inc(prob_done, 1)

            def turn(pair, j):
                n = (j % NT + 1) * P
                dve.wait_ge(pth_done, ITEMS * pair + j + 1)
                dve.tensor_tensor(pt_lo[:, 0:n], turned[:, 0:n], pt_hi[:, 0:n].bitcast(F32), ALU.subtract).then_inc(ptl_done, 1)

            def product(pair, j):
                if j % 4 == 3:
                    h, u = j // NT, j // 4
                    own, cols = slice(h * HEAD, (h + 1) * HEAD), slice((u % 2) * HALF, (u % 2 + 1) * HALF)
                    dve.wait_ge(mixed_saved, 16 * pair)
                    dve.wait_ge(o_moved, 4 * pair + u + 1)
                    dve.tensor_tensor(o_pair[own, cols], pv[0:HEAD, :], o_low[:], ALU.add).then_inc(o_summed, 1)
                    dve.wait_ge(silu_done, pair + 1)
                    dve.wait_ge(o_summed, 4 * pair + u + 1)
                    dve.tensor_tensor(o_pair[own, cols], o_pair[own, cols], vz[own, cols], ALU.mult).then_inc(o_done, 1)

            def steps_at(pair, kind, slot):
                for name, j in steps_of(slot):
                    if name == "norm":
                        norm(pair, kind)
                    elif name == "stack":
                        stack(pair)
                    elif name == "values":
                        values(pair)
                    elif name == "gate":
                        gate(pair)
                    elif name == "score":
                        score(pair, j, kind)
                    elif name == "turn":
                        turn(pair, j)
                    elif name == "product":
                        product(pair, j)

            def pair_body(pair, kind, s0, projecting=True):
                for g in range(PAIR_GROUPS):
                    def steps(slot, g=g):
                        steps_at(pair, kind, 8 * g + slot)
                    if projecting:
                        group(s0 + g, steps)
                    else:
                        for slot in range(8):
                            steps(slot)
                            if 0 <= 8 * g + slot - MIX_SLOT < KT - 1:
                                mix_lo_part(8 * g + slot - MIX_SLOT)
                steps_at(pair, kind, SLOTS)

            def mix_lo_part(kk):
                dve.wait_ge(mix_hi, kk + 1)
                dve.tensor_tensor(act_lo[:, OUT_ORDER[kk], :], raw[:, kk % 2, :],
                                      act_hi[:, OUT_ORDER[kk], :].bitcast(F32), ALU.subtract).then_inc(mix_lo, 1)

            pair_body(0, 0, S_LOOP_A)
            with dve.Fori(1, A_PAIRS - 1) as p:
                pair_body(p, 0, S_LOOP_A + 4 * p)
            pair_body(A_PAIRS - 1, 0, S_B0)
            with dve.Fori(0, B_PAIRS - 1) as p:
                pair_body(A_PAIRS + p, 1, S_LOOP_B + 4 * p)
            pair_body(A_PAIRS + B_PAIRS - 1, 1, None, projecting=False)

            mix_lo_part(KT - 1)

            def add_residual(cg):
                for t in range(NT):
                    dve.wait_ge(res_in[t], 16 * (cg + 1))
                    dve.wait_ge(out_ready, NT * cg + t + 1)
                    dve.tensor_tensor(res[:, t, :], banks[t], res[:, t, :], ALU.add).then_inc(out_summed, 1)

            for kk in range(KT - 1):
                split_lo(GROUPS, kk + 1)
            split_lo(GROUPS, KT)
            add_residual(0)
            with dve.Fori(1, OUT_CG - 1) as cg:
                for kk in range(KT):
                    split_lo(GROUPS + 4 * cg, kk + 1)
                add_residual(cg)
            for kk in range(KT - 1):
                split_lo(GROUPS + 4 * (OUT_CG - 1), kk + 1)
            add_residual(OUT_CG - 1)

        @block.tensor
        def _(pe):
            def half_quarter(s, kq, th):
                if th == 0:
                    pe.wait_ge(lo_done, 4 * s + kq + 1)
                if kq == 0 and not (isinstance(s, int) and s == 0):
                    pe.wait_ge(evac_done, 2 * s + th - 1)
                at = slice(th * HALF, (th + 1) * HALF)
                for k in range(4):
                    hi, lo = (w[:, kq % 2, k * P:(k + 1) * P] for w in (w_hi, w_lo))
                    xh, xl = (a[:, 4 * kq + k, at] for a in (act_hi, act_lo))
                    first, end = kq == 0 and k == 0, kq == 3 and k == 3
                    pe.matmul(bank[th][:], hi, xh, start=first, stop=False)
                    pe.matmul(bank[th][:], hi, xl, start=False, stop=False)
                    mm = pe.matmul(bank[th][:], lo, xh, start=False, stop=end)
                if kq == 3:
                    mm.then_inc(half_done, 1)
                elif th == 1:
                    mm.then_inc(quarter_done, 1)
                return mm

            def group(s, steps):
                for slot in range(8):
                    steps(slot)
                    kq, th = slot // 2, slot % 2
                    half_quarter(s, kq, th)

            for t in range(NT):
                pe.wait_ge(consts, 8)
                pe.wait_ge(x_normed, t + 1)
                for b in range(4):
                    if t >= 2:
                        pe.wait_ge(x_lo_done, 4 * (t - 2) + b + 1)
                    for k in range(4):
                        f = 4 * b + k
                        mm = pe.transpose(banks[4 * (t % 2) + b][:, k * P:(k + 1) * P],
                                          x_tile[:, t % 2, f * P:(f + 1) * P], ident[:])
                    mm.then_inc(x_turned, 1)
            pe.wait_ge(x_lo_done, 4 * NT)
            pe.wait_ge(ws_lo_done, 1)
            for th in range(2):
                at = slice(th * HALF, (th + 1) * HALF)
                for k in range(KT):
                    pe.matmul(scores[0:SMALL, at], ws_hi[:, k, :], act_hi[:, k, at], start=(k == 0), stop=False)
                    pe.matmul(scores[0:SMALL, at], ws_hi[:, k, :], act_lo[:, k, at], start=False, stop=False)
                    mm = pe.matmul(scores[0:SMALL, at], ws_lo[:, k, :], act_hi[:, k, at], start=False, stop=(k == KT - 1))
            mm.then_inc(small_done, 1)
            group(0, lambda slot: None)
            with pe.Fori(1, C_GROUPS) as s:
                group(s, lambda slot: None)

            pe.wait_ge(rounded_consts, 2)

            def gla_steps(c, slot):
                if slot == 0:
                    pe.wait_ge(gla_up_in, 16 * (c + 1))
                    pe.wait_ge(gla_rank_in, 16 * (c + 1))
                    pe.wait_ge(small_out, 1)
                    pe.wait_ge(gla_out, 2 * c)
                    for th in range(2):
                        at = slice(th * HALF, (th + 1) * HALF)
                        mm = pe.matmul(scores[0:C_DK, at], gate_up[:], rank_rows[:, at], start=True, stop=True)
                    mm.then_inc(gla_gate, 1)
                    pe.wait_ge(gla_k_in, 16 * (c + 1))
                    pe.wait_ge(gla_scaled, c + 1)
                    for t in range(NT):
                        at = slice(t * P, (t + 1) * P)
                        mm = pe.matmul(turned[:, at], g_k[:, at], g_q[:, at], start=True, stop=True)
                    mm.then_inc(gla_diag, 1)
                if 2 <= slot <= 4:
                    for l in LEVELS_AT[slot - 1]:
                        n = LEVELS * c + l
                        pe.wait_ge(gla_put, 8 * c + l if l >= 2 else 8 * c)
                        pe.wait_ge(gla_kcopy, 2 * c)
                        pe.wait_ge(gla_ql, n + 1)
                        pe.wait_ge(gla_kl, n + 1)
                        for t in range(NT):
                            mm = pe.matmul(banks[6 + l % 2][:, t * HEAD:(t + 1) * HEAD],
                                           k_level[:, l % 2, t * P:(t + 1) * P],
                                           q_level[:, l % 2, t * HEAD:(t + 1) * HEAD], start=True, stop=True)
                        mm.then_inc(gla_lv, 1)
                if slot == 4:
                    pe.wait_ge(gla_v_in, 16 * (c + 1))
                    pe.wait_ge(gla_sum, c + 1)
                    pe.wait_ge(gla_put, 8 * c + 1)
                    for i in range(4):
                        for t in (2 * i, 2 * i + 1):
                            for h in range(2):
                                o = (t % 2) * C_DV + h * C_DK
                                mm = pe.transpose(banks[2 + i][:, o:o + C_DK], g_v[:, h, t * P:(t + 1) * P],
                                                  ident[0:C_DK, 0:C_DK])
                        mm.then_inc(gla_vt, 1)
                if slot == 5:
                    pe.wait_ge(gla_put, 8 * (c + 1))
                    pe.wait_ge(gla_ke, c + 1)
                    for i in range(2):
                        for t in range(4 * i, 4 * i + 4):
                            mm = pe.transpose(banks[6 + i][:, (t % 4) * C_DK:(t % 4 + 1) * C_DK],
                                              k_carry[:, t * P:(t + 1) * P], ident[0:C_DK, 0:C_DK])
                        mm.then_inc(gla_kt, 1)
                if slot == 6:
                    pe.wait_ge(gla_vcopy, 4 * (c + 1))
                    pe.wait_ge(gla_kcopy, 2 * (c + 1))
                    for t in range(NT - 1):
                        mm = pe.matmul(banks[2 + t // 2][0:C_DK, (t % 2) * C_DV:(t % 2 + 1) * C_DV], k_rows[:, t, :],
                                       v_rows[:, t, :], start=True, stop=True)
                    mm.then_inc(gla_ds, 1)
                if slot == 7:
                    pe.wait_ge(gla_state, (NT - 1) * (c + 1))
                    pe.wait_ge(gla_qe, c + 1)
                    for t in range(NT):
                        o, at = banks[2 + t // 2][:, (t % 2) * C_DV:(t % 2 + 1) * C_DV], slice(t * P, (t + 1) * P)
                        mm = pe.matmul(o, weights_t[:, at], v_rows[:, t, :], start=True, stop=(t == 0))
                        if t > 0:
                            mm = pe.matmul(o, q_carry[:, at], state[:, t, :], start=False, stop=True)
                        if t % 2 == 1:
                            mm.then_inc(gla_o, 1)
                if slot == 8:
                    pe.wait_ge(gla_ocopy, 4 * (c + 1))
                    pe.wait_ge(gla_norm, c + 1)
                    for h in range(2):
                        for t in range(NT):
                            mm = pe.transpose((scores, turned)[h][0:C_DK, t * P:(t + 1) * P],
                                              o_rows[:, t, h * C_DK:(h + 1) * C_DK], ident[:])
                        mm.then_inc(gla_ot, 1)

            group(S_A0, lambda slot: gla_steps(0, slot))
            gla_steps(0, 8)
            with pe.Fori(1, C_HEADS) as c:
                group(S_A0 + c, lambda slot: gla_steps(c, slot))
                gla_steps(c, 8)

            def norm(pair):
                for i, ps in enumerate((scores, turned)):
                    pe.wait_ge(masked, ITEMS * pair)
                    pe.wait_ge(ptl_done, ITEMS * pair)
                    pe.wait_ge(sq_done, 2 * pair + i + 1)
                    for th in range(2):
                        at = slice(th * HALF, (th + 1) * HALF)
                        mm = pe.matmul(ps[:, at], half_ones[:], sq[:, at], start=True, stop=True)
                    mm.then_inc(ssq_done, 1)

            def values(pair):
                pe.wait_ge(root_done, 4 * (pair + 1))
                pe.wait_ge(v_in, 16 * (pair + 1))
                for b in range(2):
                    for t in range(4 * b, 4 * b + 4):
                        at = slice(t * P, (t + 1) * P)
                        mm = pe.transpose(turned[:, at], vz[:, at], ident[:])
                    mm.then_inc(v_turned, 1)

            def score(pair, j, kind):
                h, i = j // NT, j % NT
                n = (i + 1) * P
                if i == 0:
                    pe.wait_ge(ql_done, 2 * pair + h + 1)
                    pe.wait_ge(kl_done, 4 * pair + 2 * h + 2)
                    pe.wait_ge(kh_done, 4 * pair + 2 * h + 2)
                pe.wait_ge(masked, ITEMS * pair + j)
                q = q_st[:, h, i * P:(i + 1) * P]
                for c0 in range(0, n, HALF):
                    c1 = min(c0 + HALF, n)
                    pe.matmul(scores[:, c0:c1], q, k_hi[:, h, c0:c1], start=True, stop=False)
                    if kind == 1 and c1 == n:
                        pe.matmul(scores[:, i * P:n], ident_r[:], causal_r[:], start=False, stop=False)
                    mm = pe.matmul(scores[:, c0:c1], q, k_lo[:, h, c0:c1], start=False, stop=True)
                mm.then_inc(s_done, 1)

            def turn(pair, j):
                it = ITEMS * pair + j
                pe.wait_ge(vl_done, 4 * (pair + 1))
                pe.wait_ge(ptl_done, it)
                pe.wait_ge(prob_done, it + 1)
                for t in range(j % NT + 1):
                    at = slice(t * P, (t + 1) * P)
                    mm = pe.transpose(turned[:, at], prob[:, at], ident[:])
                mm.then_inc(t_done, 1)

            def product(pair, j):
                h, i = j // NT, j % NT
                if j % 4 == 0:
                    pe.wait_ge(o_summed, 4 * pair + j // 4)
                pe.wait_ge(ptl_done, ITEMS * pair + j + 1)
                o = pv[:, (j % 4) * P:(j % 4 + 1) * P]
                for t in range(i + 1):
                    at = slice(t * P, (t + 1) * P)
                    pe.matmul(o, v_st[:, h, t, :], pt_hi[:, at], start=(t == 0), stop=False)
                    mm = pe.matmul(o, v_st[:, h, t, :], pt_lo[:, at], start=False, stop=(t == i))
                mm.then_inc(pv_done, 1)

            def steps_at(pair, kind, slot):
                for name, j in steps_of(slot):
                    if name == "norm":
                        norm(pair)
                    elif name == "values":
                        values(pair)
                    elif name == "score":
                        score(pair, j, kind)
                    elif name == "turn":
                        turn(pair, j)
                    elif name == "product":
                        product(pair, j)

            def pair_body(pair, kind, s0):
                for slot in range(SLOTS + 1):
                    steps_at(pair, kind, slot)
                    if slot < SLOTS and s0 is not None:
                        half_quarter(s0 + slot // 8, slot % 8 // 2, slot % 2)

            pair_body(0, 0, S_LOOP_A)
            with pe.Fori(1, A_PAIRS - 1) as p:
                pair_body(p, 0, S_LOOP_A + 4 * p)
            pair_body(A_PAIRS - 1, 0, S_B0)
            with pe.Fori(0, B_PAIRS - 1) as p:
                pair_body(A_PAIRS + p, 1, S_LOOP_B + 4 * p)
            pair_body(A_PAIRS + B_PAIRS - 1, 1, None)

            def out_quarter(cg, kk):
                k = OUT_ORDER[kk]
                pe.wait_ge(lo_done, Q_OUT + 16 * cg + kk + 1)
                if isinstance(cg, int) and cg == 0:
                    pe.wait_ge(mix_lo, kk + 1)
                for t in range(NT):
                    if kk == 0 and not (isinstance(cg, int) and cg == 0):
                        pe.wait_ge(out_summed, NT * (cg - 1) + t + 1)
                    hi, lo = (a[:, k, t * P:(t + 1) * P] for a in (act_hi, act_lo))
                    pe.matmul(banks[t], hi, w_hi[:, kk % 2, :], start=(kk == 0), stop=False)
                    pe.matmul(banks[t], hi, w_lo[:, kk % 2, :], start=False, stop=False)
                    mm = pe.matmul(banks[t], lo, w_hi[:, kk % 2, :], start=False, stop=(kk == KT - 1))
                    if kk == KT - 1:
                        mm.then_inc(out_ready, 1)
                if kk < KT - 1:
                    mm.then_inc(quarter_done, 1)

            pe.wait_ge(o_summed, 4 * (A_PAIRS + B_PAIRS))
            pe.wait_ge(evac_done, 2 * GROUPS)
            for kk in range(KT):
                out_quarter(0, kk)
            with pe.Fori(1, OUT_CG) as cg:
                for kk in range(KT):
                    out_quarter(cg, kk)


_INS = ["x", "norm_g", "w_in", "a_q_gain", "a_k_gain", "b_q_gain", "b_k_gain", "fox_bias", "gla_gate_up",
        "gla_gate_bias", "gla_out_gain", "w_out"]


def kernel(**inputs):
    import numpy as _np
    import concourse.bacc as _bacc
    from concourse import mybir as _mybir
    from concourse.bass_utils import run_bass_kernel_spmd as _run

    nc = _bacc.Bacc("TRN2", target_bir_lowering=False, num_devices=1, dynamic_dma_scratch_size=1024)
    arrays, args = {}, []
    for name in _INS:
        a = _np.ascontiguousarray(inputs[name])
        arrays[f"in_{name}_dram"] = a
        args.append(nc.dram_tensor(f"in_{name}_dram", a.shape, _mybir.dt.from_np(a.dtype), kind="ExternalInput").ap())
    args.append(nc.dram_tensor("out_0_dram", (1, SEQ, D_MODEL), _mybir.dt.float32, kind="ExternalOutput").ap())
    build(nc, *args)
    r = _run(nc, [arrays], core_ids=[0])
    return r.results[0]["out_0_dram"]
```

```python
import concourse.bass as bass
from concourse import mybir
from contextlib import ExitStack

P = 128
SEQ = 1024
D_MODEL = 2048
KT = D_MODEL // P
NT = SEQ // P
HALF = 512
HEAD = 64
A_WIDTH = 768
B_WIDTH = 512
B_HEADS = B_WIDTH // HEAD
C_HEADS = 4
C_DV = 192
C_DK = 96
C_K = C_HEADS * C_DK
C_V = C_HEADS * C_DV
RANK = 16
A_PAIRS = A_WIDTH // P
B_PAIRS = B_WIDTH // P
COL_B = 4 * A_WIDTH
COL_BF = COL_B + 4 * B_WIDTH
COL_CQ = COL_BF + B_HEADS
COL_CK = COL_CQ + C_K
COL_CV = COL_CK + C_K
COL_CZ = COL_CV + C_V
COL_CR = COL_CZ + C_V
IN_WIDTH = COL_CR + RANK
SMALL = B_HEADS + RANK
C_FIRST = 2 * C_K // P + 2
C_ALONE = C_FIRST + 2
HEAD_GROUPS = 3
PAIR_GROUPS = 4
ITEMS = 2 * NT
LEVELS = 7
S_LOOP_A = C_ALONE + HEAD_GROUPS * C_HEADS
S_PAIRS = S_LOOP_A - PAIR_GROUPS
S_B0 = S_LOOP_A + PAIR_GROUPS * (A_PAIRS - 1)
S_LOOP_B = S_B0 + PAIR_GROUPS
GROUPS = S_LOOP_B + PAIR_GROUPS * (B_PAIRS - 1)
Q_OUT = 4 * GROUPS
OUT_CG = D_MODEL // HALF
EPS = 1e-6
FAR = 1e30
LOWEST = -80.0
LN_EXP_SET = 6
LN2, LN3 = 0.6931471805599453, 1.0986122886681098

F32 = mybir.dt.float32
F32R = mybir.dt.float32r
I32 = mybir.dt.int32
ALU = mybir.AluOpType
ACT = mybir.ActivationFunctionType
AX_X = mybir.AxisListType.X

SLOTS = 8 * PAIR_GROUPS
G_GATE, G_TURN_V, G_CARRY, G_TURN_K, G_STATE, G_Z, G_OUT, G_NORM, G_FINAL = 2, 12, 14, 16, 17, 18, 19, 20, 22
G_LEVEL = [6 + l for l in range(LEVELS)]
SLOT_SCORE = [1 + (j * 28) // (ITEMS - 1) for j in range(ITEMS)]
SLOT_SCALE = [s + 1 for s in SLOT_SCORE]
SLOT_TURN = [s + 2 for s in SLOT_SCORE]
SLOT_PRODUCT = [s + 3 for s in SLOT_SCORE]
SLOT_VALUES, SLOT_STACK1, SLOT_BOUND, SLOT_GATE, SLOT_SILU = (0, 1), 2, 4, 5, 7
SLOT_SQUARE = (14, 16, 20, 22)
SLOT_ROOT = (18, 24)
SLOT_STACK0 = 26
MIX_SLOT = 4
OUT_ORDER = [k for k in range(KT) if k != A_PAIRS + B_PAIRS - 1] + [A_PAIRS + B_PAIRS - 1]


def steps_of(slot):
    out = [("values", b) for b in range(2) if SLOT_VALUES[b] == slot]
    out += [("product", j) for j in range(ITEMS) if SLOT_PRODUCT[j] == slot]
    out += [("turn", j) for j in range(ITEMS) if SLOT_TURN[j] == slot]
    out += [("scale", j) for j in range(ITEMS) if SLOT_SCALE[j] == slot]
    out += [("score", j) for j in range(ITEMS) if SLOT_SCORE[j] == slot]
    out += [("stack1", 0)] * (slot == SLOT_STACK1) + [("bound", 0)] * (slot == SLOT_BOUND)
    out += [("gate", 0)] * (slot == SLOT_GATE) + [("silu", 0)] * (slot == SLOT_SILU)
    out += [("sum", m) for m in range(4) if SLOT_SQUARE[m] + 1 == slot]
    out += [("root", i) for i in range(2) if SLOT_ROOT[i] == slot]
    out += [("square", m) for m in range(4) if SLOT_SQUARE[m] == slot]
    out += [("stack0", 0)] * (slot == SLOT_STACK0)
    return out


def first_pair(pair):
    return isinstance(pair, int) and pair == 0


def blocks(ap, b):
    return ap.rearrange("p (n u r) -> p n u r", u=2, r=b)


def build(nc, x, norm_g, w_in, a_q_gain, a_k_gain, b_q_gain, b_k_gain, fox_bias,
          gla_gate_up, gla_gate_bias, gla_out_gain, w_out, out):
    x_rows, out_rows = x[0], out[0]
    w_in, w_out = w_in[0], w_out[0]
    w_in_k = w_in.rearrange("(k p) c -> p k c", p=P)
    w_out_k = w_out.rearrange("(k p) c -> p k c", p=P)
    proj = nc.dram_tensor("proj_scratch", (IN_WIDTH, SEQ), F32, kind="Internal").ap()
    mixed = nc.dram_tensor("mixed_scratch", (D_MODEL, SEQ), F32, kind="Internal").ap()
    decay = nc.dram_tensor("decay_scratch", (B_HEADS, SEQ), F32, kind="Internal").ap()

    with ExitStack() as ctx:
        def sb(name, shape, dt=F32, scope=ctx):
            return scope.enter_context(nc.sbuf_tensor(name, shape, dt))

        def sem(name):
            return ctx.enter_context(nc.semaphore(name))

        bank = [ctx.enter_context(nc.psum_tensor(f"acc{i}", [P, HALF], F32)) for i in range(2)]
        scores = ctx.enter_context(nc.psum_tensor("scores", [P, SEQ], F32))
        turned = ctx.enter_context(nc.psum_tensor("turned", [P, SEQ], F32))
        pv = ctx.enter_context(nc.psum_tensor("pv", [P, HALF], F32))
        spare = ctx.enter_context(nc.psum_tensor("spare", [P, HALF], F32))
        banks = [bank[0][:], bank[1][:], scores[:, 0:HALF], scores[:, HALF:], turned[:, 0:HALF], turned[:, HALF:],
                 pv[:], spare[:]]

        act_hi = sb("act_hi", [P, KT, SEQ], F32R)
        act_lo = sb("act_lo", [P, KT, SEQ], F32R)
        w_raw = sb("w_raw", [P, 2, HALF])
        w_hi = sb("w_hi", [P, 2, HALF], F32R)
        w_lo = sb("w_lo", [P, 2, HALF], F32R)
        stage = sb("stage", [P, 2, HALF])
        ident = sb("ident", [P, P])
        ident_r = sb("ident_r", [P, P], F32R)
        half_ones_r = sb("half_ones_r", [P, P], F32R)
        causal_r = sb("causal_r", [P, P], F32R)
        logit_bias = sb("logit_bias", [P, 2, SEQ])
        eps_col = sb("eps_col", [P, 1])
        gains = sb("gains", [P, 4])
        out_gain = sb("out_gain", [C_DK, 2])
        fox_col = sb("fox_col", [B_HEADS, 1])
        neg_max = sb("neg_max", [P, ITEMS])
        denom = sb("denom", [P, ITEMS])
        inv_denom = sb("inv_denom", [P, ITEMS])

        first = ExitStack()
        x_tile = sb("x_tile", [P, 2, D_MODEL], scope=first)
        g_wide = sb("g_wide", [P, D_MODEL], scope=first)
        junk = sb("junk", [P, D_MODEL], scope=first)
        x_ssq = sb("x_ssq", [P, NT], scope=first)
        x_log = sb("x_log", [P, NT], scope=first)
        x_rstd = sb("x_rstd", [P, NT], scope=first)
        dist_i = sb("dist_i", [P, SEQ], I32, scope=first)
        mod_i = sb("mod_i", [P, SEQ], I32, scope=first)
        dist = sb("dist", [P, SEQ], scope=first)
        count = sb("count", [P, SEQ], scope=first)
        term = sb("term", [P, SEQ], scope=first)
        causal = sb("causal", [P, P], scope=first)
        half_ones = sb("half_ones", [P, P], scope=first)
        ws_raw = sb("ws_raw", [P, KT, SMALL], scope=first)
        ws_hi = sb("ws_hi", [P, KT, SMALL], F32R, scope=first)
        ws_lo = sb("ws_lo", [P, KT, SMALL], F32R, scope=first)
        small = sb("small", [SMALL, SEQ], scope=first)
        lf_abs, lf_min = junk[0:B_HEADS, 0:SEQ], junk[0:B_HEADS, SEQ:]
        c_sum = sb("c_sum", [B_HEADS, SEQ], scope=first)
        first.close()

        gla = ExitStack()
        level_mask = sb("level_mask", [P, LEVELS, HEAD], scope=gla)
        gate_up = sb("gate_up", [RANK, C_DK], scope=gla)
        gate_bias = sb("gate_bias", [C_DK, 1], scope=gla)
        g_qk = sb("g_qk", [P, 2, SEQ], scope=gla)
        g_v = sb("g_v", [C_DK, 2, SEQ], scope=gla)
        g_z = sb("g_z", [C_DK, 2, SEQ], scope=gla)
        g_b = sb("g_b", [C_DK, SEQ], scope=gla)
        g_t = sb("g_t", [C_DK, 2, SEQ], scope=gla)
        q_level = sb("q_level", [C_DK, 2, HALF], scope=gla)
        k_level = sb("k_level", [C_DK, 2, SEQ], scope=gla)
        v_rows = sb("v_rows", [P, NT, C_DV], scope=gla)
        k_rows = sb("k_rows", [P, NT, C_DK], scope=gla)
        state = sb("state", [C_DK, NT, C_DV], scope=gla)
        o_ssq = sb("o_ssq", [P, NT], scope=gla)
        o_rstd = sb("o_rstd", [P, NT], scope=gla)
        o_junk = sb("o_junk", [P, 2, C_DV], scope=gla)
        gla.close()
        weights_t = logit_bias[:, 0, :]
        rank_rows = v_rows[:, :, :].rearrange("p t v -> p (t v)")[0:RANK, 0:SEQ]
        g_q, g_k = g_qk[0:C_DK, 0, :], g_qk[0:C_DK, 1, :]
        o_rows = g_qk[:, :, :].rearrange("p a b -> p (a b)")[:, 0:NT * C_DV].rearrange("p (t v) -> p t v", v=C_DV)
        q_carry, k_carry = g_v[:, 0, :], g_v[:, 1, :]

        pairs = ExitStack()
        raw = sb("raw", [P, 2, SEQ], scope=pairs)
        sq = sb("sq", [P, 2, HALF], scope=pairs)
        sq_hi = sb("sq_hi", [P, HALF], F32R, scope=pairs)
        sq_lo = sb("sq_lo", [P, HALF], F32R, scope=pairs)
        vz = sb("vz", [P, SEQ], scope=pairs)
        q_st = sb("q_st", [P, 2, SEQ], F32R, scope=pairs)
        k_hi = sb("k_hi", [P, 2, SEQ], F32R, scope=pairs)
        k_lo = sb("k_lo", [P, SEQ], F32R, scope=pairs)
        v_st = sb("v_st", [P, 2, NT, P], F32R, scope=pairs)
        prob = sb("prob", [P, 2, SEQ], scope=pairs)
        pt_hi = sb("pt_hi", [P, SEQ], F32R, scope=pairs)
        pt_lo = sb("pt_lo", [P, SEQ], F32R, scope=pairs)
        o_part = sb("o_part", [P, HALF], scope=pairs)
        pairs.close()
        sq_wide = sq[:, :, :].rearrange("p a b -> p (a b)")

        last = ExitStack()
        _held = sb("held", [P, 2, SEQ], scope=last)
        res = sb("res", [P, NT, HALF], scope=last)
        last.close()

        consts, levels_ready, eps_ready, gains_in, small_in, g_in, rounded_consts = (
            sem(n) for n in "consts levels_ready eps_ready gains_in small_in g_in rounded_consts".split())
        x_squared, x_logged, x_rooted, x_normed, x_turned, x_hi_done, x_lo_done = (
            sem(n) for n in "x_squared x_logged x_rooted x_normed x_turned x_hi_done x_lo_done".split())
        dist_chain, ws_hi_done, ws_lo_done, small_done, small_out, small_saved, lf_step, c_done = (
            sem(n) for n in "dist_chain ws_hi_done ws_lo_done small_done small_out small_saved lf_step c_done".split())
        c_saved = sem("c_saved")
        hi_done, lo_done, quarter_done, half_done, evac_done = (
            sem(n) for n in "hi_done lo_done quarter_done half_done evac_done".split())
        q_in, k_in, v_in, z_in, sq_done, sq_lo_done, ssq_done = (
            sem(n) for n in "q_in k_in v_in z_in sq_done sq_lo_done ssq_done ".split())
        normed, qh_done, ql_done, kh_done, k_other_done, kl_done, v_turned, vh_done = (
            sem(n) for n in "normed qh_done ql_done kh_done k_other_done kl_done v_turned vh_done".split())
        vl_done, z_bounded, gate_chain, sigmoid_done, silu_done, ssq_logged, root_done = (
            sem(n) for n in "vl_done z_bounded gate_chain sigmoid_done silu_done ssq_logged root_done".split())
        s_done, masked, exp_done, recip_done, prob_done, t_done, pth_done, ptl_done = (
            sem(n) for n in "s_done masked exp_done recip_done prob_done t_done pth_done ptl_done".split())
        pv_done, o_moved, o_summed, o_done, mixed_saved = (
            sem(n) for n in "pv_done o_moved o_summed o_done mixed_saved".split())
        gla_rank_in, gla_up_in, gla_bias_in, gla_q_in, gla_k_in, gla_v_in, gla_z_in, gla_saved = (
            sem(n) for n in "gla_rank_in gla_up_in gla_bias_in gla_q_in gla_k_in gla_v_in gla_z_in gla_saved".split())
        gla_gate, gla_sum, gla_abs, gla_exp, gla_log, gla_min, gla_a, gla_scan = (
            sem(n) for n in "gla_gate gla_sum gla_abs gla_exp gla_log gla_min gla_a gla_scan".split())
        gla_scaled = sem("gla_scaled")
        gla_diag, gla_zero, gla_diff, gla_decay, gla_ql, gla_kl, gla_lv, gla_put = (
            sem(n) for n in "gla_diag gla_zero gla_diff gla_decay gla_ql gla_kl gla_lv gla_put".split())
        gla_vt, gla_vcopy, gla_eb, gla_qe, gla_ldiff, gla_le, gla_ke, gla_kt = (
            sem(n) for n in "gla_vt gla_vcopy gla_eb gla_qe gla_ldiff gla_le gla_ke gla_kt".split())
        gla_kcopy, gla_ds, gla_state = (
            sem(n) for n in "gla_kcopy gla_ds gla_state".split())
        gla_o, gla_ocopy, gla_osq, gla_ln, gla_rstd, gla_norm, gla_ot, gla_ez = (
            sem(n) for n in "gla_o gla_ocopy gla_osq gla_ln gla_rstd gla_norm gla_ot gla_ez".split())
        gla_zb, gla_sigmoid, gla_silu, gla_out = (
            sem(n) for n in "gla_zb gla_sigmoid gla_silu gla_out".split())
        mix_hi, mix_lo, out_ready, out_summed = (
            sem(n) for n in "mix_hi mix_lo out_ready out_summed".split())
        bias_in = [sem("bias_landed0"), sem("bias_landed1")]
        w_in_sem = [sem("w_landed0"), sem("w_landed1")]
        x_in = [sem("x_landed0"), sem("x_landed1")]
        proj_saved = [sem("proj_saved0"), sem("proj_saved1")]
        mix_in = [sem("mix_landed0"), sem("mix_landed1")]
        res_in = [sem(f"res_landed{t}") for t in range(NT)]
        out_saved = [sem(f"out_saved{t}") for t in range(NT)]

        block = ctx.enter_context(nc.Block())

        @block.sync
        def _(sp):
            def load_quarter(s, kq, col):
                if not (isinstance(s, int) and s == 0 and kq < 2):
                    sp.wait_ge(lo_done, 4 * s + kq - 1)
                sp.dma_start(w_raw[:, kq % 2, :].rearrange("p (k c) -> p k c", k=4),
                             w_in_k[:, 4 * kq:4 * kq + 4, bass.ds(col, P)]).then_inc(w_in_sem[kq % 2], 16)

            def load_rows(dst, row, n, name):
                sp.dma_start(dst, proj[bass.ds(row, n), :]).then_inc(name, 16)

            def saved(s):
                for th in range(2):
                    sp.wait_ge(proj_saved[th], 16 * (s + 1))

            sp.dma_start(g_wide[:], norm_g[0:1, :].broadcast_to([P, D_MODEL])).then_inc(g_in, 16)
            for t in range(2):
                sp.dma_start(x_tile[:, t, :], x_rows[t * P:(t + 1) * P, :]).then_inc(x_in[t], 16)
            for n, g in enumerate((a_q_gain, a_k_gain, b_q_gain, b_k_gain)):
                for h in range(2):
                    sp.dma_start(gains[h * HEAD:(h + 1) * HEAD, n:n + 1], g.rearrange("a d -> d a")).then_inc(gains_in, 16)
            for h in range(2):
                sp.dma_start(out_gain[:, h:h + 1], gla_out_gain[0:1, h * C_DK:(h + 1) * C_DK].rearrange("a d -> d a")).then_inc(gains_in, 16)
            sp.dma_start(fox_col[:], fox_bias.rearrange("a d -> d a")).then_inc(gains_in, 16)
            sp.dma_start(ws_raw[:, :, 0:B_HEADS], w_in_k[:, :, COL_BF:COL_BF + B_HEADS]).then_inc(small_in, 16)
            sp.dma_start(ws_raw[:, :, B_HEADS:SMALL], w_in_k[:, :, COL_CR:COL_CR + RANK]).then_inc(small_in, 16)
            load_quarter(0, 0, COL_CQ)
            load_quarter(0, 1, COL_CQ)
            for t in range(2, NT):
                sp.wait_ge(x_turned, 4 * (t - 1))
                sp.dma_start(x_tile[:, t % 2, :], x_rows[t * P:(t + 1) * P, :]).then_inc(x_in[t % 2], 16)
            sp.wait_ge(small_out, 1)
            sp.dma_start(proj[COL_CR:COL_CR + RANK, :], small[B_HEADS:SMALL, :]).then_inc(small_saved, 16)
            load_quarter(0, 2, COL_CQ)
            load_quarter(0, 3, COL_CQ)
            with sp.Fori(1, C_FIRST) as s:
                for kq in range(4):
                    load_quarter(s, kq, COL_CQ + s * P)
            for g in range(C_ALONE - C_FIRST):
                for kq in range(4):
                    load_quarter(C_FIRST + g, kq, COL_CZ + g * P)

            def store_head(c):
                sp.wait_ge(gla_out, 2 * (c + 1))
                sp.dma_start(mixed[bass.ds(A_WIDTH + B_WIDTH + c * C_DV, C_DV), :].rearrange("(h p) t -> p h t", p=C_DK),
                             g_z[:, :, :]).then_inc(gla_saved, 16)

            def gla_loads(c):
                s = C_ALONE + HEAD_GROUPS * c
                for kq in range(2):
                    load_quarter(s, kq, COL_CV + (2 + c) * P)
                if isinstance(c, int):
                    sp.wait_ge(c_done, 1)
                    sp.wait_ge(small_saved, 16)
                    sp.wait_ge(c_saved, 16)
                    saved(C_ALONE - 1)
                else:
                    store_head(c - 1)
                    sp.wait_ge(gla_saved, 16 * c)
                load_rows(rank_rows, COL_CR, RANK, gla_rank_in)
                sp.dma_start(gate_up[:], gla_gate_up[0][:, bass.ds(c * C_DK, C_DK)]).then_inc(gla_up_in, 16)
                sp.dma_start(gate_bias[:], gla_gate_bias[0:1, bass.ds(c * C_DK, C_DK)].rearrange("a d -> d a"))\
                    .then_inc(gla_bias_in, 16)
                load_rows(g_q, COL_CQ + c * C_DK, C_DK, gla_q_in)
                load_rows(g_k, COL_CK + c * C_DK, C_DK, gla_k_in)
                for kq in range(2, 4):
                    load_quarter(s, kq, COL_CV + (2 + c) * P)
                for kq in range(3):
                    load_quarter(s + 1, kq, COL_CZ + (2 + c) * P)
                saved(s)
                sp.dma_start(g_v[:, :, :], proj[bass.ds(COL_CV + c * C_DV, C_DV), :].rearrange("(h p) t -> p h t", p=C_DK))\
                    .then_inc(gla_v_in, 16)
                load_quarter(s + 1, 3, COL_CZ + (2 + c) * P)
                for kq in range(3):
                    load_quarter(s + 2, kq, c * A_WIDTH)
                saved(s + 1)
                sp.dma_start(g_z[:, :, :], proj[bass.ds(COL_CZ + c * C_DV, C_DV), :].rearrange("(h p) t -> p h t", p=C_DK))\
                    .then_inc(gla_z_in, 16)
                load_quarter(s + 2, 3, c * A_WIDTH)

            gla_loads(0)
            with sp.Fori(1, C_HEADS) as c:
                gla_loads(c)

            stores_counted = sp.alloc_register("stores_counted")
            sp.reg_mov(stores_counted, 0)

            def saved_of(pair, g):
                saved(S_LOOP_A - 1 if first_pair(pair) else S_PAIRS + PAIR_GROUPS * pair + g)

            def load_q(pair, base, row):
                sp.wait_ge(qh_done, 2 * pair)
                sp.wait_ge(ql_done, 2 * pair)
                saved_of(pair, 0)
                load_rows(raw[:, 0, :], base + row, P, q_in)

            def load_k(pair, base, stride, row):
                sp.wait_ge(kh_done, 2 * pair)
                sp.wait_ge(k_other_done, 2 * pair)
                sp.wait_ge(kl_done, 2 * pair)
                saved_of(pair, 1)
                load_rows(raw[:, 1, :], base + stride + row, P, k_in)

            def load_values(pair, base, stride, row):
                saved_of(pair, 2)
                sp.wait_ge(normed, 2 * (pair + 1))
                load_rows(sq_wide, base + 2 * stride + row, P, v_in)
                if base == COL_B:
                    sp.wait_ge(masked, ITEMS * (pair - 1) + NT)
                    load_bias(pair, 0)

            def load_bias(pair, h):
                sp.dma_start(logit_bias[:, h, :], decay[bass.ds(2 * (pair - A_PAIRS) + h, 1), :]
                             .broadcast_to([P, SEQ])).then_inc(bias_in[h], 16)

            def store_pair(pair):
                sp.wait_ge(o_done, 4 * (pair + 1))
                sp.dma_start(mixed[bass.ds(pair * P, P), :], vz[:]).then_inc(mixed_saved, 16)

            def pair_loads(pair, base, stride, row, next_group, next_base, next_stride, next_row):
                def weights(g, kqs):
                    if next_group is not None:
                        for kq in kqs:
                            load_quarter(next_group + g, kq, next_base + g * next_stride + next_row)

                first = isinstance(pair, int) and pair == 0
                weights(0, range(2 if first else 0, 3))
                if not first:
                    store_pair(pair - 1)
                    sp.reg_add(stores_counted, stores_counted, 16)
                saved_of(pair, 3)
                if not first:
                    sp.wait_ge(mixed_saved, stores_counted)
                load_rows(vz[:], base + 3 * stride + row, P, z_in)
                if base == COL_B:
                    load_bias(pair, 1)
                weights(0, (3,))
                weights(1, range(3))
                if next_group is not None:
                    load_q(pair + 1, next_base, next_row)
                weights(1, (3,))
                weights(2, range(3))
                if next_group is not None:
                    load_k(pair + 1, next_base, next_stride, next_row)
                weights(2, (3,))
                weights(3, range(4))
                if next_group is not None:
                    load_values(pair + 1, next_base, next_stride, next_row)

            def load_out_quarter(cg, kk):
                sp.wait_ge(lo_done, Q_OUT + 16 * cg + kk - 1)
                sp.dma_start(w_raw[:, kk % 2, :], w_out_k[:, OUT_ORDER[kk], bass.ds(cg * HALF, HALF)])\
                    .then_inc(w_in_sem[kk % 2], 16)

            for kq in range(2):
                load_quarter(S_LOOP_A, kq, P)
            store_head(C_HEADS - 1)
            sp.wait_ge(gla_saved, 16 * C_HEADS)
            load_q(0, 0, 0)
            load_k(0, 0, A_WIDTH, 0)
            load_values(0, 0, A_WIDTH, 0)
            pair_loads(0, 0, A_WIDTH, 0, S_LOOP_A, 0, A_WIDTH, P)
            with sp.Fori(1, A_PAIRS - 1) as p:
                pair_loads(p, 0, A_WIDTH, p * P, S_LOOP_A + 4 * p, 0, A_WIDTH, (p + 1) * P)
            pair_loads(A_PAIRS - 1, 0, A_WIDTH, (A_PAIRS - 1) * P, S_B0, COL_B, B_WIDTH, 0)
            with sp.Fori(0, B_PAIRS - 1) as p:
                pair_loads(A_PAIRS + p, COL_B, B_WIDTH, p * P, S_LOOP_B + 4 * p, COL_B, B_WIDTH, (p + 1) * P)
            load_out_quarter(0, 0)
            load_out_quarter(0, 1)
            pair_loads(A_PAIRS + B_PAIRS - 1, COL_B, B_WIDTH, (B_PAIRS - 1) * P, None, 0, 0, 0)

            def load_res(cg):
                for t in range(NT):
                    if not isinstance(cg, int):
                        sp.wait_ge(out_saved[t], 16 * cg)
                    sp.dma_start(res[:, t, :], x_rows[t * P:(t + 1) * P, bass.ds(cg * HALF, HALF)])\
                        .then_inc(res_in[t], 16)

            def save_out(cg, t):
                sp.wait_ge(out_summed, NT * cg + t + 1)
                sp.dma_start(out_rows[t * P:(t + 1) * P, bass.ds(cg * HALF, HALF)], res[:, t, :])\
                    .then_inc(out_saved[t], 16)

            sp.wait_ge(ql_done, 2 * (A_PAIRS + B_PAIRS))
            sp.wait_ge(qh_done, 2 * (A_PAIRS + B_PAIRS))
            sp.wait_ge(kh_done, 2 * (A_PAIRS + B_PAIRS))
            sp.wait_ge(k_other_done, 2 * (A_PAIRS + B_PAIRS))
            sp.wait_ge(kl_done, 2 * (A_PAIRS + B_PAIRS))
            for kk in range(KT):
                if kk == 0:
                    sp.wait_ge(mixed_saved, 16 * (A_PAIRS + B_PAIRS - 1))
                    sp.wait_ge(gla_saved, 16 * C_HEADS)
                if kk == KT - 1:
                    store_pair(A_PAIRS + B_PAIRS - 1)
                    sp.wait_ge(mixed_saved, 16 * (A_PAIRS + B_PAIRS))
                if kk >= 2:
                    sp.wait_ge(mix_lo, kk - 1)
                sp.dma_start(raw[:, kk % 2, :], mixed[OUT_ORDER[kk] * P:(OUT_ORDER[kk] + 1) * P, :])\
                    .then_inc(mix_in[kk % 2], 16)
            sp.wait_ge(o_done, 4 * (A_PAIRS + B_PAIRS))
            sp.wait_ge(mixed_saved, 16 * (A_PAIRS + B_PAIRS))
            load_res(0)
            for kk in range(2, KT):
                load_out_quarter(0, kk)
            with sp.Fori(1, OUT_CG) as cg:
                load_out_quarter(cg, 0)
                load_out_quarter(cg, 1)
                for t in range(NT):
                    save_out(cg - 1, t)
                load_res(cg)
                for kk in range(2, KT):
                    load_out_quarter(cg, kk)
            for t in range(NT):
                save_out(OUT_CG - 1, t)
            for t in range(NT):
                sp.wait_ge(out_saved[t], 16 * OUT_CG)

        @block.gpsimd
        def _(pool):
            pool.memset(eps_col[:], EPS).then_inc(eps_ready, 1)
            pool.memset(ident[:], 0.0).then_inc(consts, 1)
            pool.memset(causal[:], 0.0).then_inc(consts, 1)
            pool.memset(half_ones[:], 0.0).then_inc(consts, 1)
            pool.wait_ge(consts, 3)
            pool.affine_select(out=ident[:], in_=ident[:], compare_op=ALU.not_equal, fill=1.0, base=0,
                                   pattern=[[-1, P]], channel_multiplier=1).then_inc(consts, 1)
            pool.affine_select(out=causal[:], in_=causal[:], compare_op=ALU.is_ge, fill=FAR, base=0,
                                   pattern=[[-1, P]], channel_multiplier=1).then_inc(consts, 1)
            pool.wait_ge(consts, 5)
            pool.memset(half_ones[0:HEAD, 0:HEAD], 1.0).then_inc(consts, 1)
            pool.wait_ge(consts, 6)
            pool.memset(half_ones[HEAD:P, HEAD:P], 1.0).then_inc(consts, 1)
            pool.wait_ge(consts, 7)
            pool.iota(dist_i[:], [[-1, SEQ]], base=(NT - 1) * P, channel_multiplier=1).then_inc(consts, 1)

            pool.wait_ge(c_done, 1)
            pool.wait_ge(small_saved, 16)
            pool.wait_ge(c_saved, 16)
            pool.memset(level_mask[:, :, :], 1.0).then_inc(levels_ready, 1)
            pool.wait_ge(levels_ready, 1)
            for l in range(LEVELS):
                b = 1 << l
                v = level_mask[:, l, :].rearrange("p (n r) -> p n r", r=b)
                pool.affine_select(out=v, in_=v, compare_op=ALU.is_ge, fill=0.0, base=0,
                                       pattern=[[-2 * b, HEAD // b], [0, b]], channel_multiplier=1).then_inc(levels_ready, 1)
            pool.wait_ge(levels_ready, 1 + LEVELS)
            for l in range(LEVELS):
                b = 1 << l
                v = level_mask[:, l, :].rearrange("p (n r) -> p n r", r=b)
                pool.affine_select(out=v, in_=v, compare_op=ALU.is_ge, fill=0.0, base=b - 1,
                                       pattern=[[2 * b, HEAD // b], [0, b]], channel_multiplier=-1).then_inc(levels_ready, 1)
            pool.memset(k_level[:, :, :], 0.0).then_inc(levels_ready, 1)
            pool.wait_ge(levels_ready, 2 + 2 * LEVELS)

            def gla_head(c):
                pool.wait_ge(gla_scaled, c + 1)
                pool.wait_ge(gla_k_in, 16 * (c + 1))
                for l in range(LEVELS):
                    b, n = 1 << l, LEVELS * c + l
                    pool.wait_ge(gla_lv, n - 1 if l >= 2 else LEVELS * c)
                    pool.wait_ge(gla_decay, n + 1)
                    pool.tensor_tensor(q_level[:, l % 2, :].rearrange("p (n r) -> p n r", r=b),
                                           blocks(g_q, b)[:, :, 1, :], blocks(g_t[:, l % 2, :], b)[:, :, 1, :],
                                           ALU.mult).then_inc(gla_ql, 1)
                    pool.tensor_tensor(blocks(k_level[:, l % 2, :], b)[:, :, 0, :], blocks(g_k, b)[:, :, 0, :],
                                           blocks(g_t[:, l % 2, :], b)[:, :, 0, :], ALU.mult).then_inc(gla_kl, 1)
                pool.wait_ge(gla_vt, 4 * (c + 1))
                pool.wait_ge(gla_eb, c + 1)
                pool.tensor_tensor(q_carry, g_q, g_t[:, 0, :], ALU.mult).then_inc(gla_qe, 1)
                pool.wait_ge(gla_le, c + 1)
                pool.tensor_tensor(k_carry, g_k, g_t[:, 1, :], ALU.mult).then_inc(gla_ke, 1)
                pool.wait_ge(gla_sigmoid, c + 1)
                pool.tensor_tensor(g_z[:, :, :], g_z[:, :, :], g_t[:, :, :], ALU.mult).then_inc(gla_silu, 1)

            gla_head(0)
            with pool.Fori(1, C_HEADS) as c:
                gla_head(c)

            def low_parts(pair, h):
                own, other = slice(h * HEAD, (h + 1) * HEAD), slice((1 - h) * HEAD, (2 - h) * HEAD)
                pool.wait_ge(s_done, ITEMS * (pair - 1) + NT * (h + 1)) if not first_pair(pair) else None
                pool.wait_ge(qh_done, 2 * pair + h + 1)
                pool.tensor_tensor(q_st[other, h, :], raw[own, 0, :], q_st[own, h, :].bitcast(F32),
                                   ALU.subtract).then_inc(ql_done, 1)
                pool.wait_ge(kh_done, 2 * pair + h + 1)
                pool.tensor_tensor(k_lo[own, :], raw[own, 1, :], k_hi[own, h, :].bitcast(F32),
                                   ALU.subtract).then_inc(kl_done, 1)

            for h in range(2):
                low_parts(0, h)
            with pool.Fori(1, A_PAIRS + B_PAIRS) as p:
                for h in range(2):
                    low_parts(p, h)

        @block.scalar
        def _(act):
            def split_hi(s, kq):
                slot = kq % 2
                if kq == 1 and not (isinstance(s, int) and s == 0):
                    act.wait_ge(half_done, 2 * s)
                if kq >= 2:
                    act.wait_ge(quarter_done, 3 * s + kq - 1)
                act.wait_ge(w_in_sem[slot], 16 * (2 * s + kq // 2 + 1))
                act.activation(w_hi[:, slot, :], w_raw[:, slot, :], ACT.Copy).then_inc(hi_done, 1)

            def split_hi_out(cg, kk):
                slot = kk % 2
                if kk == 1:
                    act.wait_ge(half_done, 2 * GROUPS) if isinstance(cg, int) and cg == 0 else \
                        act.wait_ge(out_ready, NT * cg)
                else:
                    act.wait_ge(quarter_done, 3 * GROUPS + (KT - 1) * cg + kk - 1)
                act.wait_ge(w_in_sem[slot], 16 * (2 * GROUPS + 8 * cg + kk // 2 + 1))
                act.activation(w_hi[:, slot, :], w_raw[:, slot, :], ACT.Copy).then_inc(hi_done, 1)

            def evac(s, th):
                act.wait_ge(half_done, 2 * s + th + 1)
                if not (isinstance(s, int) and s == 0):
                    act.wait_ge(proj_saved[th], 16 * s)
                act.activation(stage[:, th, :], bank[th][:], ACT.Copy).then_inc(evac_done, 1)

            def save(s, row):
                for th in range(2):
                    act.wait_ge(evac_done, 2 * s + th + 1)
                    act.dma_start(proj[bass.ds(row, P), th * HALF:(th + 1) * HALF], stage[:, th, :])\
                        .then_inc(proj_saved[th], 16)

            def group(s, row, steps):
                for slot in range(8):
                    if slot % 2 == 0:
                        split_hi(s, slot // 2 + 1)
                    if slot == 7:
                        evac(s, 0)
                    steps(slot)
                evac(s, 1)
                save(s, row)

            act.add_instruction(mybir.InstLoadActFuncSet(name=nc.get_next_instruction_name(), act_func_set_id=LN_EXP_SET))

            act.wait_ge(eps_ready, 1)
            for t in range(NT + 1):
                if t < NT:
                    act.wait_ge(x_in[t % 2], 16 * (t // 2 + 1))
                    act.activation(junk[:], x_tile[:, t % 2, :], ACT.Square, accum_out=x_ssq[:, t:t + 1]).then_inc(x_squared, 1)
                    act.wait_ge(x_squared, t + 1)
                    act.activation(x_log[:, t:t + 1], x_ssq[:, t:t + 1], ACT.Ln, scale=1.0 / D_MODEL,
                                   bias=eps_col[:]).then_inc(x_logged, 1)
                    act.wait_ge(x_logged, t + 1)
                    act.activation(x_rstd[:, t:t + 1], x_log[:, t:t + 1], ACT.Exp, scale=-0.5).then_inc(x_rooted, 1)
                if t >= 1:
                    for b in range(4):
                        act.wait_ge(x_turned, 4 * (t - 1) + b + 1)
                        act.activation(act_hi[:, 4 * b:4 * b + 4, (t - 1) * P:t * P],
                                           banks[4 * ((t - 1) % 2) + b].rearrange("p (k t) -> p k t", k=4), ACT.Copy).then_inc(x_hi_done, 1)
            act.wait_ge(small_in, 32)
            act.activation(ws_hi[:, :, :], ws_raw[:, :, :], ACT.Copy).then_inc(ws_hi_done, 1)
            split_hi(0, 0)
            act.wait_ge(consts, 8)
            act.activation(ident_r[:], ident[:], ACT.Copy).then_inc(rounded_consts, 1)
            act.activation(causal_r[:], causal[:], ACT.Copy).then_inc(rounded_consts, 1)
            act.activation(half_ones_r[:], half_ones[:], ACT.Copy).then_inc(rounded_consts, 1)
            act.wait_ge(small_done, 1)
            act.activation(small[:], scores[0:SMALL, :], ACT.Copy).then_inc(small_out, 1)

            group(0, COL_CQ, lambda slot: None)
            with act.Fori(1, C_FIRST) as s:
                group(s, COL_CQ + s * P, lambda slot: None)
            for g in range(C_ALONE - C_FIRST):
                group(C_FIRST + g, COL_CZ + g * P, lambda slot: None)

            act.wait_ge(lf_step, 1)
            act.activation(lf_abs, lf_min, ACT.Abs).then_inc(lf_step, 1)
            act.wait_ge(lf_step, 2)
            act.activation(lf_abs, lf_abs, ACT.Exp, scale=-1.0).then_inc(lf_step, 1)
            act.wait_ge(lf_step, 3)
            act.activation(lf_abs, lf_abs, ACT.Ln, bias=1.0).then_inc(lf_step, 1)
            act.wait_ge(c_done, 1)
            act.dma_start(decay[:, :], c_sum[:]).then_inc(c_saved, 16)

            def gla_steps(c, slot):
                if slot == G_GATE:
                    act.wait_ge(gla_q_in, 16 * (c + 1))
                    act.mul(g_q, g_q, float(C_DK) ** -0.5).then_inc(gla_scaled, 1)
                    act.wait_ge(gla_sum, c + 1)
                    act.activation(g_t[:, 1, :], g_t[:, 0, :], ACT.Abs).then_inc(gla_abs, 1)
                    act.wait_ge(gla_abs, c + 1)
                    act.activation(g_t[:, 1, :], g_t[:, 1, :], ACT.Exp, scale=-1.0).then_inc(gla_exp, 1)
                    act.wait_ge(gla_exp, c + 1)
                    act.activation(g_t[:, 1, :], g_t[:, 1, :], ACT.Ln, bias=1.0).then_inc(gla_log, 1)
                for l in range(LEVELS):
                    if slot == G_LEVEL[l]:
                        act.wait_ge(gla_diff, 2 * (LEVELS * c + l) + 2)
                        act.activation(g_t[:, l % 2, :], g_t[:, l % 2, :], ACT.Exp).then_inc(gla_decay, 1)
                if slot == G_TURN_V:
                    for i in range(4):
                        act.wait_ge(gla_vt, 4 * c + i + 1)
                        act.activation(v_rows[:, 2 * i:2 * i + 2, :],
                                       banks[2 + i][:, 0:2 * C_DV].rearrange("p (t v) -> p t v", t=2), ACT.Copy)\
                            .then_inc(gla_vcopy, 1)
                if slot == G_CARRY:
                    act.wait_ge(gla_kl, LEVELS * (c + 1))
                    act.activation(g_t[:, 0, :], g_b[:], ACT.Exp).then_inc(gla_eb, 1)
                    act.wait_ge(gla_ldiff, c + 1)
                    act.activation(g_t[:, 1, :], g_t[:, 1, :], ACT.Exp).then_inc(gla_le, 1)
                if slot == G_TURN_K:
                    for i in range(2):
                        act.wait_ge(gla_kt, 2 * c + i + 1)
                        act.activation(k_rows[:, 4 * i:4 * i + 4, :],
                                       banks[6 + i][:, 0:4 * C_DK].rearrange("p (t d) -> p t d", t=4), ACT.Copy)\
                            .then_inc(gla_kcopy, 1)
                if slot == G_Z:
                    act.wait_ge(gla_zb, c + 1)
                    act.activation(g_t[:, :, :], g_t[:, :, :], ACT.Exp, scale=-1.0).then_inc(gla_ez, 1)
                    act.wait_ge(gla_ez, 2 * c + 1)
                    act.activation(g_t[:, :, :], g_t[:, :, :], ACT.Ln, bias=1.0).then_inc(gla_ez, 1)
                    act.wait_ge(gla_ez, 2 * c + 2)
                    act.activation(g_t[:, :, :], g_t[:, :, :], ACT.Exp, scale=-1.0).then_inc(gla_sigmoid, 1)
                if slot == G_OUT:
                    for i in range(4):
                        act.wait_ge(gla_o, 4 * c + i + 1)
                        act.activation(o_rows[:, 2 * i:2 * i + 2, :],
                                       banks[2 + i][:, 0:2 * C_DV].rearrange("p (t v) -> p t v", t=2), ACT.Copy)\
                            .then_inc(gla_ocopy, 1)
                        act.wait_ge(gla_ocopy, 4 * c + i + 1)
                        for t in (2 * i, 2 * i + 1):
                            act.wait_ge(gla_osq, NT * c + max(t - 1, 0))
                            act.activation(o_junk[:, t % 2, :], o_rows[:, t, :], ACT.Square,
                                           accum_out=o_ssq[:, t:t + 1]).then_inc(gla_osq, 1)
                    act.wait_ge(gla_osq, NT * (c + 1))
                    act.activation(o_rstd[:], o_ssq[:], ACT.Ln, scale=1.0 / C_DV, bias=eps_col[:]).then_inc(gla_ln, 1)
                    act.wait_ge(gla_ln, c + 1)
                    act.activation(o_rstd[:], o_rstd[:], ACT.Exp, scale=-0.5).then_inc(gla_rstd, 1)

            def gla_head(c):
                s = C_ALONE + HEAD_GROUPS * c
                group(s, COL_CV + (2 + c) * P, lambda slot: gla_steps(c, slot))
                group(s + 1, COL_CZ + (2 + c) * P, lambda slot: gla_steps(c, 8 + slot))
                group(s + 2, c * A_WIDTH, lambda slot: gla_steps(c, 16 + slot))

            gla_head(0)
            with act.Fori(1, C_HEADS) as c:
                gla_head(c)

            def square(pair, m):
                if m % 2 == 0:
                    act.wait_ge((q_in, k_in)[m // 2], 16 * (pair + 1))
                if m < 2:
                    act.wait_ge(silu_done, pair)
                else:
                    act.wait_ge(normed, 2 * pair + 1)
                if m > 0:
                    act.wait_ge(ssq_done, 4 * pair + m)
                src = raw[:, m // 2, (m % 2) * HALF:(m % 2 + 1) * HALF]
                act.activation(sq[:, m % 2, :], src, ACT.Square).then_inc(sq_done, 1)
                act.activation(sq_hi[:], src, ACT.Square).then_inc(sq_done, 1)

            def log_sum(pair, m):
                act.wait_ge(ssq_done, 4 * pair + m + 1)
                act.activation(sq[:, m % 2, :], spare[:], ACT.Ln, scale=1.0 / HEAD, bias=eps_col[:]).then_inc(ssq_logged, 1)

            def root(pair, i):
                act.wait_ge(ssq_logged, 4 * pair + 2 * i + 2)
                act.activation(sq_wide, sq_wide, ACT.Exp, scale=-0.5).then_inc(root_done, 1)

            def stack(pair, h):
                own = slice(h * HEAD, (h + 1) * HEAD)
                if not first_pair(pair):
                    act.wait_ge(s_done, ITEMS * (pair - 1) + NT * (h + 1))
                act.wait_ge(normed, 2 * (pair + 1))
                act.activation(q_st[own, h, :], raw[own, 0, :], ACT.Copy).then_inc(qh_done, 1)
                act.activation(k_hi[own, h, :], raw[own, 1, :], ACT.Copy).then_inc(kh_done, 1)

            def values(pair, b):
                act.wait_ge(pv_done, ITEMS * pair)
                act.wait_ge(v_turned, 2 * pair + b + 1)
                act.activation(v_st[:, :, 4 * b:4 * b + 4, 0:HEAD],
                               spare[:].rearrange("p (t h c) -> p h t c", t=4, h=2), ACT.Copy).then_inc(vh_done, 1)

            def gate(pair):
                act.wait_ge(z_bounded, pair + 1)
                act.activation(sq_wide, sq_wide, ACT.Exp, scale=-1.0).then_inc(gate_chain, 1)
                act.wait_ge(gate_chain, 2 * pair + 1)
                act.activation(sq_wide, sq_wide, ACT.Ln, bias=1.0).then_inc(gate_chain, 1)
                act.wait_ge(gate_chain, 2 * pair + 2)
                act.activation(sq_wide, sq_wide, ACT.Exp, scale=-1.0).then_inc(sigmoid_done, 1)

            def score(pair, j):
                n = (j % NT + 1) * P
                act.wait_ge(masked, ITEMS * pair + j + 1)
                act.activation(prob[:, j % 2, 0:n], prob[:, j % 2, 0:n], ACT.Exp, scale=-1.0, bias=neg_max[:, j:j + 1],
                                   accum_out=denom[:, j:j + 1]).then_inc(exp_done, 1)

            def turn(pair, j):
                n = (j % NT + 1) * P
                act.wait_ge(pv_done, ITEMS * pair + j)
                act.wait_ge(t_done, ITEMS * pair + j + 1)
                act.activation(pt_hi[:, 0:n], turned[:, 0:n], ACT.Copy).then_inc(pth_done, 1)

            def product(pair, j):
                if j % 4 == 3:
                    h, u = j // NT, j // 4
                    own, other = slice(h * HEAD, (h + 1) * HEAD), slice((1 - h) * HEAD, (2 - h) * HEAD)
                    act.wait_ge(o_done, 4 * pair + u)
                    act.wait_ge(pv_done, ITEMS * pair + j + 1)
                    act.activation(o_part[own, :], pv[other, :], ACT.Copy).then_inc(o_moved, 1)

            def steps_at(pair, slot, has_next=True):
                for name, j in steps_of(slot):
                    if name == "values":
                        values(pair, j)
                    elif name == "product":
                        product(pair, j)
                    elif name == "turn":
                        turn(pair, j)
                    elif name == "score":
                        score(pair, j)
                    elif name == "stack1":
                        stack(pair, 1)
                    elif name == "gate":
                        gate(pair)
                    elif name == "square" and has_next:
                        square(pair + 1, j)
                    elif name == "sum" and has_next:
                        log_sum(pair + 1, j)
                    elif name == "root" and has_next:
                        root(pair + 1, j)
                    elif name == "stack0" and has_next:
                        stack(pair + 1, 0)

            for i in range(2):
                square(0, 2 * i)
                square(0, 2 * i + 1)
                log_sum(0, 2 * i)
                log_sum(0, 2 * i + 1)
                root(0, i)
            stack(0, 0)

            def pair_body(pair, s0, base, stride, row, projecting=True):
                for g in range(PAIR_GROUPS):
                    def steps(slot, g=g):
                        steps_at(pair, 8 * g + slot, projecting)
                    if projecting:
                        group(s0 + g, base + g * stride + row, steps)
                    else:
                        for slot in range(8):
                            steps(slot)
                            mix_hi_part(8 * g + slot - MIX_SLOT)
                steps_at(pair, SLOTS)

            def mix_hi_part(kk):
                if 0 <= kk < KT - 1:
                    act.wait_ge(mix_in[kk % 2], 16 * (kk // 2 + 1))
                    act.wait_ge(half_done, 2 * GROUPS)
                    act.activation(act_hi[:, OUT_ORDER[kk], :], raw[:, kk % 2, :], ACT.Copy).then_inc(mix_hi, 1)

            pair_body(0, S_LOOP_A, 0, A_WIDTH, P)
            with act.Fori(1, A_PAIRS - 1) as p:
                pair_body(p, S_LOOP_A + 4 * p, 0, A_WIDTH, (p + 1) * P)
            pair_body(A_PAIRS - 1, S_B0, COL_B, B_WIDTH, 0)
            with act.Fori(0, B_PAIRS - 1) as p:
                pair_body(A_PAIRS + p, S_LOOP_B + 4 * p, COL_B, B_WIDTH, (p + 1) * P)
            pair_body(A_PAIRS + B_PAIRS - 1, None, 0, 0, 0, projecting=False)

            kk = KT - 1
            act.wait_ge(mix_in[kk % 2], 16 * (kk // 2 + 1))
            act.activation(act_hi[:, OUT_ORDER[kk], :], raw[:, kk % 2, :], ACT.Copy).then_inc(mix_hi, 1)
            for kk in range(KT):
                split_hi_out(0, kk + 1)
            with act.Fori(1, OUT_CG - 1) as cg:
                for kk in range(KT):
                    split_hi_out(cg, kk + 1)
            for kk in range(KT - 1):
                split_hi_out(OUT_CG - 1, kk + 1)

        @block.vector
        def _(dve):
            def split_lo(s, kq):
                slot = kq % 2
                dve.wait_ge(hi_done, 4 * s + kq + 1)
                dve.tensor_tensor(w_lo[:, slot, :], w_raw[:, slot, :], w_hi[:, slot, :].bitcast(F32), ALU.subtract).then_inc(lo_done, 1)

            def group(s, steps):
                for slot in range(8):
                    if slot % 2 == 0:
                        split_lo(s, slot // 2 + 1)
                    steps(slot)

            for t in range(NT + 1):
                if t < NT:
                    dve.wait_ge(g_in, 16)
                    dve.wait_ge(x_rooted, t + 1)
                    dve.scalar_tensor_tensor(out=x_tile[:, t % 2, :], in0=x_tile[:, t % 2, :],
                                                 scalar=x_rstd[:, t:t + 1], in1=g_wide[:], op0=ALU.mult, op1=ALU.mult).then_inc(x_normed, 1)
                if t >= 1:
                    for b in range(4):
                        dve.wait_ge(x_hi_done, 4 * (t - 1) + b + 1)
                        at = (slice(None), slice(4 * b, 4 * b + 4), slice((t - 1) * P, t * P))
                        dve.tensor_tensor(act_lo[at], banks[4 * ((t - 1) % 2) + b].rearrange(
                            "p (k t) -> p k t", k=4), act_hi[at].bitcast(F32), ALU.subtract).then_inc(x_lo_done, 1)
            dve.wait_ge(ws_hi_done, 1)
            dve.tensor_tensor(ws_lo[:, :, :], ws_raw[:, :, :], ws_hi[:, :, :].bitcast(F32), ALU.subtract).then_inc(ws_lo_done, 1)
            split_lo(0, 0)

            step = [0]

            def link(ins):
                step[0] += 1
                ins.then_inc(dist_chain, 1)
                dve.wait_ge(dist_chain, step[0])

            dve.wait_ge(consts, 8)
            link(dve.tensor_copy(dist[:], dist_i[:]))
            link(dve.tensor_scalar(mod_i[:], dist_i[:], 3, None, ALU.bitwise_and))
            link(dve.tensor_copy(term[:], mod_i[:]))
            link(dve.tensor_scalar(term[:], term[:], 0.0, None, ALU.is_equal))
            link(dve.scalar_tensor_tensor(out=count[:], in0=dist[:], scalar=512.0, in1=term[:], op0=ALU.is_le, op1=ALU.mult))
            link(dve.scalar_tensor_tensor(out=count[:], in0=dist[:], scalar=128.0, in1=count[:], op0=ALU.is_le, op1=ALU.add))
            link(dve.tensor_scalar(mod_i[:], dist_i[:], 15, None, ALU.bitwise_and))
            link(dve.tensor_copy(term[:], mod_i[:]))
            link(dve.tensor_scalar(term[:], term[:], 0.0, None, ALU.is_equal))
            link(dve.tensor_tensor(count[:], count[:], term[:], ALU.add))
            link(dve.scalar_tensor_tensor(out=count[:], in0=dist[:], scalar=0.0, in1=count[:], op0=ALU.is_ge, op1=ALU.mult))
            link(dve.tensor_scalar(term[:], count[:], 0.5, FAR, ALU.is_lt, ALU.mult))
            link(dve.tensor_scalar(dist[:], count[:], 1.5, -LN2, ALU.is_ge, ALU.mult))
            link(dve.tensor_tensor(term[:], term[:], dist[:], ALU.add))
            link(dve.tensor_scalar(dist[:], count[:], 2.5, LN2 - LN3, ALU.is_ge, ALU.mult))
            link(dve.tensor_tensor(logit_bias[:, 1, :], term[:], dist[:], ALU.add))
            dve.wait_ge(gains_in, 16 * 11)
            for n in (0, 2):
                link(dve.tensor_scalar(gains[:, n:n + 1], gains[:, n:n + 1], -float(HEAD) ** -0.5, None, ALU.mult))

            group(0, lambda slot: None)
            with dve.Fori(1, C_ALONE) as s:
                group(s, lambda slot: None)

            dve.wait_ge(small_out, 1)
            dve.tensor_scalar(lf_min, small[0:B_HEADS, :], fox_col[:], None, ALU.add).then_inc(lf_step, 1)
            dve.wait_ge(lf_step, 4)
            dve.scalar_tensor_tensor(out=lf_min, in0=lf_min, scalar=0.0, in1=lf_abs, op0=ALU.min,
                                         op1=ALU.subtract).then_inc(lf_step, 1)
            dve.wait_ge(lf_step, 5)
            dve.tensor_tensor_scan(out=c_sum[:], data0=lf_min, data1=lf_min, initial=0.0, op0=ALU.add,
                                       op1=ALU.bypass).then_inc(c_done, 1)

            dve.wait_ge(levels_ready, 2 + 2 * LEVELS)
            levels_put, items_scored = dve.alloc_register("levels_put"), dve.alloc_register("items_scored")
            dve.reg_mov(levels_put, 0)
            dve.reg_mov(items_scored, 0)

            def gla_steps(c, slot):
                if slot == G_GATE:
                    dve.wait_ge(gla_bias_in, 16 * (c + 1))
                    dve.wait_ge(gla_silu, c)
                    dve.wait_ge(gla_gate, c + 1)
                    dve.tensor_scalar(g_t[:, 0, :], scores[0:C_DK, :], gate_bias[:], None, ALU.add).then_inc(gla_sum, 1)
                    dve.wait_ge(gla_log, c + 1)
                    dve.tensor_scalar(g_t[:, 0, :], g_t[:, 0, :], 0.0, 1.0 / 16, ALU.min, ALU.mult).then_inc(gla_min, 1)
                    dve.wait_ge(gla_min, c + 1)
                    dve.scalar_tensor_tensor(out=g_t[:, 0, :], in0=g_t[:, 1, :], scalar=-1.0 / 16, in1=g_t[:, 0, :],
                                                 op0=ALU.mult, op1=ALU.add).then_inc(gla_a, 1)
                    dve.wait_ge(gla_a, c + 1)
                    for t in range(NT):
                        at = slice(t * P, (t + 1) * P)
                        dve.tensor_tensor_scan(out=g_b[:, at], data0=g_t[:, 0, at], data1=g_t[:, 0, at],
                                                   initial=0.0, op0=ALU.add, op1=ALU.bypass).then_inc(gla_scan, 1)
                    dve.wait_ge(gla_scan, NT * (c + 1))
                    dve.memset(weights_t, 0.0).then_inc(gla_zero, 1)
                    dve.wait_ge(gla_zero, c + 1)
                    dve.wait_ge(gla_diag, c + 1)
                    put(weights_t.rearrange("p (t q) -> p t q", t=NT),
                        ident[:].unsqueeze(1).broadcast_to([P, NT, P]), turned[:].rearrange("p (t q) -> p t q", t=NT))
                for l in range(LEVELS):
                    if slot == G_LEVEL[l]:
                        b, n = 1 << l, LEVELS * c + l
                        bv, ev = blocks(g_b[:], b), blocks(g_t[:, l % 2, :], b)
                        edge = bv[:, :, 0, b - 1:b].broadcast_to([C_DK, SEQ // (2 * b), b])
                        dve.wait_ge(gla_kl, n - 1 if l >= 2 else LEVELS * c)
                        dve.tensor_tensor(ev[:, :, 1, :], bv[:, :, 1, :], edge, ALU.subtract).then_inc(gla_diff, 1)
                        dve.tensor_tensor(ev[:, :, 0, :], edge, bv[:, :, 0, :], ALU.subtract).then_inc(gla_diff, 1)
                        if l >= 1:
                            put_level(c, l - 1)
                if slot == G_CARRY - 1:
                    dve.wait_ge(gla_kl, LEVELS * (c + 1) - 1)
                    bt = g_b[:].rearrange("p (t q) -> p t q", t=NT)
                    dve.tensor_tensor(g_t[:, 1, :].rearrange("p (t q) -> p t q", t=NT),
                                          bt[:, :, P - 1:P].broadcast_to([C_DK, NT, P]), bt, ALU.subtract).then_inc(gla_ldiff, 1)
                if slot == G_CARRY:
                    put_level(c, LEVELS - 1)
                if slot == G_STATE:
                    for t in range(1, NT):
                        i = t - 1
                        src = banks[2 + i // 2][0:C_DK, (i % 2) * C_DV:(i % 2 + 1) * C_DV]
                        if t == 1:
                            dve.wait_ge(gla_eb, c + 1)
                            dve.wait_ge(gla_ds, c + 1)
                            dve.tensor_copy(state[:, 1, :], src).then_inc(gla_state, 1)
                        else:
                            dve.wait_ge(gla_state, (NT - 1) * c + t - 1)
                            dve.scalar_tensor_tensor(out=state[:, t, :], in0=state[:, t - 1, :],
                                                         scalar=g_t[:, 0, i * P + P - 1:i * P + P], in1=src,
                                                         op0=ALU.mult, op1=ALU.add).then_inc(gla_state, 1)
                if slot == G_Z:
                    dve.wait_ge(gla_ke, c + 1)
                    dve.wait_ge(gla_z_in, 16 * (c + 1))
                    dve.wait_ge(gla_state, (NT - 1) * (c + 1))
                    dve.tensor_scalar(g_t[:, :, :], g_z[:, :, :], LOWEST, None, ALU.max).then_inc(gla_zb, 1)
                if slot == G_NORM:
                    dve.wait_ge(gla_rstd, c + 1)
                    dve.tensor_tensor(o_rows, o_rows, o_rstd[:].unsqueeze(2).broadcast_to([P, NT, C_DV]), ALU.mult).then_inc(gla_norm, 1)
                if slot == G_FINAL:
                    dve.wait_ge(gla_silu, c + 1)
                    for h in range(2):
                        dve.wait_ge(gla_ot, 2 * c + h + 1)
                        dve.scalar_tensor_tensor(out=g_z[:, h, :], in0=(scores, turned)[h][0:C_DK, :],
                                                     scalar=out_gain[:, h:h + 1], in1=g_z[:, h, :], op0=ALU.mult,
                                                     op1=ALU.mult).then_inc(gla_out, 1)

            def put(dst, mask, data):
                dve.reg_add(levels_put, levels_put, 1)
                dve.copy_predicated(dst, mask.bitcast(I32), data).then_inc(gla_put, 1)

            def put_level(c, l):
                b = 1 << l
                dve.wait_ge(gla_put, levels_put)
                dve.wait_ge(gla_lv, LEVELS * c + l + 1)
                put(blocks(weights_t, b)[:, :, 1, :].rearrange("p (t n) r -> p t n r", t=NT),
                    level_mask[:, l, :].rearrange("p (n r) -> p n r", r=b).unsqueeze(1).broadcast_to([P, NT, HEAD // b, b]),
                    banks[6 + l % 2].rearrange("p (t n r) -> p t n r", t=NT, r=b))

            def gla_head(c):
                for g in range(HEAD_GROUPS):
                    group(C_ALONE + HEAD_GROUPS * c + g, lambda slot: gla_steps(c, 8 * g + slot))

            gla_head(0)
            with dve.Fori(1, C_HEADS) as c:
                gla_head(c)

            def square(pair, m):
                dve.wait_ge(sq_done, 2 * (4 * pair + m + 1))
                dve.tensor_tensor(sq_lo[:], sq[:, m % 2, :], sq_hi[:].bitcast(F32),
                                  ALU.subtract).then_inc(sq_lo_done, 1)

            def norm(pair, i, kind):
                dve.wait_ge(root_done, 2 * pair + i + 1)
                dve.scalar_tensor_tensor(out=raw[:, i, :], in0=raw[:, i, :], scalar=gains[:, 2 * kind + i:2 * kind + i + 1],
                                         in1=sq_wide, op0=ALU.mult, op1=ALU.mult).then_inc(normed, 1)

            def stack(pair, h):
                own, other = slice(h * HEAD, (h + 1) * HEAD), slice((1 - h) * HEAD, (2 - h) * HEAD)
                dve.wait_ge(normed, 2 * (pair + 1))
                if not first_pair(pair):
                    dve.wait_ge(s_done, ITEMS * (pair - 1) + NT * (h + 1))
                dve.tensor_copy(k_hi[other, h, :], raw[own, 1, :]).then_inc(k_other_done, 1)

            def values(pair, b):
                dve.wait_ge(vh_done, 2 * pair + b + 1)
                at = v_st[:, :, 4 * b:4 * b + 4, :]
                dve.tensor_tensor(at[:, :, :, HEAD:P], spare[:].rearrange("p (t h c) -> p h t c", t=4, h=2),
                                  at[:, :, :, 0:HEAD].bitcast(F32), ALU.subtract).then_inc(vl_done, 1)

            def bound(pair):
                dve.wait_ge(z_in, 16 * (pair + 1))
                dve.wait_ge(v_turned, 2 * (pair + 1))
                dve.tensor_scalar(sq_wide, vz[:], LOWEST, None, ALU.max).then_inc(z_bounded, 1)

            def silu(pair):
                dve.wait_ge(sigmoid_done, pair + 1)
                dve.tensor_tensor(vz[:], vz[:], sq_wide, ALU.mult).then_inc(silu_done, 1)

            def score(pair, j, kind):
                h, i = j // NT, j % NT
                n = (i + 1) * P
                it = ITEMS * pair + j
                bias = logit_bias[:, 1, (NT - 1 - i) * P:SEQ] if kind == 0 else logit_bias[:, h, 0:n]
                if not (first_pair(pair) and j < 2):
                    dve.wait_ge(t_done, it - 1)
                if kind == 1 and i == 0:
                    dve.wait_ge(bias_in[h], 16 * (pair - A_PAIRS + 1))
                dve.wait_ge(s_done, it + 1)
                dve.reg_add(items_scored, items_scored, 1)
                dve.tensor_tensor_reduce(out=prob[:, j % 2, 0:n], in0=scores[:, 0:n], in1=bias, scale=1.0, scalar=3e38,
                                             op0=ALU.add, op1=ALU.min, accum_out=neg_max[:, j:j + 1]).then_inc(masked, 1)

            def scale(pair, j):
                n = (j % NT + 1) * P
                it = ITEMS * pair + j
                dve.wait_ge(exp_done, items_scored)
                dve.reciprocal(inv_denom[:, j:j + 1], denom[:, j:j + 1]).then_inc(recip_done, 1)
                dve.wait_ge(recip_done, it + 1)
                dve.tensor_scalar(prob[:, j % 2, 0:n], prob[:, j % 2, 0:n], inv_denom[:, j:j + 1], None, ALU.mult).then_inc(prob_done, 1)

            def turn(pair, j):
                n = (j % NT + 1) * P
                dve.wait_ge(pth_done, ITEMS * pair + j + 1)
                dve.tensor_tensor(pt_lo[:, 0:n], turned[:, 0:n], pt_hi[:, 0:n].bitcast(F32), ALU.subtract).then_inc(ptl_done, 1)

            def product(pair, j):
                if j % 4 == 3:
                    h, u = j // NT, j // 4
                    own, cols = slice(h * HEAD, (h + 1) * HEAD), slice((u % 2) * HALF, (u % 2 + 1) * HALF)
                    dve.wait_ge(o_moved, 4 * pair + u + 1)
                    dve.tensor_tensor(o_part[own, :], pv[own, :], o_part[own, :], ALU.add).then_inc(o_summed, 1)
                    dve.wait_ge(silu_done, pair + 1)
                    dve.wait_ge(o_summed, 4 * pair + u + 1)
                    dve.tensor_tensor(vz[own, cols], o_part[own, :], vz[own, cols], ALU.mult).then_inc(o_done, 1)

            def steps_at(pair, kind, slot, next_kind):
                for name, j in steps_of(slot):
                    if name == "values":
                        values(pair, j)
                    elif name == "product":
                        product(pair, j)
                    elif name == "turn":
                        turn(pair, j)
                    elif name == "scale":
                        scale(pair, j)
                    elif name == "score":
                        score(pair, j, kind)
                    elif name == "stack1":
                        stack(pair, 1)
                    elif name == "bound":
                        bound(pair)
                    elif name == "silu":
                        silu(pair)
                    elif name == "root" and next_kind is not None:
                        norm(pair + 1, j, next_kind)
                    elif name == "square" and next_kind is not None:
                        square(pair + 1, j)
                    elif name == "stack0" and next_kind is not None:
                        stack(pair + 1, 0)

            for i in range(2):
                for m in (2 * i, 2 * i + 1):
                    square(0, m)
                norm(0, i, 0)
            stack(0, 0)

            def pair_body(pair, kind, s0, next_kind):
                for g in range(PAIR_GROUPS):
                    def steps(slot, g=g):
                        steps_at(pair, kind, 8 * g + slot, next_kind)
                    if next_kind is not None:
                        group(s0 + g, steps)
                    else:
                        for slot in range(8):
                            steps(slot)
                            if 0 <= 8 * g + slot - MIX_SLOT < KT - 1:
                                mix_lo_part(8 * g + slot - MIX_SLOT)
                steps_at(pair, kind, SLOTS, next_kind)

            def mix_lo_part(kk):
                dve.wait_ge(mix_hi, kk + 1)
                dve.tensor_tensor(act_lo[:, OUT_ORDER[kk], :], raw[:, kk % 2, :],
                                      act_hi[:, OUT_ORDER[kk], :].bitcast(F32), ALU.subtract).then_inc(mix_lo, 1)

            pair_body(0, 0, S_LOOP_A, 0)
            with dve.Fori(1, A_PAIRS - 1) as p:
                pair_body(p, 0, S_LOOP_A + 4 * p, 0)
            pair_body(A_PAIRS - 1, 0, S_B0, 1)
            with dve.Fori(0, B_PAIRS - 1) as p:
                pair_body(A_PAIRS + p, 1, S_LOOP_B + 4 * p, 1)
            pair_body(A_PAIRS + B_PAIRS - 1, 1, None, None)

            mix_lo_part(KT - 1)

            def add_residual(cg):
                for t in range(NT):
                    dve.wait_ge(res_in[t], 16 * (cg + 1))
                    dve.wait_ge(out_ready, NT * cg + t + 1)
                    dve.tensor_tensor(res[:, t, :], banks[t], res[:, t, :], ALU.add).then_inc(out_summed, 1)

            for kk in range(KT - 1):
                split_lo(GROUPS, kk + 1)
            split_lo(GROUPS, KT)
            add_residual(0)
            with dve.Fori(1, OUT_CG - 1) as cg:
                for kk in range(KT):
                    split_lo(GROUPS + 4 * cg, kk + 1)
                add_residual(cg)
            for kk in range(KT - 1):
                split_lo(GROUPS + 4 * (OUT_CG - 1), kk + 1)
            add_residual(OUT_CG - 1)

        @block.tensor
        def _(pe):
            def half_quarter(s, kq, th):
                if th == 0:
                    pe.wait_ge(lo_done, 4 * s + kq + 1)
                if kq == 0 and not (isinstance(s, int) and s == 0):
                    pe.wait_ge(evac_done, 2 * s + th - 1)
                at = slice(th * HALF, (th + 1) * HALF)
                for k in range(4):
                    hi, lo = (w[:, kq % 2, k * P:(k + 1) * P] for w in (w_hi, w_lo))
                    xh, xl = (a[:, 4 * kq + k, at] for a in (act_hi, act_lo))
                    first, end = kq == 0 and k == 0, kq == 3 and k == 3
                    pe.matmul(bank[th][:], hi, xh, start=first, stop=False)
                    pe.matmul(bank[th][:], hi, xl, start=False, stop=False)
                    mm = pe.matmul(bank[th][:], lo, xh, start=False, stop=end)
                if kq == 3:
                    mm.then_inc(half_done, 1)
                elif th == 1:
                    mm.then_inc(quarter_done, 1)
                return mm

            def group(s, steps):
                for slot in range(8):
                    steps(slot)
                    kq, th = slot // 2, slot % 2
                    half_quarter(s, kq, th)

            for t in range(NT):
                pe.wait_ge(consts, 8)
                pe.wait_ge(x_normed, t + 1)
                for b in range(4):
                    if t >= 2:
                        pe.wait_ge(x_lo_done, 4 * (t - 2) + b + 1)
                    for k in range(4):
                        f = 4 * b + k
                        mm = pe.transpose(banks[4 * (t % 2) + b][:, k * P:(k + 1) * P],
                                          x_tile[:, t % 2, f * P:(f + 1) * P], ident[:])
                    mm.then_inc(x_turned, 1)
            pe.wait_ge(x_lo_done, 4 * NT)
            pe.wait_ge(ws_lo_done, 1)
            for th in range(2):
                at = slice(th * HALF, (th + 1) * HALF)
                for k in range(KT):
                    pe.matmul(scores[0:SMALL, at], ws_hi[:, k, :], act_hi[:, k, at], start=(k == 0), stop=False)
                    pe.matmul(scores[0:SMALL, at], ws_hi[:, k, :], act_lo[:, k, at], start=False, stop=False)
                    mm = pe.matmul(scores[0:SMALL, at], ws_lo[:, k, :], act_hi[:, k, at], start=False, stop=(k == KT - 1))
            mm.then_inc(small_done, 1)
            group(0, lambda slot: None)
            with pe.Fori(1, C_ALONE) as s:
                group(s, lambda slot: None)

            pe.wait_ge(rounded_consts, 3)

            def gla_steps(c, slot):
                if slot == G_GATE:
                    pe.wait_ge(gla_up_in, 16 * (c + 1))
                    pe.wait_ge(gla_rank_in, 16 * (c + 1))
                    pe.wait_ge(small_out, 1)
                    pe.wait_ge(gla_out, 2 * c)
                    for th in range(2):
                        at = slice(th * HALF, (th + 1) * HALF)
                        mm = pe.matmul(scores[0:C_DK, at], gate_up[:], rank_rows[:, at], start=True, stop=True)
                    mm.then_inc(gla_gate, 1)
                    pe.wait_ge(gla_k_in, 16 * (c + 1))
                    pe.wait_ge(gla_scaled, c + 1)
                    for t in range(NT):
                        at = slice(t * P, (t + 1) * P)
                        mm = pe.matmul(turned[:, at], g_k[:, at], g_q[:, at], start=True, stop=True)
                    mm.then_inc(gla_diag, 1)
                for l in range(LEVELS):
                    if slot == G_LEVEL[l] + 1:
                        n = LEVELS * c + l
                        pe.wait_ge(gla_put, 8 * c + l if l >= 2 else 8 * c)
                        pe.wait_ge(gla_kcopy, 2 * c)
                        pe.wait_ge(gla_ql, n + 1)
                        pe.wait_ge(gla_kl, n + 1)
                        for t in range(NT):
                            mm = pe.matmul(banks[6 + l % 2][:, t * HEAD:(t + 1) * HEAD],
                                           k_level[:, l % 2, t * P:(t + 1) * P],
                                           q_level[:, l % 2, t * HEAD:(t + 1) * HEAD], start=True, stop=True)
                        mm.then_inc(gla_lv, 1)
                if slot == G_TURN_V:
                    pe.wait_ge(gla_v_in, 16 * (c + 1))
                    pe.wait_ge(gla_sum, c + 1)
                    pe.wait_ge(gla_put, 8 * c + 1)
                    for i in range(4):
                        for t in (2 * i, 2 * i + 1):
                            for h in range(2):
                                o = (t % 2) * C_DV + h * C_DK
                                mm = pe.transpose(banks[2 + i][:, o:o + C_DK], g_v[:, h, t * P:(t + 1) * P],
                                                  ident[0:C_DK, 0:C_DK])
                        mm.then_inc(gla_vt, 1)
                if slot == G_TURN_K:
                    pe.wait_ge(gla_put, 8 * (c + 1))
                    pe.wait_ge(gla_ke, c + 1)
                    for i in range(2):
                        for t in range(4 * i, 4 * i + 4):
                            mm = pe.transpose(banks[6 + i][:, (t % 4) * C_DK:(t % 4 + 1) * C_DK],
                                              k_carry[:, t * P:(t + 1) * P], ident[0:C_DK, 0:C_DK])
                        mm.then_inc(gla_kt, 1)
                if slot == G_STATE:
                    pe.wait_ge(gla_vcopy, 4 * (c + 1))
                    pe.wait_ge(gla_kcopy, 2 * (c + 1))
                    for t in range(NT - 1):
                        mm = pe.matmul(banks[2 + t // 2][0:C_DK, (t % 2) * C_DV:(t % 2 + 1) * C_DV], k_rows[:, t, :],
                                       v_rows[:, t, :], start=True, stop=True)
                    mm.then_inc(gla_ds, 1)
                if slot == G_OUT:
                    pe.wait_ge(gla_state, (NT - 1) * (c + 1))
                    pe.wait_ge(gla_qe, c + 1)
                    for t in range(NT):
                        o, at = banks[2 + t // 2][:, (t % 2) * C_DV:(t % 2 + 1) * C_DV], slice(t * P, (t + 1) * P)
                        mm = pe.matmul(o, weights_t[:, at], v_rows[:, t, :], start=True, stop=(t == 0))
                        if t > 0:
                            mm = pe.matmul(o, q_carry[:, at], state[:, t, :], start=False, stop=True)
                        if t % 2 == 1:
                            mm.then_inc(gla_o, 1)
                if slot == G_FINAL:
                    pe.wait_ge(gla_ocopy, 4 * (c + 1))
                    pe.wait_ge(gla_norm, c + 1)
                    for h in range(2):
                        for t in range(NT):
                            mm = pe.transpose((scores, turned)[h][0:C_DK, t * P:(t + 1) * P],
                                              o_rows[:, t, h * C_DK:(h + 1) * C_DK], ident[:])
                        mm.then_inc(gla_ot, 1)

            def gla_head(c):
                for g in range(HEAD_GROUPS):
                    group(C_ALONE + HEAD_GROUPS * c + g, lambda slot: gla_steps(c, 8 * g + slot))

            gla_head(0)
            with pe.Fori(1, C_HEADS) as c:
                gla_head(c)

            def sum_squares(pair, m):
                if m > 0:
                    pe.wait_ge(ssq_logged, 4 * pair + m)
                else:
                    pe.wait_ge(vl_done, 2 * pair)
                pe.wait_ge(sq_lo_done, 4 * pair + m + 1)
                pe.matmul(spare[:], half_ones_r[:], sq_hi[:], start=True, stop=False)
                pe.matmul(spare[:], half_ones_r[:], sq_lo[:], start=False, stop=True).then_inc(ssq_done, 1)

            def values(pair, b):
                pe.wait_ge(v_in, 16 * (pair + 1))
                if b == 0:
                    pe.wait_ge(ssq_logged, 4 * (pair + 1))
                else:
                    pe.wait_ge(vl_done, 2 * pair + 1)
                for t in range(4 * b, 4 * b + 4):
                    mm = pe.transpose(spare[:, (t - 4 * b) * P:(t - 4 * b + 1) * P], sq_wide[:, t * P:(t + 1) * P], ident[:])
                mm.then_inc(v_turned, 1)

            def score(pair, j, kind):
                h, i = j // NT, j % NT
                n = (i + 1) * P
                if i == 0:
                    pe.wait_ge(ql_done, 2 * pair + h + 1)
                    pe.wait_ge(kl_done, 2 * pair + h + 1)
                    pe.wait_ge(k_other_done, 2 * pair + h + 1)
                pe.wait_ge(masked, ITEMS * pair + j)
                q, own = q_st[:, h, i * P:(i + 1) * P], slice(h * HEAD, (h + 1) * HEAD)
                for c0 in range(0, n, HALF):
                    c1 = min(c0 + HALF, n)
                    pe.matmul(scores[:, c0:c1], q, k_hi[:, h, c0:c1], start=True, stop=False)
                    if kind == 1 and c1 == n:
                        pe.matmul(scores[:, i * P:n], ident_r[:], causal_r[:], start=False, stop=False)
                    mm = pe.matmul(scores[:, c0:c1], q_st[own, h, i * P:(i + 1) * P], k_lo[own, c0:c1], start=False,
                                   stop=True)
                mm.then_inc(s_done, 1)

            def turn(pair, j):
                it = ITEMS * pair + j
                pe.wait_ge(vl_done, 2 * (pair + 1))
                pe.wait_ge(ptl_done, it)
                pe.wait_ge(prob_done, it + 1)
                for t in range(j % NT + 1):
                    at = slice(t * P, (t + 1) * P)
                    mm = pe.transpose(turned[:, at], prob[:, j % 2, at], ident[:])
                mm.then_inc(t_done, 1)

            def product(pair, j):
                h, i = j // NT, j % NT
                if j % 4 == 0:
                    pe.wait_ge(o_summed, 4 * pair + j // 4)
                pe.wait_ge(ptl_done, ITEMS * pair + j + 1)
                o = pv[:, (j % 4) * P:(j % 4 + 1) * P]
                for t in range(i + 1):
                    at = slice(t * P, (t + 1) * P)
                    pe.matmul(o, v_st[:, h, t, :], pt_hi[:, at], start=(t == 0), stop=False)
                    mm = pe.matmul(o, v_st[:, h, t, :], pt_lo[:, at], start=False, stop=(t == i))
                mm.then_inc(pv_done, 1)

            def steps_at(pair, kind, slot, has_next):
                for name, j in steps_of(slot):
                    if name == "values":
                        values(pair, j)
                    elif name == "product":
                        product(pair, j)
                    elif name == "turn":
                        turn(pair, j)
                    elif name == "score":
                        score(pair, j, kind)
                    elif name == "sum" and has_next:
                        sum_squares(pair + 1, j)

            def pair_body(pair, kind, s0):
                for slot in range(SLOTS + 1):
                    steps_at(pair, kind, slot, s0 is not None)
                    if slot < SLOTS and s0 is not None:
                        half_quarter(s0 + slot // 8, slot % 8 // 2, slot % 2)

            for m in range(4):
                sum_squares(0, m)
            pair_body(0, 0, S_LOOP_A)
            with pe.Fori(1, A_PAIRS - 1) as p:
                pair_body(p, 0, S_LOOP_A + 4 * p)
            pair_body(A_PAIRS - 1, 0, S_B0)
            with pe.Fori(0, B_PAIRS - 1) as p:
                pair_body(A_PAIRS + p, 1, S_LOOP_B + 4 * p)
            pair_body(A_PAIRS + B_PAIRS - 1, 1, None)

            def out_quarter(cg, kk):
                k = OUT_ORDER[kk]
                pe.wait_ge(lo_done, Q_OUT + 16 * cg + kk + 1)
                if isinstance(cg, int) and cg == 0:
                    pe.wait_ge(mix_lo, kk + 1)
                for t in range(NT):
                    if kk == 0 and not (isinstance(cg, int) and cg == 0):
                        pe.wait_ge(out_summed, NT * (cg - 1) + t + 1)
                    hi, lo = (a[:, k, t * P:(t + 1) * P] for a in (act_hi, act_lo))
                    pe.matmul(banks[t], hi, w_hi[:, kk % 2, :], start=(kk == 0), stop=False)
                    pe.matmul(banks[t], hi, w_lo[:, kk % 2, :], start=False, stop=False)
                    mm = pe.matmul(banks[t], lo, w_hi[:, kk % 2, :], start=False, stop=(kk == KT - 1))
                    if kk == KT - 1:
                        mm.then_inc(out_ready, 1)
                if kk < KT - 1:
                    mm.then_inc(quarter_done, 1)

            pe.wait_ge(o_summed, 4 * (A_PAIRS + B_PAIRS))
            pe.wait_ge(evac_done, 2 * GROUPS)
            for kk in range(KT):
                out_quarter(0, kk)
            with pe.Fori(1, OUT_CG) as cg:
                for kk in range(KT):
                    out_quarter(cg, kk)


_INS = ["x", "norm_g", "w_in", "a_q_gain", "a_k_gain", "b_q_gain", "b_k_gain", "fox_bias", "gla_gate_up",
        "gla_gate_bias", "gla_out_gain", "w_out"]


def kernel(**inputs):
    import numpy as _np
    import concourse.bacc as _bacc
    from concourse import mybir as _mybir
    from concourse.bass_utils import run_bass_kernel_spmd as _run

    nc = _bacc.Bacc("TRN2", target_bir_lowering=False, num_devices=1, dynamic_dma_scratch_size=1024)
    arrays, args = {}, []
    for name in _INS:
        a = _np.ascontiguousarray(inputs[name])
        arrays[f"in_{name}_dram"] = a
        args.append(nc.dram_tensor(f"in_{name}_dram", a.shape, _mybir.dt.from_np(a.dtype), kind="ExternalInput").ap())
    args.append(nc.dram_tensor("out_0_dram", (1, SEQ, D_MODEL), _mybir.dt.float32, kind="ExternalOutput").ap())
    build(nc, *args)
    r = _run(nc, [arrays], core_ids=[0])
    return r.results[0]["out_0_dram"]
```

```python
import concourse.bass as bass
from concourse import mybir
from contextlib import ExitStack

P = 128
SEQ = 1024
D_MODEL = 2048
KT = D_MODEL // P
NT = SEQ // P
HALF = 512
HEAD = 64
A_WIDTH = 768
B_WIDTH = 512
B_HEADS = B_WIDTH // HEAD
C_HEADS = 4
C_DV = 192
C_DK = 96
C_K = C_HEADS * C_DK
C_V = C_HEADS * C_DV
RANK = 16
A_PAIRS = A_WIDTH // P
B_PAIRS = B_WIDTH // P
COL_B = 4 * A_WIDTH
COL_BF = COL_B + 4 * B_WIDTH
COL_CQ = COL_BF + B_HEADS
COL_CK = COL_CQ + C_K
COL_CV = COL_CK + C_K
COL_CZ = COL_CV + C_V
COL_CR = COL_CZ + C_V
IN_WIDTH = COL_CR + RANK
SMALL = B_HEADS + RANK
C_FIRST = 2 * C_K // P + 2
C_ALONE = C_FIRST + 1
HEAD_GROUPS = 3
PAIR_GROUPS = 4
ITEMS = 2 * NT
LEVELS = 7
S_FIRST_Z = C_ALONE + HEAD_GROUPS * C_HEADS
S_LOOP_A = S_FIRST_Z + 1
S_PAIRS = S_LOOP_A - PAIR_GROUPS
S_B0 = S_LOOP_A + PAIR_GROUPS * (A_PAIRS - 1)
S_LOOP_B = S_B0 + PAIR_GROUPS
GROUPS = S_LOOP_B + PAIR_GROUPS * (B_PAIRS - 1)
Q_OUT = 4 * GROUPS
OUT_CG = D_MODEL // HALF
EPS = 1e-6
FAR = 1e30
LOWEST = -80.0
LN_EXP_SET = 6
LN2, LN3 = 0.6931471805599453, 1.0986122886681098

F32 = mybir.dt.float32
F32R = mybir.dt.float32r
I32 = mybir.dt.int32
ALU = mybir.AluOpType
ACT = mybir.ActivationFunctionType

G_GATE, G_TURN_V, G_CARRY, G_TURN_K, G_STATE, G_Z, G_OUT, G_NORM, G_FINAL = 4, 12, 14, 17, 18, 19, 20, 21, 23
G_LEVEL = [7 + l for l in range(LEVELS)]
SLOTS = 8 * PAIR_GROUPS
SLOT_SCORE = [1, 3, 4, 6, 8, 10, 11, 13, 16, 18, 19, 21, 23, 25, 27, 28]
SLOT_SCALE = [s + 1 for s in SLOT_SCORE]
SLOT_TURN = [s + 2 for s in SLOT_SCORE]
SLOT_PRODUCT = [min(s + 2, after) for s, after in zip(SLOT_TURN, SLOT_TURN[1:] + [SLOTS])]
SLOT_VALUES, SLOT_STACK1, SLOT_BOUND, SLOT_GATE, SLOT_SILU = (0, 1), 2, 4, 5, 7
SLOT_SQUARE = (14, 16, 20, 22)
SLOT_ROOT = (18, 24)
SLOT_STACK0 = 26
FIRST_SQUARE, FIRST_ROOT, FIRST_STACK0 = (1, 2, 4, 5), (3, 6), 7
ROUNDS = ((0, 1, 2), (3, 4, 5), (6, 7))
EARLY = len(ROUNDS) * (KT - 1)
EARLY_SLOT = [6 + (n * 4) // 5 if n < KT - 1 else 18 + (n - KT + 1) // 2 for n in range(EARLY)]
MIX_SLOT = [5 + (kk * 4) // 5 for kk in range(KT - 1)]
SMALL_AT = {5: range(0, 5), 6: range(5, 10), 7: range(10, KT)}
OUT_ORDER = [k for k in range(KT) if k != A_PAIRS + B_PAIRS - 1] + [A_PAIRS + B_PAIRS - 1]


def steps_of(slot):
    out = [("values", b) for b in range(2) if SLOT_VALUES[b] == slot]
    out += [("product", j) for j in range(ITEMS) if SLOT_PRODUCT[j] == slot]
    out += [("turn", j) for j in range(ITEMS) if SLOT_TURN[j] == slot]
    out += [("scale", j) for j in range(ITEMS) if SLOT_SCALE[j] == slot]
    out += [("score", j) for j in range(ITEMS) if SLOT_SCORE[j] == slot]
    out += [("stack1", 0)] * (slot == SLOT_STACK1) + [("bound", 0)] * (slot == SLOT_BOUND)
    out += [("gate", 0)] * (slot == SLOT_GATE) + [("silu", 0)] * (slot == SLOT_SILU)
    out += [("sum", m) for m in range(4) if SLOT_SQUARE[m] + 1 == slot]
    out += [("root", i) for i in range(2) if SLOT_ROOT[i] == slot]
    out += [("square", m) for m in range(4) if SLOT_SQUARE[m] == slot]
    out += [("stack0", 0)] * (slot == SLOT_STACK0)
    return out


def head_columns(c):
    if isinstance(c, int):
        return COL_CV + 2 * P, COL_CZ + P, COL_CZ + 2 * P
    return COL_CV + (2 + c) * P, COL_CZ + (2 + c) * P, (c - 1) * A_WIDTH


def first_steps_of(slot):
    out = [("sum", m) for m in range(4) if FIRST_SQUARE[m] + 1 == slot]
    out += [("root", i) for i in range(2) if FIRST_ROOT[i] == slot]
    out += [("square", m) for m in range(4) if FIRST_SQUARE[m] == slot]
    out += [("stack0", 0)] * (slot == FIRST_STACK0)
    return out


def early_at(slot):
    return [n for n in range(EARLY) if EARLY_SLOT[n] == slot]


def first_pair(pair):
    return isinstance(pair, int) and pair == 0


def blocks(ap, b):
    return ap.rearrange("p (n u r) -> p n u r", u=2, r=b)


def build(nc, x, norm_g, w_in, a_q_gain, a_k_gain, b_q_gain, b_k_gain, fox_bias,
          gla_gate_up, gla_gate_bias, gla_out_gain, w_out, out):
    x_rows, out_rows = x[0], out[0]
    w_in, w_out = w_in[0], w_out[0]
    w_in_k = w_in.rearrange("(k p) c -> p k c", p=P)
    w_out_k = w_out.rearrange("(k p) c -> p k c", p=P)
    proj = nc.dram_tensor("proj_scratch", (IN_WIDTH, SEQ), F32, kind="Internal").ap()
    mixed = nc.dram_tensor("mixed_scratch", (D_MODEL, SEQ), F32, kind="Internal").ap()
    partial = nc.dram_tensor("partial_scratch", (SEQ, HALF), F32, kind="Internal").ap()
    decay = nc.dram_tensor("decay_scratch", (B_HEADS, SEQ), F32, kind="Internal").ap()

    with ExitStack() as ctx:
        def sb(name, shape, dt=F32, scope=ctx):
            return scope.enter_context(nc.sbuf_tensor(name, shape, dt))

        def sem(name):
            return ctx.enter_context(nc.semaphore(name))

        bank = [ctx.enter_context(nc.psum_tensor(f"acc{i}", [P, HALF], F32)) for i in range(2)]
        scores = ctx.enter_context(nc.psum_tensor("scores", [P, SEQ], F32))
        turned = ctx.enter_context(nc.psum_tensor("turned", [P, SEQ], F32))
        pv = ctx.enter_context(nc.psum_tensor("pv", [P, HALF], F32))
        side = ctx.enter_context(nc.psum_tensor("side", [P, HALF], F32))
        early_banks = [bank[0][:], bank[1][:], side[:]]
        turn_banks = [bank[0][:], bank[1][:], turned[:, 0:HALF], turned[:, HALF:], pv[:], side[:]]
        banks = [bank[0][:], bank[1][:], scores[:, 0:HALF], scores[:, HALF:], turned[:, 0:HALF], turned[:, HALF:],
                 pv[:], side[:]]

        act_hi = sb("act_hi", [P, KT, SEQ], F32R)
        act_lo = sb("act_lo", [P, KT, SEQ], F32R)
        w_raw = sb("w_raw", [P, 2, HALF])
        w_hi = sb("w_hi", [P, 2, HALF], F32R)
        w_lo = sb("w_lo", [P, 2, HALF], F32R)
        stage = sb("stage", [P, 2, HALF])
        ident = sb("ident", [P, P])
        ident_r = sb("ident_r", [P, P], F32R)
        half_ones_r = sb("half_ones_r", [P, P], F32R)
        causal_r = sb("causal_r", [P, P], F32R)
        logit_bias = sb("logit_bias", [P, 2, SEQ])
        eps_col = sb("eps_col", [P, 1])
        gains = sb("gains", [P, 4])
        out_gain = sb("out_gain", [C_DK, 2])
        fox_col = sb("fox_col", [B_HEADS, 1])
        neg_max = sb("neg_max", [P, ITEMS])
        denom = sb("denom", [P, ITEMS])
        inv_denom = sb("inv_denom", [P, ITEMS])

        first = ExitStack()
        x_tile = sb("x_tile", [P, 2, D_MODEL], scope=first)
        g_wide = sb("g_wide", [P, D_MODEL], scope=first)
        junk = sb("junk", [P, D_MODEL], scope=first)
        x_ssq = sb("x_ssq", [P, NT], scope=first)
        x_log = sb("x_log", [P, NT], scope=first)
        x_rstd = sb("x_rstd", [P, NT], scope=first)
        dist_i = sb("dist_i", [P, SEQ], I32, scope=first)
        mod_i = sb("mod_i", [P, SEQ], I32, scope=first)
        dist = sb("dist", [P, SEQ], scope=first)
        count = sb("count", [P, SEQ], scope=first)
        term = sb("term", [P, SEQ], scope=first)
        causal = sb("causal", [P, P], scope=first)
        half_ones = sb("half_ones", [P, P], scope=first)
        ws_raw = sb("ws_raw", [P, KT, SMALL], scope=first)
        ws_hi = sb("ws_hi", [P, KT, SMALL], F32R, scope=first)
        ws_lo = sb("ws_lo", [P, KT, SMALL], F32R, scope=first)
        small = sb("small", [SMALL, SEQ], scope=first)
        lf_abs, lf_min = junk[0:B_HEADS, 0:SEQ], junk[0:B_HEADS, SEQ:]
        c_sum = sb("c_sum", [B_HEADS, SEQ], scope=first)
        first.close()

        gla = ExitStack()
        level_mask = sb("level_mask", [P, LEVELS, HEAD], scope=gla)
        gate_up = sb("gate_up", [RANK, C_DK], scope=gla)
        gate_bias = sb("gate_bias", [C_DK, 1], scope=gla)
        g_qk = sb("g_qk", [P, 2, SEQ], scope=gla)
        g_v = sb("g_v", [C_DK, 2, SEQ], scope=gla)
        g_z = sb("g_z", [C_DK, 2, SEQ], scope=gla)
        g_b = sb("g_b", [C_DK, SEQ], scope=gla)
        g_t = sb("g_t", [C_DK, 2, SEQ], scope=gla)
        q_level = sb("q_level", [C_DK, 2, HALF], scope=gla)
        k_level = sb("k_level", [C_DK, 2, SEQ], scope=gla)
        v_rows = sb("v_rows", [P, NT, C_DV], scope=gla)
        k_rows = sb("k_rows", [P, NT, C_DK], scope=gla)
        state = sb("state", [C_DK, NT, C_DV], scope=gla)
        o_ssq = sb("o_ssq", [P, NT], scope=gla)
        o_rstd = sb("o_rstd", [P, NT], scope=gla)
        o_junk = sb("o_junk", [P, 2, C_DV], scope=gla)
        gla.close()
        weights_t = logit_bias[:, 0, :]
        rank_rows = v_rows[:, :, :].rearrange("p t v -> p (t v)")[0:RANK, 0:SEQ]
        g_q, g_k = g_qk[0:C_DK, 0, :], g_qk[0:C_DK, 1, :]
        o_rows = g_qk[:, :, :].rearrange("p a b -> p (a b)")[:, 0:NT * C_DV].rearrange("p (t v) -> p t v", v=C_DV)
        q_carry, k_carry = g_v[:, 0, :], g_v[:, 1, :]

        pairs = ExitStack()
        raw = sb("raw", [P, 2, SEQ], scope=pairs)
        sq = sb("sq", [P, 2, HALF], scope=pairs)
        sq_hi = sb("sq_hi", [P, HALF], F32R, scope=pairs)
        sq_lo = sb("sq_lo", [P, HALF], F32R, scope=pairs)
        vz = sb("vz", [P, SEQ], scope=pairs)
        q_st = sb("q_st", [P, 2, SEQ], F32R, scope=pairs)
        k_hi = sb("k_hi", [P, 2, SEQ], F32R, scope=pairs)
        k_lo = sb("k_lo", [P, SEQ], F32R, scope=pairs)
        v_st = sb("v_st", [P, 2, NT, P], F32R, scope=pairs)
        prob = sb("prob", [P, 2, SEQ], scope=pairs)
        pt_hi = sb("pt_hi", [P, SEQ], F32R, scope=pairs)
        pt_lo = sb("pt_lo", [P, SEQ], F32R, scope=pairs)
        o_part = sb("o_part", [P, HALF], scope=pairs)
        pairs.close()
        sq_wide = sq[:, :, :].rearrange("p a b -> p (a b)")

        last = ExitStack()
        _held = sb("held", [P, 2, SEQ], scope=last)
        res = sb("res", [P, NT, HALF], scope=last)
        res_first = sb("res_first", [P, NT, HALF], scope=last)
        last.close()

        def early_stage(t):
            return (stage, sq)[t // 2 % 2][:, t % 2, :]


        consts, levels_ready, eps_ready, gains_in, small_in, g_in, rounded_consts = (
            sem(n) for n in "consts levels_ready eps_ready gains_in small_in g_in rounded_consts".split())
        x_squared, x_logged, x_rooted, x_normed, x_turned, x_hi_done, x_lo_done = (
            sem(n) for n in "x_squared x_logged x_rooted x_normed x_turned x_hi_done x_lo_done".split())
        dist_chain, ws_hi_done, ws_lo_done, small_done, small_out, small_saved, lf_step, c_done = (
            sem(n) for n in "dist_chain ws_hi_done ws_lo_done small_done small_out small_saved lf_step c_done".split())
        c_saved = sem("c_saved")
        hi_done, lo_done, quarter_done, half_done, evac_done = (
            sem(n) for n in "hi_done lo_done quarter_done half_done evac_done".split())
        q_in, k_in, v_in, z_in, sq_done, sq_lo_done, ssq_done = (
            sem(n) for n in "q_in k_in v_in z_in sq_done sq_lo_done ssq_done ".split())
        normed, qh_done, ql_done, kh_done, k_other_done, kl_done, v_turned, vh_done = (
            sem(n) for n in "normed qh_done ql_done kh_done k_other_done kl_done v_turned vh_done".split())
        vl_done, z_bounded, gate_chain, sigmoid_done, silu_done, ssq_logged, root_done = (
            sem(n) for n in "vl_done z_bounded gate_chain sigmoid_done silu_done ssq_logged root_done".split())
        s_done, masked, exp_done, recip_done, prob_done, t_done, pth_done, ptl_done = (
            sem(n) for n in "s_done masked exp_done recip_done prob_done t_done pth_done ptl_done".split())
        pv_done, o_moved, o_summed, o_done, mixed_saved = (
            sem(n) for n in "pv_done o_moved o_summed o_done mixed_saved".split())
        gla_rank_in, gla_up_in, gla_bias_in, gla_q_in, gla_k_in, gla_v_in, gla_z_in, gla_saved = (
            sem(n) for n in "gla_rank_in gla_up_in gla_bias_in gla_q_in gla_k_in gla_v_in gla_z_in gla_saved".split())
        gla_gate, gla_sum, gla_abs, gla_exp, gla_log, gla_min, gla_a, gla_scan = (
            sem(n) for n in "gla_gate gla_sum gla_abs gla_exp gla_log gla_min gla_a gla_scan".split())
        gla_scaled = sem("gla_scaled")
        gla_diag, gla_zero, gla_diff, gla_decay, gla_ql, gla_kl, gla_lv, gla_put = (
            sem(n) for n in "gla_diag gla_zero gla_diff gla_decay gla_ql gla_kl gla_lv gla_put".split())
        gla_vt, gla_vcopy, gla_eb, gla_qe, gla_ldiff, gla_le, gla_ke, gla_kt = (
            sem(n) for n in "gla_vt gla_vcopy gla_eb gla_qe gla_ldiff gla_le gla_ke gla_kt".split())
        gla_kcopy, gla_ds, gla_state = (
            sem(n) for n in "gla_kcopy gla_ds gla_state".split())
        gla_o, gla_ocopy, gla_osq, gla_ln, gla_rstd, gla_norm, gla_ot, gla_ez = (
            sem(n) for n in "gla_o gla_ocopy gla_osq gla_ln gla_rstd gla_norm gla_ot gla_ez".split())
        gla_zb, gla_sigmoid, gla_silu, gla_out = (
            sem(n) for n in "gla_zb gla_sigmoid gla_silu gla_out".split())
        mix_hi, mix_lo, out_ready, out_summed, partial_ready, partial_summed = (
            sem(n) for n in "mix_hi mix_lo out_ready out_summed partial_ready partial_summed".split())
        bias_in = [sem("bias_landed0"), sem("bias_landed1")]
        w_in_sem = [sem("w_landed0"), sem("w_landed1")]
        x_in = [sem("x_landed0"), sem("x_landed1")]
        proj_saved = [sem("proj_saved0"), sem("proj_saved1")]
        mix_in = [sem("mix_landed0"), sem("mix_landed1")]
        res_in = [sem(f"res_landed{t}") for t in range(NT)]
        out_saved = [sem(f"out_saved{t}") for t in range(NT)]

        block = ctx.enter_context(nc.Block())

        @block.sync
        def _(sp):
            def load_quarter(s, kq, col):
                if not (isinstance(s, int) and s == 0 and kq < 2):
                    sp.wait_ge(lo_done, 4 * s + kq - 1)
                sp.dma_start(w_raw[:, kq % 2, :].rearrange("p (k c) -> p k c", k=4),
                             w_in_k[:, 4 * kq:4 * kq + 4, bass.ds(col, P)]).then_inc(w_in_sem[kq % 2], 16)

            def load_rows(dst, row, n, name):
                sp.dma_start(dst, proj[bass.ds(row, n), :]).then_inc(name, 16)

            def saved(s):
                for th in range(2):
                    sp.wait_ge(proj_saved[th], 16 * (s + 1))

            for t in range(2):
                sp.dma_start(x_tile[:, t, :], x_rows[t * P:(t + 1) * P, :]).then_inc(x_in[t], 16)
                if t == 0:
                    sp.dma_start(g_wide[:], norm_g[0:1, :].broadcast_to([P, D_MODEL])).then_inc(g_in, 16)
            for n, g in enumerate((a_q_gain, a_k_gain, b_q_gain, b_k_gain)):
                for h in range(2):
                    sp.dma_start(gains[h * HEAD:(h + 1) * HEAD, n:n + 1], g.rearrange("a d -> d a"))\
                        .then_inc(gains_in, 16)
            for h in range(2):
                sp.dma_start(out_gain[:, h:h + 1], gla_out_gain[0:1, h * C_DK:(h + 1) * C_DK].rearrange("a d -> d a"))\
                    .then_inc(gains_in, 16)
            sp.dma_start(fox_col[:], fox_bias.rearrange("a d -> d a")).then_inc(gains_in, 16)
            sp.dma_start(ws_raw[:, :, 0:B_HEADS], w_in_k[:, :, COL_BF:COL_BF + B_HEADS]).then_inc(small_in, 16)
            sp.dma_start(ws_raw[:, :, B_HEADS:SMALL], w_in_k[:, :, COL_CR:COL_CR + RANK]).then_inc(small_in, 16)
            load_quarter(0, 0, COL_CQ)
            load_quarter(0, 1, COL_CQ)
            for t in range(2, NT):
                sp.wait_ge(x_turned, 4 * (t - 1))
                sp.dma_start(x_tile[:, t % 2, :], x_rows[t * P:(t + 1) * P, :]).then_inc(x_in[t % 2], 16)
            sp.wait_ge(small_out, 1)
            sp.dma_start(proj[COL_CR:COL_CR + RANK, :], small[B_HEADS:SMALL, :]).then_inc(small_saved, 16)
            load_quarter(0, 2, COL_CQ)
            load_quarter(0, 3, COL_CQ)
            with sp.Fori(1, C_FIRST) as s:
                for kq in range(4):
                    load_quarter(s, kq, COL_CQ + s * P)
            for g in range(C_ALONE - C_FIRST):
                for kq in range(4):
                    load_quarter(C_FIRST + g, kq, COL_CZ + g * P)

            def store_head(c):
                sp.wait_ge(gla_out, 2 * (c + 1))
                sp.dma_start(mixed[bass.ds(A_WIDTH + B_WIDTH + c * C_DV, C_DV), :].rearrange("(h p) t -> p h t", p=C_DK),
                             g_z[:, :, :]).then_inc(gla_saved, 16)

            def gla_loads(c):
                s = C_ALONE + HEAD_GROUPS * c
                col = head_columns(c)
                for kq in range(2):
                    load_quarter(s, kq, col[0])
                if isinstance(c, int):
                    sp.wait_ge(c_done, 1)
                    sp.wait_ge(small_saved, 16)
                    sp.wait_ge(c_saved, 16)
                    saved(C_ALONE - 1)
                else:
                    store_head(c - 1)
                    sp.wait_ge(gla_saved, 16 * c)
                load_rows(rank_rows, COL_CR, RANK, gla_rank_in)
                sp.dma_start(gate_up[:], gla_gate_up[0][:, bass.ds(c * C_DK, C_DK)]).then_inc(gla_up_in, 16)
                sp.dma_start(gate_bias[:], gla_gate_bias[0:1, bass.ds(c * C_DK, C_DK)].rearrange("a d -> d a"))\
                    .then_inc(gla_bias_in, 16)
                load_rows(g_q, COL_CQ + c * C_DK, C_DK, gla_q_in)
                load_rows(g_k, COL_CK + c * C_DK, C_DK, gla_k_in)
                for kq in range(2, 4):
                    load_quarter(s, kq, col[0])
                for kq in range(3):
                    load_quarter(s + 1, kq, col[1])
                saved(s)
                sp.dma_start(g_v[:, :, :], proj[bass.ds(COL_CV + c * C_DV, C_DV), :].rearrange("(h p) t -> p h t", p=C_DK))\
                    .then_inc(gla_v_in, 16)
                load_quarter(s + 1, 3, col[1])
                for kq in range(3):
                    load_quarter(s + 2, kq, col[2])
                saved(s + 1)
                sp.dma_start(g_z[:, :, :], proj[bass.ds(COL_CZ + c * C_DV, C_DV), :].rearrange("(h p) t -> p h t", p=C_DK))\
                    .then_inc(gla_z_in, 16)
                load_quarter(s + 2, 3, col[2])

            gla_loads(0)
            with sp.Fori(1, C_HEADS) as c:
                gla_loads(c)

            stores_counted = sp.alloc_register("stores_counted")
            sp.reg_mov(stores_counted, 0)

            def saved_of(pair, g):
                if first_pair(pair):
                    saved(S_FIRST_Z if g == 3 else S_FIRST_Z - 1)
                else:
                    saved(S_PAIRS + PAIR_GROUPS * pair + g)

            def load_q(pair, base, row):
                sp.wait_ge(qh_done, 2 * pair)
                sp.wait_ge(ql_done, 2 * pair)
                saved_of(pair, 0)
                load_rows(raw[:, 0, :], base + row, P, q_in)

            def load_k(pair, base, stride, row):
                sp.wait_ge(kh_done, 2 * pair)
                sp.wait_ge(k_other_done, 2 * pair)
                sp.wait_ge(kl_done, 2 * pair)
                saved_of(pair, 1)
                load_rows(raw[:, 1, :], base + stride + row, P, k_in)

            def load_values(pair, base, stride, row):
                saved_of(pair, 2)
                sp.wait_ge(normed, 2 * (pair + 1))
                load_rows(sq_wide, base + 2 * stride + row, P, v_in)
                if base == COL_B:
                    sp.wait_ge(masked, ITEMS * (pair - 1) + NT)
                    load_bias(pair, 0)

            def load_bias(pair, h):
                sp.dma_start(logit_bias[:, h, :], decay[bass.ds(2 * (pair - A_PAIRS) + h, 1), :]
                             .broadcast_to([P, SEQ])).then_inc(bias_in[h], 16)

            def store_pair(pair):
                sp.wait_ge(o_done, 4 * (pair + 1))
                sp.dma_start(mixed[bass.ds(pair * P, P), :], vz[:]).then_inc(mixed_saved, 16)

            def pair_loads(pair, base, stride, row, next_group, next_base, next_stride, next_row):
                def weights(g, kqs):
                    if next_group is not None:
                        for kq in kqs:
                            load_quarter(next_group + g, kq, next_base + g * next_stride + next_row)

                first = isinstance(pair, int) and pair == 0
                weights(0, range(2 if first else 0, 3))
                if not first:
                    store_pair(pair - 1)
                    sp.reg_add(stores_counted, stores_counted, 16)
                saved_of(pair, 3)
                if not first:
                    sp.wait_ge(mixed_saved, stores_counted)
                load_rows(vz[:], base + 3 * stride + row, P, z_in)
                if base == COL_B:
                    load_bias(pair, 1)
                weights(0, (3,))
                weights(1, range(3))
                if next_group is not None:
                    load_q(pair + 1, next_base, next_row)
                weights(1, (3,))
                weights(2, range(3))
                if next_group is not None:
                    load_k(pair + 1, next_base, next_stride, next_row)
                weights(2, (3,))
                weights(3, range(4))
                if next_group is not None:
                    load_values(pair + 1, next_base, next_stride, next_row)

            def load_out_rows(n, kk, col):
                sp.wait_ge(lo_done, Q_OUT + n - 1)
                slot = (EARLY + kk) % 2 if not isinstance(n, int) else n % 2
                sp.dma_start(w_raw[:, slot, :], w_out_k[:, OUT_ORDER[kk], bass.ds(col, HALF)])\
                    .then_inc(w_in_sem[slot], 16)

            def load_out_quarter(cg, kk):
                load_out_rows(EARLY + KT * (cg - 1) + kk, kk, cg * HALF)

            for kq in range(2):
                load_quarter(S_FIRST_Z, kq, 3 * A_WIDTH)
            store_head(C_HEADS - 1)
            load_q(0, 0, 0)
            sp.wait_ge(gla_saved, 16 * C_HEADS)
            load_k(0, 0, A_WIDTH, 0)
            for kq in range(2, 4):
                load_quarter(S_FIRST_Z, kq, 3 * A_WIDTH)
            for kq in range(2):
                load_quarter(S_LOOP_A, kq, P)
            load_values(0, 0, A_WIDTH, 0)
            pair_loads(0, 0, A_WIDTH, 0, S_LOOP_A, 0, A_WIDTH, P)
            with sp.Fori(1, A_PAIRS - 1) as p:
                pair_loads(p, 0, A_WIDTH, p * P, S_LOOP_A + 4 * p, 0, A_WIDTH, (p + 1) * P)
            pair_loads(A_PAIRS - 1, 0, A_WIDTH, (A_PAIRS - 1) * P, S_B0, COL_B, B_WIDTH, 0)
            with sp.Fori(0, B_PAIRS - 1) as p:
                pair_loads(A_PAIRS + p, COL_B, B_WIDTH, p * P, S_LOOP_B + 4 * p, COL_B, B_WIDTH, (p + 1) * P)
            for n in range(2):
                load_out_rows(n, n, 0)
            pair_loads(A_PAIRS + B_PAIRS - 1, COL_B, B_WIDTH, (B_PAIRS - 1) * P, None, 0, 0, 0)

            def load_mixed(kk):
                if kk >= 2:
                    sp.wait_ge(mix_lo, kk - 1)
                sp.dma_start(raw[:, kk % 2, :], mixed[OUT_ORDER[kk] * P:(OUT_ORDER[kk] + 1) * P, :])\
                    .then_inc(mix_in[kk % 2], 16)

            def load_early_residual(t):
                if t >= 4:
                    sp.wait_ge(out_saved[t - 4], 16)
                sp.dma_start(early_stage(t), x_rows[t * P:(t + 1) * P, 0:HALF]).then_inc(res_in[t], 16)

            def store_partial(t):
                sp.wait_ge(partial_summed, t + 1)
                sp.dma_start(partial[t * P:(t + 1) * P, :], early_stage(t)).then_inc(out_saved[t], 16)

            for split in (ql_done, qh_done, kh_done, k_other_done, kl_done):
                sp.wait_ge(split, 2 * (A_PAIRS + B_PAIRS))
            sp.wait_ge(mixed_saved, 16 * (A_PAIRS + B_PAIRS - 1))
            sp.wait_ge(gla_saved, 16 * C_HEADS)
            load_mixed(0)
            load_mixed(1)
            for n in range(2, EARLY):
                load_out_rows(n, n % (KT - 1), 0)
                if n < KT - 1:
                    load_mixed(n)
                if n == 4:
                    for th in range(2):
                        sp.wait_ge(proj_saved[th], 16 * GROUPS)
                    sp.wait_ge(silu_done, A_PAIRS + B_PAIRS)
                    for t in range(4):
                        load_early_residual(t)
                for r, tiles in enumerate(ROUNDS[:-1]):
                    if n == (KT - 1) * (r + 1) + 3:
                        for t in tiles:
                            store_partial(t)
                        for t in ROUNDS[r + 1]:
                            if t >= 4:
                                load_early_residual(t)

            def load_res(cg):
                for t in range(NT):
                    sp.wait_ge(out_saved[t], 16 * cg)
                    sp.dma_start(res[:, t, :], x_rows[t * P:(t + 1) * P, bass.ds(cg * HALF, HALF)])\
                        .then_inc(res_in[t], 16)

            def save_out(cg, t):
                only = isinstance(cg, int) and cg == OUT_CG
                col, src = (0, res_first) if only else (cg * HALF, res)
                sp.wait_ge(out_summed, NT * (cg - 1) + t + 1)
                sp.dma_start(out_rows[t * P:(t + 1) * P, bass.ds(col, HALF)], src[:, t, :]).then_inc(out_saved[t], 16)

            for kk in range(3):
                load_out_quarter(1, kk)
            for t in ROUNDS[-1]:
                store_partial(t)
            store_pair(A_PAIRS + B_PAIRS - 1)
            sp.wait_ge(mixed_saved, 16 * (A_PAIRS + B_PAIRS))
            load_mixed(KT - 1)
            for t in range(NT):
                sp.wait_ge(out_saved[t], 16)
            for kk in range(3, 6):
                load_out_quarter(1, kk)
            load_res(1)
            for kk in range(6, KT):
                load_out_quarter(1, kk)
            with sp.Fori(2, OUT_CG) as cg:
                for kk in range(2):
                    load_out_quarter(cg, kk)
                for t in range(NT):
                    save_out(cg - 1, t)
                for kk in range(2, 6):
                    load_out_quarter(cg, kk)
                load_res(cg)
                for kk in range(6, KT):
                    load_out_quarter(cg, kk)
            load_out_rows(EARLY + KT * (OUT_CG - 1), KT - 1, 0)
            for t in range(NT):
                sp.dma_start(res_first[:, t, :], partial[t * P:(t + 1) * P, :]).then_inc(res_in[t], 16)
            for t in range(NT):
                save_out(OUT_CG - 1, t)
            for t in range(NT):
                save_out(OUT_CG, t)
            for t in range(NT):
                sp.wait_ge(out_saved[t], 16 * (OUT_CG + 1))

        @block.gpsimd
        def _(pool):
            pool.memset(eps_col[:], EPS).then_inc(eps_ready, 1)
            pool.memset(ident[:], 0.0).then_inc(consts, 1)
            pool.memset(causal[:], 0.0).then_inc(consts, 1)
            pool.memset(half_ones[:], 0.0).then_inc(consts, 1)
            pool.wait_ge(consts, 3)
            pool.affine_select(out=ident[:], in_=ident[:], compare_op=ALU.not_equal, fill=1.0, base=0,
                                   pattern=[[-1, P]], channel_multiplier=1).then_inc(consts, 1)
            pool.affine_select(out=causal[:], in_=causal[:], compare_op=ALU.is_ge, fill=FAR, base=0,
                                   pattern=[[-1, P]], channel_multiplier=1).then_inc(consts, 1)
            pool.wait_ge(consts, 5)
            pool.memset(half_ones[0:HEAD, 0:HEAD], 1.0).then_inc(consts, 1)
            pool.wait_ge(consts, 6)
            pool.memset(half_ones[HEAD:P, HEAD:P], 1.0).then_inc(consts, 1)
            pool.wait_ge(consts, 7)
            pool.iota(dist_i[:], [[-1, SEQ]], base=(NT - 1) * P, channel_multiplier=1).then_inc(consts, 1)

            pool.wait_ge(c_done, 1)
            pool.wait_ge(small_saved, 16)
            pool.wait_ge(c_saved, 16)
            pool.memset(level_mask[:, :, :], 1.0).then_inc(levels_ready, 1)
            pool.wait_ge(levels_ready, 1)
            for l in range(LEVELS):
                b = 1 << l
                v = level_mask[:, l, :].rearrange("p (n r) -> p n r", r=b)
                pool.affine_select(out=v, in_=v, compare_op=ALU.is_ge, fill=0.0, base=0,
                                       pattern=[[-2 * b, HEAD // b], [0, b]], channel_multiplier=1)\
                                       .then_inc(levels_ready, 1)
            pool.wait_ge(levels_ready, 1 + LEVELS)
            for l in range(LEVELS):
                b = 1 << l
                v = level_mask[:, l, :].rearrange("p (n r) -> p n r", r=b)
                pool.affine_select(out=v, in_=v, compare_op=ALU.is_ge, fill=0.0, base=b - 1,
                                       pattern=[[2 * b, HEAD // b], [0, b]], channel_multiplier=-1)\
                                       .then_inc(levels_ready, 1)
            pool.memset(k_level[:, :, :], 0.0).then_inc(levels_ready, 1)
            pool.wait_ge(levels_ready, 2 + 2 * LEVELS)

            def gla_head(c):
                pool.wait_ge(gla_scaled, c + 1)
                pool.wait_ge(gla_k_in, 16 * (c + 1))
                for l in range(LEVELS):
                    b, n = 1 << l, LEVELS * c + l
                    pool.wait_ge(gla_lv, n - 1 if l >= 2 else LEVELS * c)
                    pool.wait_ge(gla_decay, n + 1)
                    pool.tensor_tensor(q_level[:, l % 2, :].rearrange("p (n r) -> p n r", r=b),
                                           blocks(g_q, b)[:, :, 1, :], blocks(g_t[:, l % 2, :], b)[:, :, 1, :],
                                           ALU.mult).then_inc(gla_ql, 1)
                    pool.tensor_tensor(blocks(k_level[:, l % 2, :], b)[:, :, 0, :], blocks(g_k, b)[:, :, 0, :],
                                           blocks(g_t[:, l % 2, :], b)[:, :, 0, :], ALU.mult).then_inc(gla_kl, 1)
                pool.wait_ge(gla_vt, 4 * (c + 1))
                pool.wait_ge(gla_eb, c + 1)
                pool.tensor_tensor(q_carry, g_q, g_t[:, 0, :], ALU.mult).then_inc(gla_qe, 1)
                pool.wait_ge(gla_le, c + 1)
                pool.tensor_tensor(k_carry, g_k, g_t[:, 1, :], ALU.mult).then_inc(gla_ke, 1)
                pool.wait_ge(gla_sigmoid, c + 1)
                pool.tensor_tensor(g_z[:, :, :], g_z[:, :, :], g_t[:, :, :], ALU.mult).then_inc(gla_silu, 1)

            gla_head(0)
            with pool.Fori(1, C_HEADS) as c:
                gla_head(c)

            def low_parts(pair, h):
                own, other = slice(h * HEAD, (h + 1) * HEAD), slice((1 - h) * HEAD, (2 - h) * HEAD)
                if not first_pair(pair):
                    pool.wait_ge(s_done, ITEMS * (pair - 1) + NT * (h + 1))
                pool.wait_ge(qh_done, 2 * pair + h + 1)
                pool.tensor_tensor(q_st[other, h, :], raw[own, 0, :], q_st[own, h, :].bitcast(F32),
                                   ALU.subtract).then_inc(ql_done, 1)
                pool.wait_ge(kh_done, 2 * pair + h + 1)
                pool.tensor_tensor(k_lo[own, :], raw[own, 1, :], k_hi[own, h, :].bitcast(F32),
                                   ALU.subtract).then_inc(kl_done, 1)

            for h in range(2):
                low_parts(0, h)
            with pool.Fori(1, A_PAIRS + B_PAIRS) as p:
                for h in range(2):
                    low_parts(p, h)

        @block.scalar
        def _(act):
            def split_hi(s, kq):
                slot = kq % 2
                if kq == 1 and not (isinstance(s, int) and s == 0):
                    act.wait_ge(half_done, 2 * s)
                if kq >= 2:
                    act.wait_ge(quarter_done, 3 * s + kq - 1)
                act.wait_ge(w_in_sem[slot], 16 * (2 * s + kq // 2 + 1))
                act.activation(w_hi[:, slot, :], w_raw[:, slot, :], ACT.Copy).then_inc(hi_done, 1)

            def split_hi_out(cg, kk):
                slot = (EARLY + kk) % 2
                if kk == 1:
                    if isinstance(cg, int) and cg == 1:
                        act.wait_ge(partial_ready, NT)
                    else:
                        act.wait_ge(out_ready, NT * (cg - 1))
                else:
                    act.wait_ge(quarter_done, 3 * GROUPS + EARLY - len(ROUNDS) + (KT - 1) * (cg - 1) + kk - 1 + (kk == 0))
                act.wait_ge(w_in_sem[slot], 16 * (2 * GROUPS + (KT // 2) * (cg - 1) + (EARLY + kk) // 2 + 1))
                act.activation(w_hi[:, slot, :], w_raw[:, slot, :], ACT.Copy).then_inc(hi_done, 1)

            def split_hi_early(n):
                r, kk = (n - 2) // (KT - 1), (n - 2) % (KT - 1)
                if n == 1:
                    act.wait_ge(half_done, 2 * GROUPS)
                elif kk == KT - 2:
                    act.wait_ge(partial_ready, ROUNDS[r][-1] + 1)
                else:
                    act.wait_ge(quarter_done, 3 * GROUPS + (KT - 2) * r + kk + 1)
                act.wait_ge(w_in_sem[n % 2], 16 * (2 * GROUPS + n // 2 + 1))
                act.activation(w_hi[:, n % 2, :], w_raw[:, n % 2, :], ACT.Copy).then_inc(hi_done, 1)

            def evac(s, th):
                act.wait_ge(half_done, 2 * s + th + 1)
                if not (isinstance(s, int) and s == 0):
                    act.wait_ge(proj_saved[th], 16 * s)
                act.activation(stage[:, th, :], bank[th][:], ACT.Copy).then_inc(evac_done, 1)

            def save(s, row):
                for th in range(2):
                    act.wait_ge(evac_done, 2 * s + th + 1)
                    act.dma_start(proj[bass.ds(row, P), th * HALF:(th + 1) * HALF], stage[:, th, :])\
                        .then_inc(proj_saved[th], 16)

            def group(s, row, steps):
                for slot in range(8):
                    if slot % 2 == 0:
                        split_hi(s, slot // 2 + 1)
                    if slot == 7:
                        evac(s, 0)
                    steps(slot)
                evac(s, 1)
                save(s, row)

            act.add_instruction(mybir.InstLoadActFuncSet(name=nc.get_next_instruction_name(), act_func_set_id=LN_EXP_SET))

            act.wait_ge(eps_ready, 1)
            for t in range(NT + 1):
                if t < NT:
                    act.wait_ge(x_in[t % 2], 16 * (t // 2 + 1))
                    act.activation(junk[:], x_tile[:, t % 2, :], ACT.Square, accum_out=x_ssq[:, t:t + 1])\
                        .then_inc(x_squared, 1)
                    act.wait_ge(x_squared, t + 1)
                    act.activation(x_log[:, t:t + 1], x_ssq[:, t:t + 1], ACT.Ln, scale=1.0 / D_MODEL,
                                   bias=eps_col[:]).then_inc(x_logged, 1)
                    act.wait_ge(x_logged, t + 1)
                    act.activation(x_rstd[:, t:t + 1], x_log[:, t:t + 1], ACT.Exp, scale=-0.5).then_inc(x_rooted, 1)
                if t >= 1:
                    for b in range(4):
                        n = 4 * (t - 1) + b
                        act.wait_ge(x_turned, n + 1)
                        act.activation(act_hi[:, 4 * b:4 * b + 4, (t - 1) * P:t * P],
                                       turn_banks[n % 6].rearrange("p (k t) -> p k t", k=4), ACT.Copy)\
                                           .then_inc(x_hi_done, 1)
                if t == 2:
                    act.wait_ge(small_in, 32)
                    act.activation(ws_hi[:, :, :], ws_raw[:, :, :], ACT.Copy).then_inc(ws_hi_done, 1)
            split_hi(0, 0)
            act.wait_ge(consts, 8)
            act.activation(ident_r[:], ident[:], ACT.Copy).then_inc(rounded_consts, 1)
            act.activation(causal_r[:], causal[:], ACT.Copy).then_inc(rounded_consts, 1)
            act.activation(half_ones_r[:], half_ones[:], ACT.Copy).then_inc(rounded_consts, 1)
            act.wait_ge(small_done, 1)
            act.activation(small[:], scores[0:SMALL, :], ACT.Copy).then_inc(small_out, 1)

            def forget(slot):
                if slot == 2:
                    act.wait_ge(lf_step, 1)
                    act.activation(lf_abs, lf_min, ACT.Abs).then_inc(lf_step, 1)
                    act.wait_ge(lf_step, 2)
                    act.activation(lf_abs, lf_abs, ACT.Exp, scale=-1.0).then_inc(lf_step, 1)
                    act.wait_ge(lf_step, 3)
                    act.activation(lf_abs, lf_abs, ACT.Ln, bias=1.0).then_inc(lf_step, 1)
                if slot == 6:
                    act.wait_ge(c_done, 1)
                    act.dma_start(decay[:, :], c_sum[:]).then_inc(c_saved, 16)

            group(0, COL_CQ, forget)
            with act.Fori(1, C_FIRST) as s:
                group(s, COL_CQ + s * P, lambda slot: None)
            for g in range(C_ALONE - C_FIRST):
                group(C_FIRST + g, COL_CZ + g * P, lambda slot: None)

            def gla_steps(c, slot):
                if slot == G_GATE:
                    act.wait_ge(gla_q_in, 16 * (c + 1))
                    act.mul(g_q, g_q, float(C_DK) ** -0.5).then_inc(gla_scaled, 1)
                    act.wait_ge(gla_sum, c + 1)
                    act.activation(g_t[:, 1, :], g_t[:, 0, :], ACT.Abs).then_inc(gla_abs, 1)
                    act.wait_ge(gla_abs, c + 1)
                    act.activation(g_t[:, 1, :], g_t[:, 1, :], ACT.Exp, scale=-1.0).then_inc(gla_exp, 1)
                    act.wait_ge(gla_exp, c + 1)
                    act.activation(g_t[:, 1, :], g_t[:, 1, :], ACT.Ln, bias=1.0).then_inc(gla_log, 1)
                for l in range(LEVELS):
                    if slot == G_LEVEL[l]:
                        act.wait_ge(gla_diff, 2 * (LEVELS * c + l) + 2)
                        act.activation(g_t[:, l % 2, :], g_t[:, l % 2, :], ACT.Exp).then_inc(gla_decay, 1)
                if slot == G_TURN_V:
                    for i in range(4):
                        act.wait_ge(gla_vt, 4 * c + i + 1)
                        act.activation(v_rows[:, 2 * i:2 * i + 2, :],
                                       banks[2 + i][:, 0:2 * C_DV].rearrange("p (t v) -> p t v", t=2), ACT.Copy)\
                            .then_inc(gla_vcopy, 1)
                if slot == G_CARRY:
                    act.wait_ge(gla_kl, LEVELS * (c + 1))
                    act.activation(g_t[:, 0, :], g_b[:], ACT.Exp).then_inc(gla_eb, 1)
                    act.wait_ge(gla_ldiff, c + 1)
                    act.activation(g_t[:, 1, :], g_t[:, 1, :], ACT.Exp).then_inc(gla_le, 1)
                if slot == G_TURN_K:
                    for i in range(2):
                        act.wait_ge(gla_kt, 2 * c + i + 1)
                        act.activation(k_rows[:, 4 * i:4 * i + 4, :],
                                       banks[6 + i][:, 0:4 * C_DK].rearrange("p (t d) -> p t d", t=4), ACT.Copy)\
                            .then_inc(gla_kcopy, 1)
                if slot == G_Z:
                    act.wait_ge(gla_zb, c + 1)
                    act.activation(g_t[:, :, :], g_t[:, :, :], ACT.Exp, scale=-1.0).then_inc(gla_ez, 1)
                    act.wait_ge(gla_ez, 2 * c + 1)
                    act.activation(g_t[:, :, :], g_t[:, :, :], ACT.Ln, bias=1.0).then_inc(gla_ez, 1)
                    act.wait_ge(gla_ez, 2 * c + 2)
                    act.activation(g_t[:, :, :], g_t[:, :, :], ACT.Exp, scale=-1.0).then_inc(gla_sigmoid, 1)
                if slot == G_OUT:
                    for i in range(4):
                        act.wait_ge(gla_o, 4 * c + i + 1)
                        act.activation(o_rows[:, 2 * i:2 * i + 2, :],
                                       banks[2 + i][:, 0:2 * C_DV].rearrange("p (t v) -> p t v", t=2), ACT.Copy)\
                            .then_inc(gla_ocopy, 1)
                        act.wait_ge(gla_ocopy, 4 * c + i + 1)
                        for t in (2 * i, 2 * i + 1):
                            act.wait_ge(gla_osq, NT * c + max(t - 1, 0))
                            act.activation(o_junk[:, t % 2, :], o_rows[:, t, :], ACT.Square,
                                           accum_out=o_ssq[:, t:t + 1]).then_inc(gla_osq, 1)
                    act.wait_ge(gla_osq, NT * (c + 1))
                    act.activation(o_rstd[:], o_ssq[:], ACT.Ln, scale=1.0 / C_DV, bias=eps_col[:]).then_inc(gla_ln, 1)
                    act.wait_ge(gla_ln, c + 1)
                    act.activation(o_rstd[:], o_rstd[:], ACT.Exp, scale=-0.5).then_inc(gla_rstd, 1)

            def gla_head(c):
                col = head_columns(c)
                for g in range(HEAD_GROUPS):
                    group(C_ALONE + HEAD_GROUPS * c + g, col[g], lambda slot: gla_steps(c, 8 * g + slot))

            gla_head(0)
            with act.Fori(1, C_HEADS) as c:
                gla_head(c)

            def square(pair, m):
                if m % 2 == 0:
                    act.wait_ge((q_in, k_in)[m // 2], 16 * (pair + 1))
                if m < 2:
                    act.wait_ge(silu_done, pair)
                else:
                    act.wait_ge(normed, 2 * pair + 1)
                if m > 0:
                    act.wait_ge(ssq_done, 4 * pair + m)
                src = raw[:, m // 2, (m % 2) * HALF:(m % 2 + 1) * HALF]
                act.activation(sq[:, m % 2, :], src, ACT.Square).then_inc(sq_done, 1)
                act.activation(sq_hi[:], src, ACT.Square).then_inc(sq_done, 1)

            def log_sum(pair, m):
                act.wait_ge(ssq_done, 4 * pair + m + 1)
                act.activation(sq[:, m % 2, :], side[:], ACT.Ln, scale=1.0 / HEAD, bias=eps_col[:])\
                    .then_inc(ssq_logged, 1)

            def root(pair, i):
                act.wait_ge(ssq_logged, 4 * pair + 2 * i + 2)
                act.activation(sq_wide, sq_wide, ACT.Exp, scale=-0.5).then_inc(root_done, 1)

            def stack(pair, h):
                own = slice(h * HEAD, (h + 1) * HEAD)
                if not first_pair(pair):
                    act.wait_ge(s_done, ITEMS * (pair - 1) + NT * (h + 1))
                act.wait_ge(normed, 2 * (pair + 1))
                act.activation(q_st[own, h, :], raw[own, 0, :], ACT.Copy).then_inc(qh_done, 1)
                act.activation(k_hi[own, h, :], raw[own, 1, :], ACT.Copy).then_inc(kh_done, 1)

            def values(pair, b):
                act.wait_ge(pv_done, ITEMS * pair)
                act.wait_ge(v_turned, 2 * pair + b + 1)
                act.activation(v_st[:, :, 4 * b:4 * b + 4, 0:HEAD],
                               side[:].rearrange("p (t h c) -> p h t c", t=4, h=2), ACT.Copy).then_inc(vh_done, 1)

            def gate(pair):
                act.wait_ge(z_bounded, pair + 1)
                act.activation(sq_wide, sq_wide, ACT.Exp, scale=-1.0).then_inc(gate_chain, 1)
                act.wait_ge(gate_chain, 2 * pair + 1)
                act.activation(sq_wide, sq_wide, ACT.Ln, bias=1.0).then_inc(gate_chain, 1)
                act.wait_ge(gate_chain, 2 * pair + 2)
                act.activation(sq_wide, sq_wide, ACT.Exp, scale=-1.0).then_inc(sigmoid_done, 1)

            def score(pair, j):
                n = (j % NT + 1) * P
                act.wait_ge(masked, ITEMS * pair + j + 1)
                act.activation(prob[:, j % 2, 0:n], prob[:, j % 2, 0:n], ACT.Exp, scale=-1.0, bias=neg_max[:, j:j + 1],
                                   accum_out=denom[:, j:j + 1]).then_inc(exp_done, 1)

            def turn(pair, j):
                n = (j % NT + 1) * P
                act.wait_ge(pv_done, ITEMS * pair + j)
                act.wait_ge(t_done, ITEMS * pair + j + 1)
                act.activation(pt_hi[:, 0:n], turned[:, 0:n], ACT.Copy).then_inc(pth_done, 1)

            def product(pair, j):
                if j % 4 == 3:
                    h, u = j // NT, j // 4
                    own, other = slice(h * HEAD, (h + 1) * HEAD), slice((1 - h) * HEAD, (2 - h) * HEAD)
                    act.wait_ge(o_done, 4 * pair + u)
                    act.wait_ge(pv_done, ITEMS * pair + j + 1)
                    act.activation(o_part[own, :], pv[other, :], ACT.Copy).then_inc(o_moved, 1)

            def steps_at(pair, slot, has_next=True):
                for name, j in steps_of(slot):
                    if name == "values":
                        values(pair, j)
                    elif name == "product":
                        product(pair, j)
                    elif name == "turn":
                        turn(pair, j)
                    elif name == "score":
                        score(pair, j)
                    elif name == "stack1":
                        stack(pair, 1)
                    elif name == "gate":
                        gate(pair)
                    elif name == "square" and has_next:
                        square(pair + 1, j)
                    elif name == "sum" and has_next:
                        log_sum(pair + 1, j)
                    elif name == "root" and has_next:
                        root(pair + 1, j)
                    elif name == "stack0" and has_next:
                        stack(pair + 1, 0)

            def first_steps(slot):
                for name, j in first_steps_of(slot):
                    if name == "sum":
                        log_sum(0, j)
                    elif name == "root":
                        root(0, j)
                    elif name == "square":
                        square(0, j)
                    elif name == "stack0":
                        stack(0, 0)

            group(S_FIRST_Z, 3 * A_WIDTH, first_steps)

            def pair_body(pair, s0, base, stride, row, projecting=True):
                for g in range(PAIR_GROUPS):
                    def steps(slot, g=g):
                        steps_at(pair, 8 * g + slot, projecting)
                    if projecting:
                        group(s0 + g, base + g * stride + row, steps)
                    else:
                        for slot in range(8):
                            last_pair_slot(8 * g + slot, lambda: steps(slot))
                if projecting:
                    steps_at(pair, SLOTS)
                else:
                    last_pair_slot(SLOTS, lambda: steps_at(pair, SLOTS))

            def last_pair_slot(slot, steps):
                ahead = [n + 1 for n in early_at(slot)]
                for n in ahead[:1]:
                    split_next(n)
                steps()
                for kk in range(KT - 1):
                    if MIX_SLOT[kk] == slot:
                        mix_hi_part(kk)
                for n in ahead[1:]:
                    split_next(n)

            def split_next(n):
                if n < EARLY:
                    split_hi_early(n)
                else:
                    split_hi_out(1, 0)

            def mix_hi_part(kk):
                act.wait_ge(mix_in[kk % 2], 16 * (kk // 2 + 1))
                act.wait_ge(half_done, 2 * GROUPS)
                act.activation(act_hi[:, OUT_ORDER[kk], :], raw[:, kk % 2, :], ACT.Copy).then_inc(mix_hi, 1)

            pair_body(0, S_LOOP_A, 0, A_WIDTH, P)
            with act.Fori(1, A_PAIRS - 1) as p:
                pair_body(p, S_LOOP_A + 4 * p, 0, A_WIDTH, (p + 1) * P)
            pair_body(A_PAIRS - 1, S_B0, COL_B, B_WIDTH, 0)
            with act.Fori(0, B_PAIRS - 1) as p:
                pair_body(A_PAIRS + p, S_LOOP_B + 4 * p, COL_B, B_WIDTH, (p + 1) * P)
            pair_body(A_PAIRS + B_PAIRS - 1, None, 0, 0, 0, projecting=False)

            for kk in range(KT):
                split_hi_out(*((1, kk + 1) if kk < KT - 1 else (2, 0)))
                if kk == 6:
                    mix_hi_part(KT - 1)
            with act.Fori(2, OUT_CG) as cg:
                for kk in range(KT):
                    split_hi_out(*((cg, kk + 1) if kk < KT - 1 else (cg + 1, 0)))

        @block.vector
        def _(dve):
            def split_lo(s, kq):
                slot = kq % 2
                dve.wait_ge(hi_done, 4 * s + kq + 1)
                dve.tensor_tensor(w_lo[:, slot, :], w_raw[:, slot, :], w_hi[:, slot, :].bitcast(F32), ALU.subtract)\
                    .then_inc(lo_done, 1)

            def group(s, steps):
                for slot in range(8):
                    if slot % 2 == 0:
                        split_lo(s, slot // 2 + 1)
                    steps(slot)

            for t in range(NT + 1):
                if t < NT:
                    dve.wait_ge(g_in, 16)
                    dve.wait_ge(x_rooted, t + 1)
                    dve.scalar_tensor_tensor(out=x_tile[:, t % 2, :], in0=x_tile[:, t % 2, :],
                                                 scalar=x_rstd[:, t:t + 1], in1=g_wide[:], op0=ALU.mult, op1=ALU.mult)\
                                                 .then_inc(x_normed, 1)
                if t >= 1:
                    for b in range(4):
                        n = 4 * (t - 1) + b
                        dve.wait_ge(x_hi_done, n + 1)
                        at = (slice(None), slice(4 * b, 4 * b + 4), slice((t - 1) * P, t * P))
                        dve.tensor_tensor(act_lo[at], turn_banks[n % 6].rearrange(
                            "p (k t) -> p k t", k=4), act_hi[at].bitcast(F32), ALU.subtract).then_inc(x_lo_done, 1)
                if t == 2:
                    dve.wait_ge(ws_hi_done, 1)
                    dve.tensor_tensor(ws_lo[:, :, :], ws_raw[:, :, :], ws_hi[:, :, :].bitcast(F32),
                                      ALU.subtract).then_inc(ws_lo_done, 1)
            split_lo(0, 0)

            step = [0]

            def link(ins):
                step[0] += 1
                ins.then_inc(dist_chain, 1)
                dve.wait_ge(dist_chain, step[0])

            dve.wait_ge(consts, 8)
            link(dve.tensor_copy(dist[:], dist_i[:]))
            link(dve.tensor_scalar(mod_i[:], dist_i[:], 3, None, ALU.bitwise_and))
            link(dve.tensor_copy(term[:], mod_i[:]))
            link(dve.tensor_scalar(term[:], term[:], 0.0, None, ALU.is_equal))
            link(dve.scalar_tensor_tensor(out=count[:], in0=dist[:], scalar=512.0, in1=term[:], op0=ALU.is_le, op1=ALU.mult))
            link(dve.scalar_tensor_tensor(out=count[:], in0=dist[:], scalar=128.0, in1=count[:], op0=ALU.is_le, op1=ALU.add))
            link(dve.tensor_scalar(mod_i[:], dist_i[:], 15, None, ALU.bitwise_and))
            link(dve.tensor_copy(term[:], mod_i[:]))
            link(dve.tensor_scalar(term[:], term[:], 0.0, None, ALU.is_equal))
            link(dve.tensor_tensor(count[:], count[:], term[:], ALU.add))
            link(dve.scalar_tensor_tensor(out=count[:], in0=dist[:], scalar=0.0, in1=count[:], op0=ALU.is_ge, op1=ALU.mult))
            link(dve.tensor_scalar(term[:], count[:], 0.5, FAR, ALU.is_lt, ALU.mult))
            link(dve.tensor_scalar(dist[:], count[:], 1.5, -LN2, ALU.is_ge, ALU.mult))
            link(dve.tensor_tensor(term[:], term[:], dist[:], ALU.add))
            link(dve.tensor_scalar(dist[:], count[:], 2.5, LN2 - LN3, ALU.is_ge, ALU.mult))
            link(dve.tensor_tensor(logit_bias[:, 1, :], term[:], dist[:], ALU.add))
            dve.wait_ge(gains_in, 16 * 11)
            for n in (0, 2):
                link(dve.tensor_scalar(gains[:, n:n + 1], gains[:, n:n + 1], -float(HEAD) ** -0.5, None, ALU.mult))

            def forget(slot):
                if slot == 1:
                    dve.wait_ge(small_out, 1)
                    dve.tensor_scalar(lf_min, small[0:B_HEADS, :], fox_col[:], None, ALU.add).then_inc(lf_step, 1)
                if slot == 4:
                    dve.wait_ge(lf_step, 4)
                    dve.scalar_tensor_tensor(out=lf_min, in0=lf_min, scalar=0.0, in1=lf_abs, op0=ALU.min,
                                             op1=ALU.subtract).then_inc(lf_step, 1)
                    dve.wait_ge(lf_step, 5)
                    dve.tensor_tensor_scan(out=c_sum[:], data0=lf_min, data1=lf_min, initial=0.0, op0=ALU.add,
                                           op1=ALU.bypass).then_inc(c_done, 1)

            group(0, forget)
            with dve.Fori(1, C_ALONE) as s:
                group(s, lambda slot: None)

            dve.wait_ge(levels_ready, 2 + 2 * LEVELS)
            levels_put, items_scored = dve.alloc_register("levels_put"), dve.alloc_register("items_scored")
            dve.reg_mov(levels_put, 0)
            dve.reg_mov(items_scored, 0)

            def gla_steps(c, slot):
                if slot == G_GATE:
                    dve.wait_ge(gla_bias_in, 16 * (c + 1))
                    dve.wait_ge(gla_silu, c)
                    dve.wait_ge(gla_gate, c + 1)
                    dve.tensor_scalar(g_t[:, 0, :], scores[0:C_DK, :], gate_bias[:], None, ALU.add).then_inc(gla_sum, 1)
                    dve.wait_ge(gla_log, c + 1)
                    dve.tensor_scalar(g_t[:, 0, :], g_t[:, 0, :], 0.0, 1.0 / 16, ALU.min, ALU.mult).then_inc(gla_min, 1)
                    dve.wait_ge(gla_min, c + 1)
                    dve.scalar_tensor_tensor(out=g_t[:, 0, :], in0=g_t[:, 1, :], scalar=-1.0 / 16, in1=g_t[:, 0, :],
                                                 op0=ALU.mult, op1=ALU.add).then_inc(gla_a, 1)
                    dve.wait_ge(gla_a, c + 1)
                    for t in range(NT):
                        at = slice(t * P, (t + 1) * P)
                        dve.tensor_tensor_scan(out=g_b[:, at], data0=g_t[:, 0, at], data1=g_t[:, 0, at],
                                                   initial=0.0, op0=ALU.add, op1=ALU.bypass).then_inc(gla_scan, 1)
                    dve.wait_ge(gla_scan, NT * (c + 1))
                    dve.memset(weights_t, 0.0).then_inc(gla_zero, 1)
                    dve.wait_ge(gla_zero, c + 1)
                    dve.wait_ge(gla_diag, c + 1)
                    put(weights_t.rearrange("p (t q) -> p t q", t=NT),
                        ident[:].unsqueeze(1).broadcast_to([P, NT, P]), turned[:].rearrange("p (t q) -> p t q", t=NT))
                for l in range(LEVELS):
                    if slot == G_LEVEL[l]:
                        b, n = 1 << l, LEVELS * c + l
                        bv, ev = blocks(g_b[:], b), blocks(g_t[:, l % 2, :], b)
                        edge = bv[:, :, 0, b - 1:b].broadcast_to([C_DK, SEQ // (2 * b), b])
                        dve.wait_ge(gla_kl, n - 1 if l >= 2 else LEVELS * c)
                        dve.tensor_tensor(ev[:, :, 1, :], bv[:, :, 1, :], edge, ALU.subtract).then_inc(gla_diff, 1)
                        dve.tensor_tensor(ev[:, :, 0, :], edge, bv[:, :, 0, :], ALU.subtract).then_inc(gla_diff, 1)
                        if l >= 1:
                            put_level(c, l - 1)
                if slot == G_CARRY - 1:
                    dve.wait_ge(gla_kl, LEVELS * (c + 1) - 1)
                    bt = g_b[:].rearrange("p (t q) -> p t q", t=NT)
                    dve.tensor_tensor(g_t[:, 1, :].rearrange("p (t q) -> p t q", t=NT),
                                          bt[:, :, P - 1:P].broadcast_to([C_DK, NT, P]), bt, ALU.subtract)\
                                              .then_inc(gla_ldiff, 1)
                if slot == G_CARRY:
                    put_level(c, LEVELS - 1)
                if slot == G_STATE:
                    for t in range(1, NT):
                        i = t - 1
                        src = banks[2 + i // 2][0:C_DK, (i % 2) * C_DV:(i % 2 + 1) * C_DV]
                        if t == 1:
                            dve.wait_ge(gla_eb, c + 1)
                            dve.wait_ge(gla_ds, c + 1)
                            dve.tensor_copy(state[:, 1, :], src).then_inc(gla_state, 1)
                        else:
                            dve.wait_ge(gla_state, (NT - 1) * c + t - 1)
                            dve.scalar_tensor_tensor(out=state[:, t, :], in0=state[:, t - 1, :],
                                                         scalar=g_t[:, 0, i * P + P - 1:i * P + P], in1=src,
                                                         op0=ALU.mult, op1=ALU.add).then_inc(gla_state, 1)
                if slot == G_Z:
                    dve.wait_ge(gla_ke, c + 1)
                    dve.wait_ge(gla_z_in, 16 * (c + 1))
                    dve.wait_ge(gla_state, (NT - 1) * (c + 1))
                    dve.tensor_scalar(g_t[:, :, :], g_z[:, :, :], LOWEST, None, ALU.max).then_inc(gla_zb, 1)
                if slot == G_NORM:
                    dve.wait_ge(gla_rstd, c + 1)
                    dve.tensor_tensor(o_rows, o_rows, o_rstd[:].unsqueeze(2).broadcast_to([P, NT, C_DV]), ALU.mult)\
                        .then_inc(gla_norm, 1)
                if slot == G_FINAL:
                    dve.wait_ge(gla_silu, c + 1)
                    for h in range(2):
                        dve.wait_ge(gla_ot, 2 * c + h + 1)
                        dve.scalar_tensor_tensor(out=g_z[:, h, :], in0=(scores, turned)[h][0:C_DK, :],
                                                     scalar=out_gain[:, h:h + 1], in1=g_z[:, h, :], op0=ALU.mult,
                                                     op1=ALU.mult).then_inc(gla_out, 1)

            def put(dst, mask, data):
                dve.reg_add(levels_put, levels_put, 1)
                dve.copy_predicated(dst, mask.bitcast(I32), data).then_inc(gla_put, 1)

            def put_level(c, l):
                b = 1 << l
                dve.wait_ge(gla_put, levels_put)
                dve.wait_ge(gla_lv, LEVELS * c + l + 1)
                put(blocks(weights_t, b)[:, :, 1, :].rearrange("p (t n) r -> p t n r", t=NT),
                    level_mask[:, l, :].rearrange("p (n r) -> p n r", r=b).unsqueeze(1).broadcast_to([P, NT, HEAD // b, b]),
                    banks[6 + l % 2].rearrange("p (t n r) -> p t n r", t=NT, r=b))

            def gla_head(c):
                for g in range(HEAD_GROUPS):
                    group(C_ALONE + HEAD_GROUPS * c + g, lambda slot: gla_steps(c, 8 * g + slot))

            gla_head(0)
            with dve.Fori(1, C_HEADS) as c:
                gla_head(c)

            def square(pair, m):
                dve.wait_ge(sq_done, 2 * (4 * pair + m + 1))
                dve.tensor_tensor(sq_lo[:], sq[:, m % 2, :], sq_hi[:].bitcast(F32),
                                  ALU.subtract).then_inc(sq_lo_done, 1)

            def norm(pair, i, kind):
                dve.wait_ge(root_done, 2 * pair + i + 1)
                dve.scalar_tensor_tensor(out=raw[:, i, :], in0=raw[:, i, :], scalar=gains[:, 2 * kind + i:2 * kind + i + 1],
                                         in1=sq_wide, op0=ALU.mult, op1=ALU.mult).then_inc(normed, 1)

            def stack(pair, h):
                own, other = slice(h * HEAD, (h + 1) * HEAD), slice((1 - h) * HEAD, (2 - h) * HEAD)
                dve.wait_ge(normed, 2 * (pair + 1))
                if not first_pair(pair):
                    dve.wait_ge(s_done, ITEMS * (pair - 1) + NT * (h + 1))
                dve.tensor_copy(k_hi[other, h, :], raw[own, 1, :]).then_inc(k_other_done, 1)

            def values(pair, b):
                dve.wait_ge(vh_done, 2 * pair + b + 1)
                at = v_st[:, :, 4 * b:4 * b + 4, :]
                dve.tensor_tensor(at[:, :, :, HEAD:P], side[:].rearrange("p (t h c) -> p h t c", t=4, h=2),
                                  at[:, :, :, 0:HEAD].bitcast(F32), ALU.subtract).then_inc(vl_done, 1)

            def bound(pair):
                dve.wait_ge(z_in, 16 * (pair + 1))
                dve.wait_ge(v_turned, 2 * (pair + 1))
                dve.tensor_scalar(sq_wide, vz[:], LOWEST, None, ALU.max).then_inc(z_bounded, 1)

            def silu(pair):
                dve.wait_ge(sigmoid_done, pair + 1)
                dve.tensor_tensor(vz[:], vz[:], sq_wide, ALU.mult).then_inc(silu_done, 1)

            def score(pair, j, kind):
                h, i = j // NT, j % NT
                n = (i + 1) * P
                it = ITEMS * pair + j
                bias = logit_bias[:, 1, (NT - 1 - i) * P:SEQ] if kind == 0 else logit_bias[:, h, 0:n]
                if not (first_pair(pair) and j < 2):
                    dve.wait_ge(t_done, it - 1)
                if kind == 1 and i == 0:
                    dve.wait_ge(bias_in[h], 16 * (pair - A_PAIRS + 1))
                dve.wait_ge(s_done, it + 1)
                dve.reg_add(items_scored, items_scored, 1)
                dve.tensor_tensor_reduce(out=prob[:, j % 2, 0:n], in0=scores[:, 0:n], in1=bias, scale=1.0, scalar=3e38,
                                             op0=ALU.add, op1=ALU.min, accum_out=neg_max[:, j:j + 1])\
                                                 .then_inc(masked, 1)

            def scale(pair, j):
                n = (j % NT + 1) * P
                it = ITEMS * pair + j
                dve.wait_ge(exp_done, items_scored)
                dve.reciprocal(inv_denom[:, j:j + 1], denom[:, j:j + 1]).then_inc(recip_done, 1)
                dve.wait_ge(recip_done, it + 1)
                dve.tensor_scalar(prob[:, j % 2, 0:n], prob[:, j % 2, 0:n], inv_denom[:, j:j + 1], None, ALU.mult)\
                    .then_inc(prob_done, 1)

            def turn(pair, j):
                n = (j % NT + 1) * P
                dve.wait_ge(pth_done, ITEMS * pair + j + 1)
                dve.tensor_tensor(pt_lo[:, 0:n], turned[:, 0:n], pt_hi[:, 0:n].bitcast(F32), ALU.subtract)\
                    .then_inc(ptl_done, 1)

            def product(pair, j):
                if j % 4 == 3:
                    h, u = j // NT, j // 4
                    own, cols = slice(h * HEAD, (h + 1) * HEAD), slice((u % 2) * HALF, (u % 2 + 1) * HALF)
                    dve.wait_ge(o_moved, 4 * pair + u + 1)
                    dve.tensor_tensor(o_part[own, :], pv[own, :], o_part[own, :], ALU.add).then_inc(o_summed, 1)
                    dve.wait_ge(silu_done, pair + 1)
                    dve.wait_ge(o_summed, 4 * pair + u + 1)
                    dve.tensor_tensor(vz[own, cols], o_part[own, :], vz[own, cols], ALU.mult).then_inc(o_done, 1)

            def steps_at(pair, kind, slot, next_kind):
                for name, j in steps_of(slot):
                    if name == "values":
                        values(pair, j)
                    elif name == "product":
                        product(pair, j)
                    elif name == "turn":
                        turn(pair, j)
                    elif name == "scale":
                        scale(pair, j)
                    elif name == "score":
                        score(pair, j, kind)
                    elif name == "stack1":
                        stack(pair, 1)
                    elif name == "bound":
                        bound(pair)
                    elif name == "silu":
                        silu(pair)
                    elif name == "root" and next_kind is not None:
                        norm(pair + 1, j, next_kind)
                    elif name == "square" and next_kind is not None:
                        square(pair + 1, j)
                    elif name == "stack0" and next_kind is not None:
                        stack(pair + 1, 0)

            def first_steps(slot):
                for name, j in first_steps_of(slot):
                    if name == "root":
                        norm(0, j, 0)
                    elif name == "square":
                        square(0, j)
                    elif name == "stack0":
                        stack(0, 0)

            group(S_FIRST_Z, first_steps)

            def pair_body(pair, kind, s0, next_kind):
                for g in range(PAIR_GROUPS):
                    def steps(slot, g=g):
                        steps_at(pair, kind, 8 * g + slot, next_kind)
                    if next_kind is not None:
                        group(s0 + g, steps)
                    else:
                        for slot in range(8):
                            last_pair_slot(8 * g + slot, lambda: steps(slot))
                if next_kind is None:
                    last_pair_slot(SLOTS, lambda: steps_at(pair, kind, SLOTS, None))
                else:
                    steps_at(pair, kind, SLOTS, next_kind)

            def last_pair_slot(slot, steps):
                quarters = early_at(slot)
                for n in quarters[:1]:
                    split_next(n)
                steps()
                for kk in range(KT - 1):
                    if MIX_SLOT[kk] == slot:
                        mix_lo_part(kk)
                for n in quarters[1:]:
                    split_next(n)

            def split_next(n):
                split_lo_out(n + 1)
                if n % (KT - 1) == 0 and n > 0:
                    early_sums(n // (KT - 1) - 1)

            def split_lo_out(n):
                slot = n % 2
                dve.wait_ge(hi_done, Q_OUT + n + 1)
                dve.tensor_tensor(w_lo[:, slot, :], w_raw[:, slot, :], w_hi[:, slot, :].bitcast(F32),
                                  ALU.subtract).then_inc(lo_done, 1)

            def early_sums(r):
                for i, t in enumerate(ROUNDS[r]):
                    dve.wait_ge(res_in[t], 16)
                    dve.wait_ge(partial_ready, t + 1)
                    dve.tensor_tensor(early_stage(t), early_banks[i], early_stage(t), ALU.add)\
                        .then_inc(partial_summed, 1)

            def mix_lo_part(kk):
                dve.wait_ge(mix_hi, kk + 1)
                dve.tensor_tensor(act_lo[:, OUT_ORDER[kk], :], raw[:, kk % 2, :],
                                      act_hi[:, OUT_ORDER[kk], :].bitcast(F32), ALU.subtract).then_inc(mix_lo, 1)

            pair_body(0, 0, S_LOOP_A, 0)
            with dve.Fori(1, A_PAIRS - 1) as p:
                pair_body(p, 0, S_LOOP_A + 4 * p, 0)
            pair_body(A_PAIRS - 1, 0, S_B0, 1)
            with dve.Fori(0, B_PAIRS - 1) as p:
                pair_body(A_PAIRS + p, 1, S_LOOP_B + 4 * p, 1)
            pair_body(A_PAIRS + B_PAIRS - 1, 1, None, None)

            early_sums(len(ROUNDS) - 1)

            def add_residual(cg):
                for t in range(NT):
                    dve.wait_ge(res_in[t], 16 * (cg + 1))
                    dve.wait_ge(out_ready, NT * (cg - 1) + t + 1)
                    to = (res_first if isinstance(cg, int) and cg == OUT_CG else res)[:, t, :]
                    dve.tensor_tensor(to, banks[t], to, ALU.add).then_inc(out_summed, 1)

            def split_lo_group(cg, kk):
                slot = (EARLY + kk) % 2
                dve.wait_ge(hi_done, Q_OUT + EARLY + KT * (cg - 1) + kk + 1)
                dve.tensor_tensor(w_lo[:, slot, :], w_raw[:, slot, :], w_hi[:, slot, :].bitcast(F32),
                                  ALU.subtract).then_inc(lo_done, 1)

            for kk in range(KT):
                split_lo_group(*((1, kk + 1) if kk < KT - 1 else (2, 0)))
                if kk == 6:
                    mix_lo_part(KT - 1)
            add_residual(1)
            with dve.Fori(2, OUT_CG) as cg:
                for kk in range(KT):
                    split_lo_group(*((cg, kk + 1) if kk < KT - 1 else (cg + 1, 0)))
                add_residual(cg)
            add_residual(OUT_CG)

        @block.tensor
        def _(pe):
            def half_quarter(s, kq, th):
                if th == 0:
                    pe.wait_ge(lo_done, 4 * s + kq + 1)
                if kq == 0 and not (isinstance(s, int) and s == 0):
                    pe.wait_ge(evac_done, 2 * s + th - 1)
                at = slice(th * HALF, (th + 1) * HALF)
                for k in range(4):
                    hi, lo = (w[:, kq % 2, k * P:(k + 1) * P] for w in (w_hi, w_lo))
                    xh, xl = (a[:, 4 * kq + k, at] for a in (act_hi, act_lo))
                    first, end = kq == 0 and k == 0, kq == 3 and k == 3
                    pe.matmul(bank[th][:], hi, xh, start=first, stop=False)
                    pe.matmul(bank[th][:], hi, xl, start=False, stop=False)
                    mm = pe.matmul(bank[th][:], lo, xh, start=False, stop=end)
                if kq == 3:
                    mm.then_inc(half_done, 1)
                elif th == 1:
                    mm.then_inc(quarter_done, 1)
                return mm

            def group(s, steps):
                for slot in range(8):
                    steps(slot)
                    kq, th = slot // 2, slot % 2
                    half_quarter(s, kq, th)

            def small_columns(th, ks):
                pe.wait_ge(x_lo_done, 2 * NT * (th + 1))
                pe.wait_ge(ws_lo_done, 1)
                at = slice(th * HALF, (th + 1) * HALF)
                for k in ks:
                    pe.matmul(scores[0:SMALL, at], ws_hi[:, k, :], act_hi[:, k, at], start=(k == 0), stop=False)
                    pe.matmul(scores[0:SMALL, at], ws_hi[:, k, :], act_lo[:, k, at], start=False, stop=False)
                    mm = pe.matmul(scores[0:SMALL, at], ws_lo[:, k, :], act_hi[:, k, at], start=False, stop=(k == KT - 1))
                return mm

            for t in range(NT):
                pe.wait_ge(consts, 8)
                pe.wait_ge(x_normed, t + 1)
                for b in range(4):
                    n = 4 * t + b
                    if n >= 6:
                        pe.wait_ge(x_lo_done, n - 5)
                    for k in range(4):
                        f = 4 * b + k
                        mm = pe.transpose(turn_banks[n % 6][:, k * P:(k + 1) * P],
                                          x_tile[:, t % 2, f * P:(f + 1) * P], ident[:])
                    mm.then_inc(x_turned, 1)
                if t in SMALL_AT:
                    small_columns(0, SMALL_AT[t])
            small_columns(1, range(KT)).then_inc(small_done, 1)
            group(0, lambda slot: None)
            with pe.Fori(1, C_ALONE) as s:
                group(s, lambda slot: None)

            pe.wait_ge(rounded_consts, 3)

            def gla_steps(c, slot):
                if slot == G_GATE:
                    pe.wait_ge(gla_up_in, 16 * (c + 1))
                    pe.wait_ge(gla_rank_in, 16 * (c + 1))
                    pe.wait_ge(small_out, 1)
                    pe.wait_ge(gla_out, 2 * c)
                    for th in range(2):
                        at = slice(th * HALF, (th + 1) * HALF)
                        mm = pe.matmul(scores[0:C_DK, at], gate_up[:], rank_rows[:, at], start=True, stop=True)
                    mm.then_inc(gla_gate, 1)
                    pe.wait_ge(gla_k_in, 16 * (c + 1))
                    pe.wait_ge(gla_scaled, c + 1)
                    for t in range(NT):
                        at = slice(t * P, (t + 1) * P)
                        mm = pe.matmul(turned[:, at], g_k[:, at], g_q[:, at], start=True, stop=True)
                    mm.then_inc(gla_diag, 1)
                for l in range(LEVELS):
                    if slot == G_LEVEL[l] + 1:
                        n = LEVELS * c + l
                        pe.wait_ge(gla_put, 8 * c + l if l >= 2 else 8 * c)
                        pe.wait_ge(gla_kcopy, 2 * c)
                        pe.wait_ge(gla_ql, n + 1)
                        pe.wait_ge(gla_kl, n + 1)
                        for t in range(NT):
                            mm = pe.matmul(banks[6 + l % 2][:, t * HEAD:(t + 1) * HEAD],
                                           k_level[:, l % 2, t * P:(t + 1) * P],
                                           q_level[:, l % 2, t * HEAD:(t + 1) * HEAD], start=True, stop=True)
                        mm.then_inc(gla_lv, 1)
                if slot == G_TURN_V:
                    pe.wait_ge(gla_v_in, 16 * (c + 1))
                    pe.wait_ge(gla_sum, c + 1)
                    pe.wait_ge(gla_put, 8 * c + 1)
                    for i in range(4):
                        for t in (2 * i, 2 * i + 1):
                            for h in range(2):
                                o = (t % 2) * C_DV + h * C_DK
                                mm = pe.transpose(banks[2 + i][:, o:o + C_DK], g_v[:, h, t * P:(t + 1) * P],
                                                  ident[0:C_DK, 0:C_DK])
                        mm.then_inc(gla_vt, 1)
                if slot == G_TURN_K:
                    pe.wait_ge(gla_put, 8 * (c + 1))
                    pe.wait_ge(gla_ke, c + 1)
                    for i in range(2):
                        for t in range(4 * i, 4 * i + 4):
                            mm = pe.transpose(banks[6 + i][:, (t % 4) * C_DK:(t % 4 + 1) * C_DK],
                                              k_carry[:, t * P:(t + 1) * P], ident[0:C_DK, 0:C_DK])
                        mm.then_inc(gla_kt, 1)
                if slot == G_STATE:
                    pe.wait_ge(gla_vcopy, 4 * (c + 1))
                    pe.wait_ge(gla_kcopy, 2 * (c + 1))
                    for t in range(NT - 1):
                        mm = pe.matmul(banks[2 + t // 2][0:C_DK, (t % 2) * C_DV:(t % 2 + 1) * C_DV], k_rows[:, t, :],
                                       v_rows[:, t, :], start=True, stop=True)
                    mm.then_inc(gla_ds, 1)
                if slot == G_OUT:
                    pe.wait_ge(gla_state, (NT - 1) * (c + 1))
                    pe.wait_ge(gla_qe, c + 1)
                    for t in range(NT):
                        o, at = banks[2 + t // 2][:, (t % 2) * C_DV:(t % 2 + 1) * C_DV], slice(t * P, (t + 1) * P)
                        mm = pe.matmul(o, weights_t[:, at], v_rows[:, t, :], start=True, stop=(t == 0))
                        if t > 0:
                            mm = pe.matmul(o, q_carry[:, at], state[:, t, :], start=False, stop=True)
                        if t % 2 == 1:
                            mm.then_inc(gla_o, 1)
                if slot == G_FINAL:
                    pe.wait_ge(gla_ocopy, 4 * (c + 1))
                    pe.wait_ge(gla_norm, c + 1)
                    for h in range(2):
                        for t in range(NT):
                            mm = pe.transpose((scores, turned)[h][0:C_DK, t * P:(t + 1) * P],
                                              o_rows[:, t, h * C_DK:(h + 1) * C_DK], ident[:])
                        mm.then_inc(gla_ot, 1)

            def gla_head(c):
                for g in range(HEAD_GROUPS):
                    group(C_ALONE + HEAD_GROUPS * c + g, lambda slot: gla_steps(c, 8 * g + slot))

            gla_head(0)
            with pe.Fori(1, C_HEADS) as c:
                gla_head(c)

            def sum_squares(pair, m):
                if m > 0:
                    pe.wait_ge(ssq_logged, 4 * pair + m)
                else:
                    pe.wait_ge(vl_done, 2 * pair)
                pe.wait_ge(sq_lo_done, 4 * pair + m + 1)
                pe.matmul(side[:], half_ones_r[:], sq_hi[:], start=True, stop=False)
                pe.matmul(side[:], half_ones_r[:], sq_lo[:], start=False, stop=True).then_inc(ssq_done, 1)

            def values(pair, b):
                pe.wait_ge(v_in, 16 * (pair + 1))
                if b == 0:
                    pe.wait_ge(ssq_logged, 4 * (pair + 1))
                else:
                    pe.wait_ge(vl_done, 2 * pair + 1)
                for t in range(4 * b, 4 * b + 4):
                    mm = pe.transpose(side[:, (t - 4 * b) * P:(t - 4 * b + 1) * P], sq_wide[:, t * P:(t + 1) * P], ident[:])
                mm.then_inc(v_turned, 1)

            def score(pair, j, kind):
                h, i = j // NT, j % NT
                n = (i + 1) * P
                if i == 0:
                    pe.wait_ge(ql_done, 2 * pair + h + 1)
                    pe.wait_ge(kl_done, 2 * pair + h + 1)
                    pe.wait_ge(k_other_done, 2 * pair + h + 1)
                pe.wait_ge(masked, ITEMS * pair + j)
                q, own = q_st[:, h, i * P:(i + 1) * P], slice(h * HEAD, (h + 1) * HEAD)
                for c0 in range(0, n, HALF):
                    c1 = min(c0 + HALF, n)
                    pe.matmul(scores[:, c0:c1], q, k_hi[:, h, c0:c1], start=True, stop=False)
                    if kind == 1 and c1 == n:
                        pe.matmul(scores[:, i * P:n], ident_r[:], causal_r[:], start=False, stop=False)
                    mm = pe.matmul(scores[:, c0:c1], q_st[own, h, i * P:(i + 1) * P], k_lo[own, c0:c1], start=False,
                                   stop=True)
                mm.then_inc(s_done, 1)

            def turn(pair, j):
                it = ITEMS * pair + j
                pe.wait_ge(vl_done, 2 * (pair + 1))
                pe.wait_ge(ptl_done, it)
                pe.wait_ge(prob_done, it + 1)
                for t in range(j % NT + 1):
                    at = slice(t * P, (t + 1) * P)
                    mm = pe.transpose(turned[:, at], prob[:, j % 2, at], ident[:])
                mm.then_inc(t_done, 1)

            def product(pair, j):
                h, i = j // NT, j % NT
                if j % 4 == 0:
                    pe.wait_ge(o_summed, 4 * pair + j // 4)
                pe.wait_ge(ptl_done, ITEMS * pair + j + 1)
                o = pv[:, (j % 4) * P:(j % 4 + 1) * P]
                for t in range(i + 1):
                    at = slice(t * P, (t + 1) * P)
                    pe.matmul(o, v_st[:, h, t, :], pt_hi[:, at], start=(t == 0), stop=False)
                    mm = pe.matmul(o, v_st[:, h, t, :], pt_lo[:, at], start=False, stop=(t == i))
                mm.then_inc(pv_done, 1)

            def steps_at(pair, kind, slot, has_next):
                for name, j in steps_of(slot):
                    if name == "values":
                        values(pair, j)
                    elif name == "product":
                        product(pair, j)
                    elif name == "turn":
                        turn(pair, j)
                    elif name == "score":
                        score(pair, j, kind)
                    elif name == "sum" and has_next:
                        sum_squares(pair + 1, j)

            def pair_body(pair, kind, s0):
                for slot in range(SLOTS + 1):
                    steps_at(pair, kind, slot, s0 is not None)
                    if s0 is None:
                        for n in early_at(slot):
                            early_quarter(n)
                    elif slot < SLOTS:
                        half_quarter(s0 + slot // 8, slot % 8 // 2, slot % 2)

            def early_quarter(n):
                r, kk = n // (KT - 1), n % (KT - 1)
                k = OUT_ORDER[kk]
                pe.wait_ge(lo_done, Q_OUT + n + 1)
                pe.wait_ge(mix_lo, kk + 1)
                for i, t in enumerate(ROUNDS[r]):
                    if kk == 0:
                        pe.wait_ge(evac_done, 2 * GROUPS)
                        pe.wait_ge(vl_done, 2 * (A_PAIRS + B_PAIRS))
                        if r > 0:
                            pe.wait_ge(partial_summed, ROUNDS[r - 1][i] + 1)
                    hi, lo = (a[:, k, t * P:(t + 1) * P] for a in (act_hi, act_lo))
                    pe.matmul(early_banks[i], hi, w_hi[:, n % 2, :], start=(kk == 0), stop=False)
                    pe.matmul(early_banks[i], hi, w_lo[:, n % 2, :], start=False, stop=False)
                    mm = pe.matmul(early_banks[i], lo, w_hi[:, n % 2, :], start=False, stop=(kk == KT - 2))
                    if kk == KT - 2:
                        mm.then_inc(partial_ready, 1)
                if kk < KT - 2:
                    mm.then_inc(quarter_done, 1)

            def first_steps(slot):
                for name, j in first_steps_of(slot):
                    if name == "sum":
                        sum_squares(0, j)

            group(S_FIRST_Z, first_steps)
            pair_body(0, 0, S_LOOP_A)
            with pe.Fori(1, A_PAIRS - 1) as p:
                pair_body(p, 0, S_LOOP_A + 4 * p)
            pair_body(A_PAIRS - 1, 0, S_B0)
            with pe.Fori(0, B_PAIRS - 1) as p:
                pair_body(A_PAIRS + p, 1, S_LOOP_B + 4 * p)
            pair_body(A_PAIRS + B_PAIRS - 1, 1, None)

            def out_quarter(cg, kk, only=False):
                at_end = kk == KT - 1
                slot = EARLY % 2 if only else (EARLY + kk) % 2
                k = OUT_ORDER[kk]
                pe.wait_ge(lo_done, Q_OUT + EARLY + KT * (cg - 1) + (0 if only else kk) + 1)
                if at_end:
                    pe.wait_ge(mix_lo, KT)
                for t in range(NT):
                    if kk == 0 and isinstance(cg, int):
                        pe.wait_ge(o_summed, 4 * (A_PAIRS + B_PAIRS))
                        pe.wait_ge(partial_summed, NT)
                    elif kk == 0 or only:
                        pe.wait_ge(out_summed, NT * (cg - 2) + t + 1)
                    hi, lo = (a[:, k, t * P:(t + 1) * P] for a in (act_hi, act_lo))
                    pe.matmul(banks[t], hi, w_hi[:, slot, :], start=(kk == 0 or only), stop=False)
                    pe.matmul(banks[t], hi, w_lo[:, slot, :], start=False, stop=False)
                    mm = pe.matmul(banks[t], lo, w_hi[:, slot, :], start=False, stop=at_end)
                    if at_end:
                        mm.then_inc(out_ready, 1)
                if not at_end:
                    mm.then_inc(quarter_done, 1)

            for kk in range(KT):
                out_quarter(1, kk)
            with pe.Fori(2, OUT_CG) as cg:
                for kk in range(KT):
                    out_quarter(cg, kk)
            out_quarter(OUT_CG, KT - 1, only=True)


_INS = ["x", "norm_g", "w_in", "a_q_gain", "a_k_gain", "b_q_gain", "b_k_gain", "fox_bias", "gla_gate_up",
        "gla_gate_bias", "gla_out_gain", "w_out"]


def kernel(**inputs):
    import numpy as _np
    import concourse.bacc as _bacc
    from concourse import mybir as _mybir
    from concourse.bass_utils import run_bass_kernel_spmd as _run

    nc = _bacc.Bacc("TRN2", target_bir_lowering=False, num_devices=1, dynamic_dma_scratch_size=1024)
    arrays, args = {}, []
    for name in _INS:
        a = _np.ascontiguousarray(inputs[name])
        arrays[f"in_{name}_dram"] = a
        args.append(nc.dram_tensor(f"in_{name}_dram", a.shape, _mybir.dt.from_np(a.dtype), kind="ExternalInput").ap())
    args.append(nc.dram_tensor("out_0_dram", (1, SEQ, D_MODEL), _mybir.dt.float32, kind="ExternalOutput").ap())
    build(nc, *args)
    r = _run(nc, [arrays], core_ids=[0])
    return r.results[0]["out_0_dram"]
```
